# Optimizing a Trainium2 kernel written in Bass

```python
import math, functools
import jax, jax.numpy as jnp
from jax import lax
import numpy as np

D_MODEL = 1024
BATCH = 1
SEQ = 512
DEPTH = 1
DEC_BATCH = 8
DEC_SEQ = 8
PAST_LEN = 2048
PAGE_SIZE = 128

D_MIX = D_MODEL
A_HEADS = 4
A_DK = 128
A_DV = 128
A_WIDTH = A_HEADS * A_DV
B_HEADS = 8
B_DH = 64
B_WIDTH = B_HEADS * B_DH
IDX_HEADS = 16
IDX_DIM = 64
TOPK_MAX = 256
ROPE_THETA = 500000.0
B_ROT = B_DH // 4
IDX_ROT = IDX_DIM // 4
HGRN_CHUNK = 64
Q_BLOCK = 128
LN_EPS = 1e-5
ALPHA = (2.0 * DEPTH) ** 0.25
BETA = (8.0 * DEPTH) ** -0.25
IN_WIDTHS = (A_HEADS * A_DK, A_HEADS * A_DK, A_WIDTH, A_WIDTH,
             B_WIDTH, B_WIDTH, B_WIDTH, B_WIDTH,
             IDX_HEADS * IDX_DIM, IDX_DIM, IDX_HEADS)
IN_OFFSETS = tuple(sum(IN_WIDTHS[: i + 1]) for i in range(len(IN_WIDTHS) - 1))
D_IN = sum(IN_WIDTHS)

kernel_name = "hymba_hgrn2_dsa_deepnorm_step"

def layer_norm(x, g, b):
    xf = x.astype(jnp.float32)
    mu = jnp.mean(xf, -1, keepdims=True)
    var = jnp.mean(jnp.square(xf - mu), -1, keepdims=True)
    return ((xf - mu) * lax.rsqrt(var + LN_EPS) * g + b).astype(x.dtype)

def rms_norm(x, g):
    xf = x.astype(jnp.float32)
    return xf * lax.rsqrt(jnp.mean(xf * xf, -1, keepdims=True) + LN_EPS) * g

def partial_rope(x, pos, rot):
    half = rot // 2
    inv = ROPE_THETA ** (-jnp.arange(half, dtype=jnp.float32) / half)
    ang = pos.astype(jnp.float32)[:, None] * inv[None, :]
    cos = jnp.cos(ang)[:, None, :]
    sin = jnp.sin(ang)[:, None, :]
    xf = x.astype(jnp.float32)
    x1, x2 = xf[..., :half], xf[..., half:rot]
    out = jnp.concatenate([x1 * cos - x2 * sin, x1 * sin + x2 * cos, xf[..., rot:]], -1)
    return out.astype(x.dtype)

def hgrn_lower_bounds(lb_logits):
    p = jax.nn.softmax(lb_logits.astype(jnp.float32), axis=0)
    return jnp.cumsum(p, axis=0)[:DEPTH]

def hgrn2_recurrence(q, k, v, logf, s0):
    B, L, H, _ = q.shape
    DV = v.shape[-1]
    c = math.gcd(L, HGRN_CHUNK)
    n = L // c

    def chunks(a):
        return a.astype(jnp.float32).reshape(B, n, c, H, a.shape[-1]).transpose(1, 0, 3, 2, 4)

    causal = jnp.tril(jnp.ones((c, c), dtype=bool))[:, :, None]

    def step(S, inp):
        qc, kc, vc, gc = inp
        cum = jnp.cumsum(gc, axis=2)
        o_inter = jnp.einsum('bhtk,bhkv->bhtv', qc * jnp.exp(cum), S)
        rel = jnp.where(causal, cum[:, :, :, None, :] - cum[:, :, None, :, :], -jnp.inf)
        scores = jnp.einsum('bhtk,bhsk,bhtsk->bhts', qc, kc, jnp.exp(rel))
        o_intra = jnp.einsum('bhts,bhsv->bhtv', scores, vc)
        last = cum[:, :, -1:, :]
        S_new = (jnp.exp(last[:, :, 0, :])[..., None] * S
                 + jnp.einsum('bhsk,bhsv->bhkv', kc * jnp.exp(last - cum), vc))
        return S_new, o_inter + o_intra

    s_final, o = lax.scan(step, s0.astype(jnp.float32),
                          (chunks(q), chunks(k), chunks(v), chunks(logf)))
    o = o.transpose(1, 0, 3, 2, 4).reshape(B, L, H, DV)
    return o, s_final

def hgrn2_branch(qa, fa, ia, ga, lb, norm_g, s0):
    B, L, _ = qa.shape
    hd = lambda a, d: a.reshape(B, L, A_HEADS, d)
    fa32 = fa.astype(jnp.float32)
    logf = jnp.log(lb + (1.0 - lb) * jax.nn.sigmoid(fa32))
    key = (1.0 - lb) * jax.nn.sigmoid(-fa32)
    o, s_new = hgrn2_recurrence(hd(jax.nn.silu(qa), A_DK), hd(key, A_DK),
                                hd(ia, A_DV), hd(logf, A_DK), s0)
    o = rms_norm(o, norm_g).reshape(B, L, A_WIDTH)
    return o * jax.nn.silu(ga.astype(jnp.float32)), s_new

def dsa_inputs(qb, kb, vb, qi, ki, wi, pos, kn_g, kn_b):
    B, L, _ = qb.shape
    q = partial_rope(qb.reshape(B, L, B_HEADS, B_DH), pos, B_ROT)
    k = partial_rope(kb.reshape(B, L, B_HEADS, B_DH), pos, B_ROT)
    v = vb.reshape(B, L, B_HEADS, B_DH)
    qi = partial_rope(qi.reshape(B, L, IDX_HEADS, IDX_DIM), pos, IDX_ROT)
    ki = partial_rope(layer_norm(ki, kn_g, kn_b)[:, :, None, :], pos, IDX_ROT)[:, :, 0, :]
    wi = wi * (IDX_HEADS ** -0.5 * IDX_DIM ** -0.5)
    return q, k, v, qi, ki, wi

def indexer_scores(qi, wi, ki, qpos, kpos):
    rel = jax.nn.relu(jnp.einsum('bthd,bsd->bths', qi.astype(jnp.float32), ki.astype(jnp.float32)))
    s = jnp.einsum('bths,bth->bts', rel, wi.astype(jnp.float32))
    return jnp.where(kpos[None, None, :] <= qpos[None, :, None], s, -jnp.inf)

def attend_selected(q, kg, vg, valid):
    logits = jnp.einsum('bthd,btkhd->bhtk', q.astype(jnp.float32), kg.astype(jnp.float32)) * (B_DH ** -0.5)
    logits = jnp.where(valid[:, None], logits, -jnp.inf)
    p = jax.nn.softmax(logits, axis=-1)
    return jnp.einsum('bhtk,btkhd->bthd', p, vg.astype(jnp.float32))

def dsa_prompt(q, k, v, qi, ki, wi):
    B, L = q.shape[:2]
    topk = min(TOPK_MAX, L // 4)
    blk = math.gcd(L, Q_BLOCK)
    kpos = jnp.arange(L, dtype=jnp.int32)
    gather = jax.vmap(lambda rows, idx: rows[idx])

    def one_block(i):
        start = i * blk
        qpos = start + jnp.arange(blk, dtype=jnp.int32)
        sl = lambda a: lax.dynamic_slice_in_dim(a, start, blk, axis=1)
        scores = indexer_scores(sl(qi), sl(wi), ki, qpos, kpos)
        _, sel = lax.top_k(scores, topk)
        valid = sel <= qpos[None, :, None]
        return attend_selected(sl(q), gather(k, sel), gather(v, sel), valid)

    o = lax.map(one_block, jnp.arange(L // blk))
    return o.transpose(1, 0, 2, 3, 4).reshape(B, L, B_HEADS, B_DH)

def dsa_sample(q, k, v, qi, ki, wi, cache_k, cache_v, cache_kidx, page_table, layer):
    Bd, T = q.shape[:2]
    n_pages = page_table.shape[1]
    page = cache_k.shape[2]
    past = n_pages * page
    L = past + T
    topk = min(TOPK_MAX, L // 4)
    ki_past = cache_kidx[page_table, layer].reshape(Bd, past, IDX_DIM)
    ki_all = jnp.concatenate([ki_past.astype(jnp.float32), ki.astype(jnp.float32)], axis=1)
    qpos = past + jnp.arange(T, dtype=jnp.int32)
    kpos = jnp.arange(L, dtype=jnp.int32)
    scores = indexer_scores(qi, wi, ki_all, qpos, kpos)
    _, sel = lax.top_k(scores, topk)
    valid = sel <= qpos[None, :, None]
    from_past = (sel < past)[..., None, None]
    p_sel = jnp.minimum(sel, past - 1)
    phys = jnp.take_along_axis(page_table, (p_sel // page).reshape(Bd, -1), axis=1).reshape(p_sel.shape)
    off = p_sel % page
    n_sel = jnp.clip(sel - past, 0, T - 1)
    gather = jax.vmap(lambda rows, idx: rows[idx])
    kg = jnp.where(from_past, cache_k[phys, layer, off].astype(jnp.float32), gather(k, n_sel).astype(jnp.float32))
    vg = jnp.where(from_past, cache_v[phys, layer, off].astype(jnp.float32), gather(v, n_sel).astype(jnp.float32))
    return attend_selected(q, kg, vg, valid)

def merge_and_norm(x, o_a, o_b, g_b, w_out_l, ln_g_l, ln_b_l):
    B, L, _ = x.shape
    o_b = o_b.reshape(B, L, B_WIDTH) * jax.nn.silu(g_b.astype(jnp.float32))
    mix = jnp.concatenate([o_a, o_b], axis=-1).astype(x.dtype)
    y = jnp.einsum('ble,ed->bld', mix, w_out_l)
    return layer_norm(ALPHA * x + y, ln_g_l, ln_b_l)

def layer_forward(x, pos, s0, attend, w_in_l, lb_l, norm_g_l, kn_g_l, kn_b_l, w_out_l, ln_g_l, ln_b_l):
    h = jnp.einsum('bld,de->ble', x, w_in_l)
    qa, fa, ia, ga, qb, kb, vb, gb, qi, ki, wi = jnp.split(h, IN_OFFSETS, axis=-1)
    o_a, s_new = hgrn2_branch(qa, fa, ia, ga, lb_l, norm_g_l, s0)
    q, k, v, qi, ki, wi = dsa_inputs(qb, kb, vb, qi, ki, wi, pos, kn_g_l, kn_b_l)
    o_b = attend(q, k, v, qi, ki, wi)
    x_new = merge_and_norm(x, o_a, o_b, gb, w_out_l, ln_g_l, ln_b_l)
    return x_new, k, v, ki, s_new

def setup_inputs(seed: int = 0) -> dict:
    key = jax.random.key(seed)
    ks = jax.random.split(key, 16)
    n_pages = PAST_LEN // PAGE_SIZE
    n_used = DEC_BATCH * n_pages
    n_pool = (n_used * 5) // 4
    f32 = jnp.float32
    nrm = lambda k, shape, s: s * jax.random.normal(k, shape, f32)
    page_table = jax.random.permutation(ks[0], n_pool)[:n_used].reshape(DEC_BATCH, n_pages).astype(jnp.int32)
    return {
        "x_prompt": nrm(ks[1], (BATCH, SEQ, D_MODEL), 1.0),
        "x_sample": nrm(ks[2], (DEC_BATCH, DEC_SEQ, D_MODEL), 1.0),
        "cache_k": nrm(ks[3], (n_pool, DEPTH, PAGE_SIZE, B_HEADS, B_DH), 1.0),
        "cache_v": nrm(ks[4], (n_pool, DEPTH, PAGE_SIZE, B_HEADS, B_DH), 1.0),
        "cache_kidx": nrm(ks[5], (n_pool, DEPTH, PAGE_SIZE, IDX_DIM), 1.0),
        "state_hgrn": nrm(ks[6], (DEPTH, DEC_BATCH, A_HEADS, A_DK, A_DV), 0.5),
        "page_table": page_table,
        "w_in": nrm(ks[7], (DEPTH, D_MODEL, D_IN), D_MODEL ** -0.5),
        "hgrn_lb_logits": nrm(ks[8], (DEPTH + 1, A_HEADS * A_DK), 0.5),
        "hgrn_norm_g": 1.0 + nrm(ks[9], (DEPTH, A_DV), 0.02),
        "idx_norm_g": 1.0 + nrm(ks[10], (DEPTH, IDX_DIM), 0.02),
        "idx_norm_b": nrm(ks[11], (DEPTH, IDX_DIM), 0.02),
        "w_out": nrm(ks[12], (DEPTH, D_MIX, D_MODEL), BETA * D_MIX ** -0.5),
        "ln_g": 1.0 + nrm(ks[13], (DEPTH, D_MODEL), 0.02),
        "ln_b": nrm(ks[14], (DEPTH, D_MODEL), 0.02),
    }

def reference(x_prompt, x_sample, cache_k, cache_v, cache_kidx, state_hgrn, page_table,
              w_in, hgrn_lb_logits, hgrn_norm_g, idx_norm_g, idx_norm_b, w_out, ln_g, ln_b):
    lbs = hgrn_lower_bounds(hgrn_lb_logits)
    B, L, _ = x_prompt.shape
    Bd, T, _ = x_sample.shape
    page = cache_k.shape[2]
    past = page_table.shape[1] * page
    pos_p = jnp.arange(L, dtype=jnp.int32)
    pos_s = past + jnp.arange(T, dtype=jnp.int32)
    s0_prompt = jnp.zeros((B, A_HEADS, A_DK, A_DV), jnp.float32)
    xp, xs = x_prompt, x_sample
    kp, vp, kip, sp = [], [], [], []
    ksm, vsm, kism, ssm = [], [], [], []
    for l in range(DEPTH):
        w_l = (w_in[l], lbs[l], hgrn_norm_g[l], idx_norm_g[l], idx_norm_b[l], w_out[l], ln_g[l], ln_b[l])
        xp, k, v, ki, s = layer_forward(xp, pos_p, s0_prompt, dsa_prompt, *w_l)
        kp.append(k.reshape(B, L // page, page, B_HEADS, B_DH))
        vp.append(v.reshape(B, L // page, page, B_HEADS, B_DH))
        kip.append(ki.reshape(B, L // page, page, IDX_DIM))
        sp.append(s)
        attend_s = functools.partial(dsa_sample, cache_k=cache_k, cache_v=cache_v,
                                     cache_kidx=cache_kidx, page_table=page_table, layer=l)
        xs, k, v, ki, s = layer_forward(xs, pos_s, state_hgrn[l], attend_s, *w_l)
        ksm.append(k)
        vsm.append(v)
        kism.append(ki)
        ssm.append(s)
    new_k_prompt = jnp.stack(kp, axis=2)
    new_v_prompt = jnp.stack(vp, axis=2)
    new_kidx_prompt = jnp.stack(kip, axis=2)
    new_state_prompt = jnp.stack(sp, axis=0)
    new_k_sample = jnp.stack(ksm, axis=1)
    new_v_sample = jnp.stack(vsm, axis=1)
    new_kidx_sample = jnp.stack(kism, axis=1)
    new_state_sample = jnp.stack(ssm, axis=0)
    return (xp, xs, new_k_prompt, new_v_prompt, new_kidx_prompt, new_state_prompt,
            new_k_sample, new_v_sample, new_kidx_sample, new_state_sample)


_drawn_inputs = setup_inputs


def setup_inputs(seed=0):
    import zlib

    import numpy as np

    out = dict(_drawn_inputs(seed))
    spreads = {}
    factors = {'cache_k': 3.409,
     'cache_v': 2.709,
     'cache_kidx': 2.885,
     'hgrn_norm_g': 23.886,
     'idx_norm_b': 2.765,
     'ln_g': 7.447,
     'ln_b': 7.844}
    for name, (base, spread) in spreads.items():
        noise = np.random.default_rng([zlib.crc32(name.encode()), seed]).standard_normal(out[name].shape)
        drawn = base * np.exp(spread * noise) if base else spread * noise
        out[name] = __import__('jax').numpy.asarray(drawn.astype(out[name].dtype))
    for name, factor in factors.items():
        out[name] = (out[name] * factor).astype(out[name].dtype)
    return out
```

```python
from contextlib import ExitStack

import numpy as np
import concourse.bass as bass
from concourse import mybir

ALU = mybir.AluOpType
ACT = mybir.ActivationFunctionType
F32 = mybir.dt.float32
BF16 = mybir.dt.bfloat16
I32 = mybir.dt.int32
U8 = mybir.dt.uint8
AX = mybir.AxisListType

P = 128
D = 1024
SEQ = 512
NSEQ, NNEW = 8, 8
NS = NSEQ * NNEW
TOK = SEQ + NS
NT = SEQ // P
KC = D // P
HA = 4
HB, DH = 8, 64
HI = 16
PAGE, NPG = 128, 16
PAST = PAGE * NPG
W2 = HB * DH
LS = PAST + NS
TOPK_P, TOPK_S = min(256, SEQ // 4), min(256, (PAST + NNEW) // 4)
G_QA, G_FA, G_IA, G_GA = 0, 512, 1024, 1536
G_QB, G_KB, G_VB, G_GB, G_QI, G_KI = 2048, 2560, 3072, 3584, 4096, 5120
EPS = 1e-5
ALPHA = 2.0 ** 0.25
ROT = 8
TAKEN = -3.0e38
MASKED = -1.0e30
LEVELS = [0, 1, 2, 4, 8, 16, 32, 64]
POFF = [0, 128, 384, 768]
PW = 1280


def shape_constants():
    c = {}
    c["ident"] = np.eye(P, dtype=np.float32)
    half = ROT
    inv = np.float32(500000.0) ** (-np.arange(half, dtype=np.float32) / np.float32(half))
    pos = np.concatenate([np.arange(SEQ), np.tile(PAST + np.arange(NNEW), NSEQ)]).astype(np.float32)
    ang = (pos[:, None] * inv[None, :]).astype(np.float32)
    cs = np.concatenate([np.cos(ang), np.sin(ang)], 1).astype(np.float32)
    rope = np.zeros((P, NT + 1, 2 * half), np.float32)
    for t in range(NT):
        rope[:, t] = cs[t * P:(t + 1) * P]
    rope[:NS, NT] = cs[SEQ:]
    c["rope"] = rope
    q, k = np.arange(P)[:, None], np.arange(P)[None, :]
    tri = (k <= q)
    c["tri"] = np.stack([tri.astype(np.float32), np.where(tri, 0, TAKEN).astype(np.float32),
                         np.where(tri, 0, MASKED).astype(np.float32)], 1)
    sq, sk = np.arange(NS)[:, None], np.arange(NS)[None, :]
    own = (sq // NNEW == sk // NNEW) & (sk % NNEW <= sq % NNEW)
    c["own"] = np.stack([own.astype(np.float32), np.where(own, 0, TAKEN).astype(np.float32),
                         np.where(own, 0, MASKED).astype(np.float32)], 1)
    pick = np.zeros((NS, NSEQ, 4, 32), np.float32)
    for s in range(NSEQ):
        for qq in range(NNEW):
            for hh in range(2):
                pick[s * NNEW + qq, s, :, hh * NNEW + qq] = 1
    c["pick"] = pick.reshape(NS, NSEQ * P)
    c["sameq"] = (np.arange(P)[:, None] % NNEW == np.arange(NS)[None, :] % NNEW).astype(np.float32)
    lv = np.zeros((P, len(LEVELS), P), np.float32)
    s, t = np.arange(P)[:, None], np.arange(P)[None, :]
    for i, b in enumerate(LEVELS):
        lv[:, i] = (s == t) if b == 0 else ((s // (2 * b) == t // (2 * b)) & (s % (2 * b) < b) & (t % (2 * b) >= b))
    c["levels"] = lv.reshape(P, len(LEVELS) * P)
    keep = np.ones((P, TOK), np.float32)
    keep[:, 0:SEQ:P] = 0
    keep[:, SEQ::NNEW] = 0
    c["keep"] = keep
    c["seqcols"] = np.broadcast_to(np.repeat(np.eye(NSEQ, dtype=np.float32), NNEW, 1).reshape(1, -1),
                                   (P, NSEQ * NS)).copy()
    c["ofseq"] = (np.arange(NS)[:, None] // NNEW == np.arange(NSEQ)[None, :]).astype(np.float32)
    return c


def begin(e, *given):
    for sem in given:
        e.sem_inc(sem, 1)


def after(e, sem, n):
    e.wait_ge(sem, n + 1)


class Tally:

    def __init__(self, eng, sem, n=0):
        self.eng, self.sem, self.n = eng, sem, n

    def add(self, ins):
        ins.then_inc(self.sem, 1)
        self.n = self.n + 1

    def wait(self):
        self.eng.wait_ge(self.sem, self.n)

    def link(self, ins):
        self.add(ins)
        self.wait()


def hybrid_step(nc, x_prompt, x_sample, cache_k, cache_v, cache_kidx, state_hgrn, page_table,
                w_in, hgrn_lb_logits, hgrn_norm_g, idx_norm_g, idx_norm_b, w_out, ln_g, ln_b,
                c_ident, c_rope, c_tri, c_own, c_pick, c_sameq, c_levels, c_keep, c_seqcols, c_ofseq,
                y_prompt, y_sample, k_prompt, v_prompt, ki_prompt, st_prompt,
                k_sample, v_sample, ki_sample, st_sample):
    scratch = nc.dram_tensor("decode_scores", (NSEQ, NNEW, LS), F32, kind="Internal").ap()
    w_rows = w_in[0].rearrange("(c p) n -> p c n", p=P)
    wo_rows = w_out[0].rearrange("(c p) n -> p c n", p=P)
    xp_rows = x_prompt[0].rearrange("(t p) d -> t p d", p=P)
    xs_rows = x_sample.rearrange("s t d -> (s t) d")

    with ExitStack() as ctx:
        def sb(name, shape, dt=F32):
            return ctx.enter_context(nc.sbuf_tensor(name, shape, dt))

        def sem(name):
            return ctx.enter_context(nc.semaphore(name))

        def sems(name, n):
            return [sem(f"{name}{i}") for i in range(n)]

        ident = sb("ident", [P, P])
        rope = sb("rope", [P, NT + 1, 2 * ROT])
        tri = sb("tri", [P, 3, P])
        own = sb("own", [NS, 3, NS])
        pick = sb("pick", [NS, NSEQ * P], BF16)
        sameq = sb("sameq", [P, NS])
        keep = sb("keep", [P, TOK])
        ofseq = sb("ofseq", [NS, NSEQ])
        gki = sb("gki", [P, 2, DH])
        pages = sb("pages", [1, NSEQ * NPG], I32)
        xT = sb("xT", [P, KC, TOK])
        qT = sb("qT", [P, 4, TOK])
        kT = sb("kT", [P, 4, TOK])
        v_tok = sb("v_tok", [P, NT + 1, W2])
        gB = sb("gB", [P, NT + 1, W2])
        bias_s = sb("bias_s", [NS, LS], BF16)
        bias_p = sb("bias_p", [P, PW])
        small = sb("small", [P, 128])
        wbuf = sb("wbuf", [P, 2, KC, 512])
        ARENA = 25600
        arena = sb("arena", [P, ARENA])
        at = [0]

        def carve(n):
            a = at[0]
            at[0] += n
            assert at[0] <= ARENA, at[0]
            return arena[:, a:a + n]

        psum = ctx.enter_context(nc.psum_tensor("banks", [P, 8, 512], F32))

        at[0] = 0
        qi_tok = carve((NT + 1) * D).rearrange("p (t n) -> p t n", n=D)
        k_tok = qi_tok[:, :, 0:W2]
        q_tok = qi_tok[:, :, W2:D]
        qiT = carve(8 * SEQ).rearrange("p (c n) -> p c n", c=8)
        pick_f = qiT[0:NS, 0:2].rearrange("p c n -> p (c n)")
        qis = carve(NSEQ * P).rearrange("p (s h q) -> p s h q", s=NSEQ, h=HI)
        kidx = [carve(NPG * DH).rearrange("p (g n) -> p g n", n=DH) for _ in range(2)]
        kxT = [carve(PAST // 2) for _ in range(2)]
        kiT = carve(TOK)
        relu_s = carve(LS)
        relu_p = carve(4 * 512).rearrange("p (b n) -> p b n", b=4)
        S = carve(LS)[0:NS]
        SP = {b: carve((b + 1) * P) for b in (1, 2, 3)}
        kiwi = carve((NT + 1) * 80).rearrange("p (t n) -> p t n", n=80)
        kin = carve((NT + 1) * DH).rearrange("p (t n) -> p t n", n=DH)
        w_all = carve(NS)
        w_rep = carve(P)[0:NS]
        qstat = [carve(P) for _ in range(2)]
        wstat = [carve(32) for _ in range(2)]
        stage = carve(512)
        stage_n = carve(NS)[0:32]
        rtmp = carve(4 * HI * ROT).rearrange("p (a n) -> p a n", a=4)
        stats = carve((NT + 1) * 6).rearrange("p (t n) -> p t n", n=6)
        mv = carve((NT + 1) * 2).rearrange("p (t n) -> p t n", n=2)
        rstd = carve(NT + 1)
        best = carve(4 * 8).rearrange("p (a n) -> p a n", a=4)
        newbias = carve(NS)[0:NS]
        xin = arena[:, ARENA - 5 * D:ARENA].rearrange("p (t n) -> p t n", n=D)
        assert at[0] <= ARENA

        const_in, pages_in, ki_par_in = sem("const_in"), sem("pages_in"), sem("ki_par_in")
        x_in = sems("x_in", NT + 1)
        x_tr, x_ev = sem("x_tr"), sem("x_ev")
        w_got = sems("w_got", 2)
        proj, proj_ev = sem("proj"), sem("proj_ev")
        var_ok, std_ok, kin_ok = sem("var_ok"), sem("std_ok"), sem("kin_ok")
        act_own, dve_own, pool_own = sem("act_own"), sem("dve_own"), sem("pool_own")
        roped = sem("roped")
        wrep_ok = sem("wrep_ok")
        tr, tr_ev = sem("tr"), sem("tr_ev")
        tr2, tr2_ev = sem("tr2"), sem("tr2_ev")
        kidx_in, kidx_tr, kidx_ev = sems("kidx_in", 2), sem("kidx_tr"), sem("kidx_ev")
        stat_ok, rel, relu_ok, comb, comb_ev, staged = (sem("stat_ok"), sem("rel"), sem("relu_ok"),
                                                        sem("comb"), sem("comb_ev"), sem("staged"))
        prel, prelu, pacc = sem("prel"), sem("prelu"), sem("pacc")
        s_in, topk = sem("s_in"), sem("topk")
        stored = sem("stored")
        NSTORE = [0]
        dve_count, pool_count = [0], [0]

        ROWS = [P] * NT + [NS]
        GROUPS = [(G_KI, 80), (G_QI, 512), (G_QI + 512, 512), (G_VB, 512), (G_KB, 512), (G_QB, 512), (G_GB, 512)]
        BEFORE = 4
        PB = 4
        TB = 4
        CB, NB = 6, 7

        NCONST = 7 * 16

        with nc.Block() as block:
            @block.sync
            def _(sp):
                sp.dma_start(ident[:], c_ident).then_inc(const_in, 16)
                for t in range(NT + 1):
                    src = xp_rows[t] if t < NT else xs_rows
                    sp.dma_start(xin[0:ROWS[t], t, :], src).then_inc(x_in[t], 16)

                def load_w(g):
                    c0, w = GROUPS[g]
                    if g >= 2:
                        sp.wait_ge(proj, (NT + 1) * (g - 1))
                    sp.dma_start(wbuf[:, g % 2, :, 0:w], w_rows[:, :, c0:c0 + w]).then_inc(w_got[g % 2], 16)

                load_w(0)
                load_w(1)
                for dst, src in ((rope, c_rope), (tri, c_tri), (own, c_own),
                                 (sameq, c_sameq), (keep, c_keep), (pick_f, c_pick)):
                    sp.dma_start(dst[:], src).then_inc(const_in, 16)
                sp.dma_start(gki[:, 0, :], idx_norm_g.partition_broadcast(P)).then_inc(ki_par_in, 16)
                sp.dma_start(gki[:, 1, :], idx_norm_b.partition_broadcast(P)).then_inc(ki_par_in, 16)
                sp.dma_start(pages[:], page_table.rearrange("s g -> (s g)").rearrange("(a n) -> a n", a=1)).then_inc(pages_in, 16)
                for g in range(2, BEFORE + 2):
                    load_w(g)
                sp.wait_ge(pages_in, 16)
                with sp.Fori(0, NSEQ // 2) as i:
                    for u in range(2):
                        sp.wait_ge(kidx_tr, i * 4 + 2 * u + 2)
                        for g in range(NPG):
                            pg = sp.value_load(pages[0:1, bass.ds((i * 2 + u) * NPG + g, 1)], min_val=0,
                                               max_val=cache_kidx.shape[0] - 1)
                            sp.dma_start(kidx[u][:, (g % 8) * 2 + g // 8, :],
                                         cache_kidx[bass.ds(pg, 1), 0].rearrange("a p d -> p (a d)")
                                         ).then_inc(kidx_in[u], 16)
                for g in range(BEFORE + 2, len(GROUPS)):
                    load_w(g)
                sp.wait_ge(staged, 16 * 5 * NSEQ + 16)
                sp.dma_start(S, scratch.rearrange("s q n -> (s q) n")).then_inc(s_in, 16)

            def pe_project(pe, g):
                pe.wait_ge(w_got[g % 2], 16 * (g // 2 + 1))
                w = GROUPS[g][1]
                for t in range(NT + 1):
                    n = g * (NT + 1) + t
                    if n >= PB:
                        pe.wait_ge(proj_ev, n - PB + 1)
                    for c in range(KC):
                        mm = pe.matmul(psum[0:ROWS[t], n % PB, 0:w], xT[:, c, t * P:t * P + ROWS[t]],
                                       wbuf[:, g % 2, c, 0:w], start=(c == 0), stop=(c == KC - 1))
                    mm.then_inc(proj, 1)

            @block.tensor
            def _(pe):
                pe.wait_ge(const_in, 16)
                for t in range(NT + 1):
                    pe.wait_ge(x_in[t], 16)
                    for h in range(2):
                        n = 2 * t + h
                        if n >= PB:
                            pe.wait_ge(x_ev, n - PB + 1)
                        for c in range(4):
                            mm = pe.transpose(psum[:, n % PB, c * P:c * P + ROWS[t]],
                                              xin[0:ROWS[t], t, (4 * h + c) * P:(4 * h + c + 1) * P],
                                              ident[0:ROWS[t], 0:ROWS[t]])
                        mm.then_inc(x_tr, 1)
                pe.wait_ge(x_ev, 2 * (NT + 1))
                for g in range(BEFORE):
                    pe_project(pe, g)

                job = 0

                def take_bank():
                    if job >= 2:
                        pe.wait_ge(tr_ev, job - 1)
                    return TB + job % 2

                pe.wait_ge(roped, NT + 1)
                b = take_bank()
                for t in range(NT):
                    mm = pe.transpose(psum[0:DH, b, t * P:(t + 1) * P], kin[:, t, :], ident[:])
                mm.then_inc(tr, 1)
                job += 1
                b = take_bank()
                pe.transpose(psum[0:DH, b, 0:NS], kin[0:NS, NT, :], ident[0:NS, 0:NS]).then_inc(tr, 1)
                job += 1
                b = take_bank()
                pe.wait_ge(wrep_ok, 1)
                pe.matmul(psum[:, b, 0:NS], w_rep, ident[0:NS, 0:NS], start=True, stop=True).then_inc(tr, 1)
                job += 1
                for t in range(NT):
                    pe.wait_ge(roped, NT + 1 + t + 1)
                    for h in range(2):
                        b = take_bank()
                        for c in range(4):
                            mm = pe.transpose(psum[:, b, c * P:(c + 1) * P],
                                              qi_tok[:, t, (4 * h + c) * P:(4 * h + c + 1) * P], ident[:])
                        mm.then_inc(tr, 1)
                        job += 1
                pe.wait_ge(roped, 2 * (NT + 1))
                for h in range(2):
                    b = take_bank()
                    for c in range(8):
                        mm = pe.transpose(psum[0:DH, b, c * NS:(c + 1) * NS],
                                          qi_tok[0:NS, NT, (8 * h + c) * DH:(8 * h + c + 1) * DH],
                                          ident[0:NS, 0:NS])
                    mm.then_inc(tr, 1)
                    job += 1
                NJ = job
                pe.wait_ge(tr_ev, NJ)
                begin(pe, rel, comb)
                pe.sem_inc(kidx_tr, 4)
                pe.wait_ge(proj_ev, BEFORE * (NT + 1))

                with pe.Fori(0, NSEQ // 2) as i:
                    def keys(u):
                        pe.wait_ge(kidx_in[u], i * (16 * NPG) + 16 * NPG)
                        after(pe, kidx_ev, i * 4 + 2 * u)
                        for b in range(2):
                            for c in range(4):
                                mm = pe.transpose(psum[:, TB + b, c * P:(c + 1) * P],
                                                  kidx[u][:, 8 * b + 2 * c:8 * b + 2 * c + 2, :], ident[:])
                            mm.then_inc(kidx_tr, 1)

                    def relevance(u):
                        pe.wait_ge(stat_ok, i * 4 + 2 * u + 2)
                        after(pe, kidx_ev, i * 4 + 2 * u + 2)
                        after(pe, relu_ok, i * 10 + 5 * u)
                        for b in range(2):
                            for h in range(2):
                                pe.matmul(psum[:, 2 * h + b, :], qstat[u][DH * h:DH * h + DH, :],
                                          kxT[u][DH * h:DH * h + DH, b * 512:(b + 1) * 512],
                                          start=True, stop=True).then_inc(rel, 1)
                        after(pe, comb_ev, i * 4 + 2 * u)
                        pe.matmul(psum[:, NB, 0:NS], qstat[u][0:DH, :], kiT[0:DH, SEQ:TOK],
                                  start=True, stop=True).then_inc(rel, 1)

                    def combine(u):
                        after(pe, comb_ev, i * 4 + 2 * u)
                        after(pe, relu_ok, i * 10 + 5 * u + 5)
                        for g in range(4):
                            mm = pe.matmul(psum[32 * g:32 * g + 32, CB, :], wstat[u], relu_s[:, g * 512:(g + 1) * 512],
                                           start=True, stop=True)
                        mm.then_inc(comb, 1)
                        pe.matmul(psum[0:32, NB, NS:2 * NS], wstat[u], relu_s[:, PAST:LS],
                                  start=True, stop=True).then_inc(comb, 1)

                    keys(0)
                    relevance(0)
                    keys(1)
                    combine(0)
                    relevance(1)
                    combine(1)

                after(pe, relu_ok, 5 * NSEQ)
                n = 0
                for b in (1, 2, 3):
                    w = (b + 1) * P
                    for c in range(8):
                        for h in range(2):
                            if n >= 4:
                                pe.wait_ge(prelu, n - 3)
                            pe.matmul(psum[:, n % 4, 0:w], qiT[DH * h:DH * h + DH, c, b * P:(b + 1) * P],
                                      kiT[DH * h:DH * h + DH, 0:w], start=True, stop=True).then_inc(prel, 1)
                            n += 1
                pe.wait_ge(prelu, n)

                job = 0

                def turn(src, t):
                    nonlocal job
                    if job >= 2:
                        pe.wait_ge(tr2_ev, job - 1)
                    for c in range(4):
                        mm = pe.transpose(psum[:, TB + job % 2, c * P:c * P + ROWS[t]],
                                          src[0:ROWS[t], t, c * P:(c + 1) * P],
                                          ident[0:ROWS[t], 0:ROWS[t]])
                    mm.then_inc(tr2, 1)
                    job += 1

                pe_project(pe, 4)
                pe_project(pe, 5)
                for t in range(NT + 1):
                    pe.wait_ge(roped, 2 * (NT + 1) + t + 1)
                    turn(k_tok, t)
                pe_project(pe, 6)
                for t in range(NT + 1):
                    pe.wait_ge(roped, 3 * (NT + 1) + t + 1)
                    turn(q_tok, t)

            def act_evac(act, g):
                dest = (kiwi, qi_tok[:, :, 0:512], qi_tok[:, :, 512:1024], v_tok, k_tok, q_tok, gB)[g]
                w = GROUPS[g][1]
                for t in range(NT + 1):
                    n = g * (NT + 1) + t
                    act.wait_ge(proj, n + 1)
                    if g == 4 and t == 0:
                        act.wait_ge(tr, 13)
                    o, i_ = dest[0:ROWS[t], t, 0:w], psum[0:ROWS[t], n % PB, 0:w]
                    if g == 6:
                        ins = nc.scalar.activation(o, i_, ACT.Silu)
                    elif g == 5:
                        ins = nc.scalar.mul(o, i_, DH ** -0.5)
                    else:
                        ins = nc.scalar.copy(o, i_)
                    ins.then_inc(proj_ev, 1)

            @block.scalar
            def _(act):
                for n in range(2 * (NT + 1)):
                    t, h = n // 2, n % 2
                    act.wait_ge(x_tr, n + 1)
                    nc.scalar.copy(xT[:, 4 * h:4 * h + 4, t * P:t * P + ROWS[t]],
                                   psum[:, n % PB, :].rearrange("p (c n) -> p c n", c=4)[:, :, 0:ROWS[t]]
                                   ).then_inc(x_ev, 1)
                act_evac(act, 0)
                act_evac(act, 1)
                act.wait_ge(var_ok, 1)
                nc.scalar.activation(rstd[:, :], mv[:, :, 1], ACT.Sqrt).then_inc(std_ok, 1)
                act_evac(act, 2)
                act_evac(act, 3)
                begin(act, relu_ok)
                with act.Fori(0, NSEQ // 2) as i:
                    for u in range(2):
                        for g in (0, 2, 1, 3):
                            k = (0, 2, 1, 3).index(g)
                            after(act, rel, i * 10 + 5 * u + k + 1)
                            if k == 0:
                                after(act, comb, i * 4 + 2 * u)
                            nc.scalar.activation(relu_s[:, g * 512:(g + 1) * 512], psum[:, g, :],
                                                 ACT.Relu).then_inc(relu_ok, 1)
                        after(act, rel, i * 10 + 5 * u + 5)
                        nc.scalar.activation(relu_s[:, PAST:LS], psum[:, NB, 0:NS], ACT.Relu).then_inc(relu_ok, 1)
                n = 0
                for b in (1, 2, 3):
                    for h in range(HI):
                        act.wait_ge(prel, n + 1)
                        if n >= 4:
                            act.wait_ge(pacc, n - 3)
                        nc.scalar.activation(relu_p[:, n % 4, 0:(b + 1) * P], psum[:, n % 4, 0:(b + 1) * P],
                                             ACT.Relu).then_inc(prelu, 1)
                        n += 1
                act_evac(act, 4)
                act_evac(act, 5)

                def evac(dst, t, job):
                    act.wait_ge(tr2, job + 1)
                    nc.scalar.copy(dst[:, :, t * P:t * P + ROWS[t]],
                                   psum[:, TB + job % 2, :].rearrange("p (c n) -> p c n", c=4)[:, :, 0:ROWS[t]]
                                   ).then_inc(tr2_ev, 1)

                for t in range(NT + 1):
                    evac(kT, t, t)
                act_evac(act, 6)
                for t in range(NT + 1):
                    evac(qT, t, NT + 1 + t)

            @block.vector
            def _(dve):
                me = Tally(dve, dve_own)
                dve.wait_ge(x_ev, 2 * (NT + 1))
                me.link(nc.vector.memset(mv[:], 1.0))
                for t in range(NT + 1):
                    dve.wait_ge(proj_ev, t + 1)
                    me.add(nc.vector.bn_stats(stats[0:ROWS[t], t, :], kiwi[0:ROWS[t], t, 0:DH]))
                me.wait()
                for t in range(NT + 1):
                    me.add(nc.vector.bn_aggr(mv[0:ROWS[t], t, :], stats[0:ROWS[t], t, :]))
                me.wait()
                nc.vector.tensor_scalar(mv[:, :, 1], mv[:, :, 1], EPS, None, ALU.add).then_inc(var_ok, 1)
                nc.vector.tensor_scalar(w_rep.rearrange("p (h q) -> p h q", h=HI),
                                        kiwi[0:NS, NT, DH:DH + HI].unsqueeze(2).to_broadcast([NS, HI, NNEW]),
                                        (HI * DH) ** -0.5, None, ALU.mult).then_inc(wrep_ok, 1)
                me.add(nc.vector.tensor_scalar(kiwi[:, 0:NT, DH:DH + HI], kiwi[:, 0:NT, DH:DH + HI],
                                               (HI * DH) ** -0.5, None, ALU.mult))
                for u in range(2):
                    me.add(nc.vector.memset(wstat[u], 0.0))
                dve.wait_ge(std_ok, 1)
                me.link(nc.vector.reciprocal(rstd[:, :], rstd[:, :]))
                dve.wait_ge(ki_par_in, 32)
                for t in range(NT + 1):
                    r = ROWS[t]
                    me.link(nc.vector.tensor_scalar(kin[0:r, t, :], kiwi[0:r, t, 0:DH], mv[0:r, t, 0:1],
                                                    rstd[0:r, t:t + 1], ALU.subtract, ALU.mult))
                    me.link(nc.vector.tensor_tensor(kin[0:r, t, :], kin[0:r, t, :], gki[0:r, 0, :], ALU.mult))
                    nc.vector.tensor_tensor(kin[0:r, t, :], kin[0:r, t, :], gki[0:r, 1, :], ALU.add).then_inc(kin_ok, 1)
                dve.wait_ge(const_in, NCONST)
                me.link(nc.vector.tensor_copy(pick[:], pick_f))
                job = 0

                def both(cols, view):
                    for h in range(2):
                        ins = nc.vector.tensor_copy(cols(h), view)
                        if h == 0:
                            me.add(ins)
                    ins.then_inc(tr_ev, 1)

                dve.wait_ge(tr, 1)
                both(lambda h: kiT[DH * h:DH * h + DH, 0:SEQ], psum[0:DH, TB, :])
                dve.wait_ge(tr, 2)
                both(lambda h: kiT[DH * h:DH * h + DH, SEQ:TOK], psum[0:DH, TB + 1, 0:NS])
                dve.wait_ge(tr, 3)
                dve.wait_ge(const_in, NCONST)
                nc.vector.tensor_tensor(w_all, psum[:, TB, 0:NS], sameq[:], ALU.mult).then_inc(tr_ev, 1)
                job = 3
                for t in range(NT):
                    for h in range(2):
                        dve.wait_ge(tr, job + 1)
                        nc.vector.tensor_copy(qiT[:, 4 * h:4 * h + 4, t * P:(t + 1) * P],
                                              psum[:, TB + job % 2, :].rearrange("p (c n) -> p c n", c=4)
                                              ).then_inc(tr_ev, 1)
                        job += 1
                for h in range(2):
                    dve.wait_ge(tr, job + 1)
                    both(lambda a: qis[DH * a:DH * a + DH, :, 8 * h:8 * h + 8, :].rearrange("p s h q -> p h s q"),
                         psum[0:DH, TB + job % 2, :].rearrange("p (h s q) -> p h s q", h=8, s=NSEQ))
                    job += 1
                me.wait()
                begin(dve, kidx_ev, comb_ev)
                with dve.Fori(0, NSEQ // 2) as i:
                    def keys_out(u):
                        for b in range(2):
                            dve.wait_ge(kidx_tr, i * 4 + 2 * u + b + 5)
                            if b == 0:
                                after(dve, rel, i * 10 + 5 * u)
                            nc.vector.tensor_copy(kxT[u][:, b * 512:(b + 1) * 512],
                                                  psum[:, TB + b, :]).then_inc(kidx_ev, 1)

                    def sums_out(u):
                        after(dve, comb, i * 4 + 2 * u + 2)
                        dve.wait_ge(staged, i * 160 + 80 * u + 16)
                        nc.vector.tensor_copy(stage, psum[:, CB, :]).then_inc(comb_ev, 1)
                        nc.vector.tensor_copy(stage_n, psum[0:32, NB, NS:2 * NS]).then_inc(comb_ev, 1)

                    keys_out(0)
                    keys_out(1)
                    sums_out(0)
                    sums_out(1)
                n = 0
                for b in (1, 2, 3):
                    for h in range(HI):
                        dve.wait_ge(prelu, n + 1)
                        wcol = kiwi[:, b, DH + h:DH + h + 1]
                        src = relu_p[:, n % 4, 0:(b + 1) * P]
                        if h == 0:
                            nc.vector.tensor_scalar(SP[b], src, wcol, None, ALU.mult).then_inc(pacc, 1)
                        else:
                            dve.wait_ge(pacc, n)
                            nc.vector.scalar_tensor_tensor(SP[b], src, wcol, SP[b], ALU.mult, ALU.add).then_inc(pacc, 1)
                        n += 1
                dve.wait_ge(pacc, n)
                for b in (1, 2, 3):
                    me.add(nc.vector.tensor_tensor(SP[b][:, b * P:], SP[b][:, b * P:], tri[:, 0, :], ALU.mult))
                dve.wait_ge(s_in, 16)
                me.add(nc.vector.tensor_tensor(S[:, PAST:], S[:, PAST:], own[:, 0, :], ALU.mult))
                me.wait()
                nc.vector.tensor_tensor(S[:, PAST:], S[:, PAST:], own[:, 1, :], ALU.add).then_inc(topk, 1)
                for b in (1, 2, 3):
                    nc.vector.tensor_tensor(SP[b][:, b * P:], SP[b][:, b * P:], tri[:, 1, :], ALU.add).then_inc(topk, 1)
                sets = [(S, best[0:NS, 0, :])] + [(SP[b], best[:, b, :]) for b in (1, 2, 3)]

                def hold(value):
                    dve.wait_ge(topk, value)
                    nc.vector.memset(small[:, 100:101], 0.0)

                with dve.Fori(0, TOPK_P // 8) as r:
                    hold(r * 8 + 4)
                    for s, m in sets:
                        nc.vector.max(m, s).then_inc(topk, 1)
                    hold(r * 8 + 8)
                    for s, m in sets:
                        nc.vector.match_replace(s, m, s, TAKEN).then_inc(topk, 1)
                base = 4 + TOPK_P
                with dve.Fori(0, (TOPK_S - TOPK_P) // 8) as r:
                    hold(r * 2 + base)
                    nc.vector.max(sets[0][1], S).then_inc(topk, 1)
                    hold(r * 2 + base + 1)
                    nc.vector.match_replace(S, sets[0][1], S, TAKEN).then_inc(topk, 1)
                dve.wait_ge(topk, base + (TOPK_S - TOPK_P) // 4)
                me.add(nc.vector.tensor_scalar(bias_s[:, 0:PAST], S[:, 0:PAST], 0.9 * TAKEN, MASKED, ALU.is_gt, ALU.mult))
                me.add(nc.vector.tensor_scalar(newbias, S[:, PAST:], 0.9 * TAKEN, MASKED, ALU.is_gt, ALU.mult))
                me.add(nc.vector.tensor_copy(bias_p[:, 0:P], tri[:, 2, :]))
                for b in (1, 2, 3):
                    me.add(nc.vector.tensor_scalar(bias_p[:, POFF[b]:POFF[b] + (b + 1) * P], SP[b], 0.9 * TAKEN,
                                                   MASKED, ALU.is_gt, ALU.mult))
                me.wait()
                me.add(nc.vector.tensor_tensor(bias_s[:, PAST:], newbias, own[:, 2, :], ALU.add))
                for b in (1, 2, 3):
                    d = bias_p[:, POFF[b] + b * P:POFF[b] + (b + 1) * P]
                    me.add(nc.vector.tensor_tensor(d, d, tri[:, 2, :], ALU.add))
                me.wait()
                dve_count[0] = me.n

            @block.gpsimd
            def _(pool):
                me = Tally(pool, pool_own)
                pool.dma_start(ofseq[:], c_ofseq).then_inc(staged, 16)
                pool.wait_ge(const_in, NCONST)

                def rotate(view, r, t, heads, scaled=False):
                    x1, x2 = view[:, :, 0:ROT], view[:, :, ROT:2 * ROT]
                    shape = [r, heads, ROT]
                    cos = rope[0:r, t, 0:ROT].unsqueeze(1).to_broadcast(shape)
                    sin = rope[0:r, t, ROT:2 * ROT].unsqueeze(1).to_broadcast(shape)
                    tmp = [rtmp[0:r, a, 0:heads * ROT].rearrange("p (h n) -> p h n", h=heads) for a in range(4)]
                    for a, (x, w) in enumerate(((x1, cos), (x2, sin), (x1, sin), (x2, cos))):
                        me.add(nc.gpsimd.tensor_tensor(tmp[a], x, w, ALU.mult))
                    me.wait()
                    me.add(nc.gpsimd.tensor_tensor(x1, tmp[0], tmp[1], ALU.subtract))
                    me.wait()
                    nc.gpsimd.tensor_tensor(x2, tmp[2], tmp[3], ALU.add).then_inc(roped, 1)

                def store(dst, src):
                    pool.dma_start(dst, src).then_inc(stored, 16)
                    NSTORE[0] += 16

                n = 0
                for t in range(NT + 1):
                    r = ROWS[t]
                    pool.wait_ge(kin_ok, t + 1)
                    if n:
                        pool.wait_ge(roped, n)
                    rotate(kin[0:r, t, :].unsqueeze(1), r, t, 1)
                    n += 1
                pool.wait_ge(roped, n)
                for t in range(NT):
                    store(ki_prompt[0, t, 0], kin[:, t, :])
                store(ki_sample[:, 0].rearrange("s t d -> (s t) d"), kin[0:NS, NT, :])
                for t in range(NT + 1):
                    r = ROWS[t]
                    pool.wait_ge(proj_ev, 2 * (NT + 1) + t + 1)
                    pool.wait_ge(roped, n)
                    rotate(qi_tok[0:r, t, :].rearrange("p (h d) -> p h d", h=HI), r, t, HI)
                    n += 1
                for t in range(NT + 1):
                    pool.wait_ge(proj_ev, 3 * (NT + 1) + t + 1)
                    if t < NT:
                        store(v_prompt[0, t, 0].rearrange("p h d -> p (h d)"), v_tok[:, t, :])
                    else:
                        store(v_sample[:, 0].rearrange("s t h d -> (s t) (h d)"), v_tok[0:NS, NT, :])
                pool.wait_ge(tr_ev, 13)
                with pool.Fori(0, NSEQ // 2) as i:
                    for u in range(2):
                        after(pool, comb, i * 4 + 2 * u)
                        nc.gpsimd.tensor_copy(qstat[u].unsqueeze(1), qis[:, bass.ds(i * 2 + u, 1)].rearrange(
                            "p s h q -> p s (h q)")).then_inc(stat_ok, 1)
                        nc.gpsimd.tensor_copy(wstat[u][:, 0:NNEW],
                                              w_all[:, bass.ds((i * 2 + u) * NNEW, NNEW)]).then_inc(stat_ok, 1)
                        after(pool, comb_ev, i * 4 + 2 * u + 2)
                        for g in range(4):
                            pool.dma_start(scratch[bass.ds(i * 2 + u, 1), :, g * 512:(g + 1) * 512].rearrange(
                                "s q n -> (s q) n"), stage[32 * g:32 * g + NNEW, :]).then_inc(staged, 16)
                        pool.dma_start(scratch[bass.ds(i * 2 + u, 1), :, PAST:LS].rearrange("s q n -> (s q) n"),
                                       stage_n[0:NNEW, :]).then_inc(staged, 16)
                for t in range(NT + 1):
                    r = ROWS[t]
                    pool.wait_ge(proj_ev, 4 * (NT + 1) + t + 1)
                    pool.wait_ge(roped, n)
                    rotate(k_tok[0:r, t, :].rearrange("p (h d) -> p h d", h=HB), r, t, HB)
                    n += 1
                pool.wait_ge(roped, n)
                for t in range(NT):
                    store(k_prompt[0, t, 0].rearrange("p h d -> p (h d)"), k_tok[:, t, :])
                store(k_sample[:, 0].rearrange("s t h d -> (s t) (h d)"), k_tok[0:NS, NT, :])
                for t in range(NT + 1):
                    r = ROWS[t]
                    pool.wait_ge(proj_ev, 5 * (NT + 1) + t + 1)
                    pool.wait_ge(roped, n)
                    rotate(q_tok[0:r, t, :].rearrange("p (h d) -> p h d", h=HB), r, t, HB)
                    n += 1
                pool_count[0] = me.n
        at[0] = 0
        aF = carve(8 * TOK).rearrange("p (c n) -> p c n", c=8)
        aT = carve((NT + 1) * D).rearrange("p (t n) -> p t n", n=D)
        osb = carve(NSEQ * P).rearrange("p (s n) -> p s n", n=P)
        KEEP2 = at[0]
        k_buf = [carve(4 * W2).rearrange("p (g n) -> p g n", n=W2) for _ in range(2)]
        v_buf = [carve(4 * W2).rearrange("p (g n) -> p g n", n=W2) for _ in range(2)]
        probs = [carve(512) for _ in range(2)]
        probs_n = carve(P)
        pT = [carve(512) for _ in range(2)]
        pT_n = carve(P)
        qbd = carve(NSEQ * P)
        q_now = carve(P)
        acc = carve(P)
        pick_now = carve(P // 2)
        w_f = carve(KC * P).rearrange("p (c n) -> p c n", c=KC)
        w_t = carve(KC * P).rearrange("p (c n) -> p c n", c=KC)
        nmx, sums, cexp = small[:, 0:5], small[:, 8:13], small[:, 16:21]
        nmax, total, rtotal = small[:, 24:25], small[:, 25:26], small[:, 26:27]
        pick_now = pick_now[0:NS].bitcast(BF16)
        qbd_v = qbd.rearrange("p (s j n) -> p s j n", s=NSEQ, j=4)
        kg = [wbuf[:, b].rearrange("p c n -> p (c n)")[:, 0:4 * 512].rearrange("p (j n) -> p j n", j=4)
              for b in range(2)]

        k_in, v_in = sems("k_in", 2), sems("v_in", 2)
        v_free = sem("v_free")
        wf_in, wt_in = sem("wf_in"), sem("wt_in")
        wf_used, wt_used = sem("wf_used"), sem("wt_used")
        kg_tr, kg_dve, kg_act = sem("kg_tr"), sem("kg_dve"), sem("kg_act")
        qk, mx, ex = sem("qk"), sem("mx"), sem("ex")
        p_tr, p_ev, pv = sem("p_tr"), sem("p_ev"), sem("pv")
        fill, fill_ev = sem("fill"), sem("fill_ev")
        nm_ok, c_ok, o_ok = sem("nm_ok"), sem("c_ok"), sem("o_ok")
        now_ok, qbd_ok, banks_ok = sem("now_ok"), sem("qbd_ok"), sem("banks_ok")
        FB, KB0, SB0, PTB, OB, MB = 0, 1, 3, 5, 6, 7
        M_S, M_O, M_P = slice(64, 128), slice(128, 256), slice(256, 384)
        NPAGES = cache_k.shape[0]

        with nc.Block() as block:
            def page_loads(e, cache, buf, arrived, s, g):
                for n in range(4):
                    pg = e.value_load(pages[0:1, bass.ds(s * NPG + 4 * g + n, 1)], min_val=0, max_val=NPAGES - 1)
                    e.dma_start(buf[g % 2][:, n, :],
                                cache[bass.ds(pg, 1), 0].rearrange("a p h d -> p (a h d)")).then_inc(arrived[g % 2], 16)

            @block.sync
            def _(sp):
                def load_wf(s):
                    sp.dma_start(w_f, w_rows[:, :, bass.ds(s * P, P)]).then_inc(wf_in, 16)

                def load_wt(s):
                    sp.dma_start(w_t, w_rows[:, :, bass.ds(s * P + G_IA, P)]).then_inc(wt_in, 16)

                def keys(s, g, after=None):
                    if after is not None:
                        sp.wait_ge(kg_tr, after)
                    page_loads(sp, cache_k, k_buf, k_in, s, g)

                load_wf(0)
                keys(0, 0)
                keys(0, 1)
                load_wt(0)

                def sequence(s, last):
                    keys(s, 2, s * 16 + 4)
                    keys(s, 3, s * 16 + 8)
                    if not last:
                        keys(s + 1, 0, s * 16 + 12)
                        sp.wait_ge(wf_used, s * 2 + 2)
                        load_wf(s + 1)
                        keys(s + 1, 1, s * 16 + 16)
                        sp.wait_ge(wt_used, s * 2 + 2)
                        load_wt(s + 1)

                with sp.Fori(0, NSEQ - 1) as s:
                    sequence(s, False)
                sequence(NSEQ - 1, True)

            @block.gpsimd
            def _(pool):
                def now(s):
                    nc.gpsimd.tensor_copy(q_now.unsqueeze(1), qbd.rearrange("p (s n) -> p s n", s=NSEQ)[:, bass.ds(s, 1), :]
                                          ).then_inc(now_ok, 1)
                    nc.gpsimd.tensor_copy(pick_now, pick[:, bass.ds(s * P, P)]).then_inc(now_ok, 1)

                me = Tally(pool, pool_own, pool_count[0])
                me.link(nc.gpsimd.memset(qbd, 0.0))
                for h in range(2):
                    nc.gpsimd.tensor_copy(
                        qbd_v[DH * h:DH * h + DH, :, :, NNEW * h:NNEW * h + NNEW],
                        qT[DH * h:DH * h + DH, :, SEQ:TOK].rearrange("p j (s q) -> p s j q", s=NSEQ)).then_inc(qbd_ok, 1)
                pool.wait_ge(qbd_ok, 2)
                with pool.Fori(0, NSEQ) as s:
                    after(pool, qk, s * 5)
                    now(s)
                    for g in range(4):
                        pool.wait_ge(v_free, s * 4 + g + 1)
                        page_loads(pool, cache_v, v_buf, v_in, s, g)
                pool_count[0] = me.n

            @block.tensor
            def _(pe):
                pe.sem_inc(v_free, 2)
                begin(pe, qk, p_tr, pv)
                pe.wait_ge(banks_ok, 4)

                def turn_keys(s, g):
                    pe.wait_ge(k_in[g % 2], s * 128 + 64 * (g // 2) + 64)
                    for j in range(4):
                        if j % 2 == 0:
                            after(pe, kg_dve, s * 8 + 2 * g + j // 2)
                        else:
                            after(pe, kg_act, s * 8 + 2 * g + j // 2)
                        for n in range(4):
                            mm = pe.transpose(psum[:, KB0 + j % 2, n * P:(n + 1) * P],
                                              k_buf[g % 2][:, n, j * P:(j + 1) * P], ident[:])
                        mm.then_inc(kg_tr, 1)

                def logits(s, g):
                    pe.wait_ge(now_ok, s * 2 + 2)
                    after(pe, kg_dve, s * 8 + 2 * g + 2)
                    after(pe, kg_act, s * 8 + 2 * g + 2)
                    after(pe, ex, s * 5 + g - 1 if g >= 2 else s * 5)
                    bank = psum[:, SB0 + g % 2, :]
                    pe.matmul(bank, pick_now, bias_s[:, g * 512:(g + 1) * 512], start=True, stop=False,
                              skip_group_check=True)
                    for j in range(4):
                        mm = pe.matmul(bank[32 * j:32 * j + 32, :], q_now[:, 32 * j:32 * j + 32], kg[g % 2][:, j, :],
                                       start=False, stop=(j == 3), skip_group_check=True)
                    mm.then_inc(qk, 1)

                def logits_new(s):
                    bank = psum[:, MB, M_S]
                    pe.matmul(bank, pick_now, bias_s[:, PAST:LS], start=True, stop=False, skip_group_check=True)
                    for j in range(4):
                        mm = pe.matmul(bank[32 * j:32 * j + 32, :], q_now[:, 32 * j:32 * j + 32], kT[:, j, SEQ:TOK],
                                       start=False, stop=(j == 3), skip_group_check=True)
                    mm.then_inc(qk, 1)

                def turn_probs(s, g):
                    after(pe, ex, s * 5 + g + 1)
                    after(pe, p_ev, s * 5 + g)
                    for n in range(4):
                        mm = pe.transpose(psum[:, PTB, n * P:(n + 1) * P], probs[g % 2][:, n * P:(n + 1) * P], ident[:])
                    mm.then_inc(p_tr, 1)

                def values(s, g):
                    after(pe, p_ev, s * 5 + g + 1)
                    pe.wait_ge(v_in[g % 2], s * 128 + 64 * (g // 2) + 64)
                    if g == 0:
                        after(pe, o_ok, s)
                    for j in range(4):
                        for n in range(4):
                            mm = pe.matmul(psum[32 * j:32 * j + 16, OB, g * P:(g + 1) * P],
                                           pT[g % 2][:, n * P + 32 * j:n * P + 32 * j + 16],
                                           v_buf[g % 2][:, n, j * P:(j + 1) * P], start=(n == 0), stop=(n == 3),
                                           skip_group_check=True)
                    mm.then_inc(v_free, 1)

                def feature_tile(s, half):
                    if half == 0:
                        pe.wait_ge(wf_in, s * 16 + 16)
                        after(pe, fill_ev, s * 4)
                    for c in range(4 * half, 4 * half + 4):
                        mm = pe.matmul(psum[:, FB, :], w_f[:, c, :], xT[:, c, 0:SEQ], start=(c == 0), stop=(c == KC - 1),
                                       skip_group_check=True)
                    if half:
                        mm.then_inc(wf_used, 1)

                def feature_new(s):
                    after(pe, fill_ev, s * 4 + 1)
                    for c in range(KC):
                        mm = pe.matmul(psum[:, FB, 0:NS], w_f[:, c, :], xT[:, c, SEQ:TOK], start=(c == 0),
                                       stop=(c == KC - 1), skip_group_check=True)
                    mm.then_inc(wf_used, 1)

                def token_tile(s, t):
                    if t == 0:
                        pe.wait_ge(wt_in, s * 16 + 16)
                        after(pe, fill_ev, s * 4 + 2)
                    if t == NT:
                        after(pe, fill_ev, s * 4 + 3)
                    r = ROWS[t]
                    out = psum[0:r, FB, (t % NT) * P:(t % NT + 1) * P]
                    for c in range(KC):
                        mm = pe.matmul(out, xT[:, c, t * P:t * P + r], w_t[:, c, :], start=(c == 0),
                                       stop=(c == KC - 1), skip_group_check=True)
                    if t >= NT - 1:
                        mm.then_inc(wt_used, 1)

                with pe.Fori(0, NSEQ) as s:
                    turn_keys(s, 0)
                    feature_tile(s, 0)
                    turn_keys(s, 1)
                    logits(s, 0)
                    feature_tile(s, 1)
                    turn_keys(s, 2)
                    logits(s, 1)
                    turn_probs(s, 0)
                    feature_new(s)
                    values(s, 0)
                    turn_keys(s, 3)
                    logits(s, 2)
                    turn_probs(s, 1)
                    token_tile(s, 0)
                    values(s, 1)
                    logits(s, 3)
                    turn_probs(s, 2)
                    logits_new(s)
                    token_tile(s, 1)
                    values(s, 2)
                    token_tile(s, 2)
                    turn_probs(s, 3)
                    token_tile(s, 3)
                    after(pe, ex, s * 5 + 5)
                    pe.transpose(psum[:, MB, M_P], probs_n, ident[:]).then_inc(p_tr, 1)
                    values(s, 3)
                    token_tile(s, 4)
                    after(pe, p_ev, s * 5 + 5)
                    for j in range(4):
                        mm = pe.matmul(psum[32 * j:32 * j + 16, MB, M_O], pT_n[:, 32 * j:32 * j + 16],
                                       v_tok[:, NT, j * P:(j + 1) * P], start=True, stop=True, skip_group_check=True)
                    mm.then_inc(pv, 1)

            @block.scalar
            def _(act):
                def keys_out(s, g):
                    for j in (1, 3):
                        act.wait_ge(kg_tr, s * 16 + 4 * g + j + 1)
                        if j == 1:
                            after(act, qk, s * 5 + g - 1 if g >= 2 else s * 5)
                        nc.scalar.copy(kg[g % 2][:, j, :], psum[:, KB0 + 1, :]).then_inc(kg_act, 1)

                def exponential(s, g):
                    act.wait_ge(mx, s * 5 + g + 1)
                    after(act, p_tr, s * 5 + g - 1 if g >= 2 else s * 5)
                    nc.scalar.activation(probs[g % 2], psum[:, SB0 + g % 2, :], ACT.Exp, bias=nmx[:, g:g + 1],
                                         accum_out=sums[:, g:g + 1]).then_inc(ex, 1)

                act.wait_ge(banks_ok, 4)
                begin(act, kg_act, ex, fill_ev)
                with act.Fori(0, NSEQ) as s:
                    keys_out(s, 0)
                    keys_out(s, 1)
                    exponential(s, 0)
                    act.wait_ge(wf_used, s * 2 + 1)
                    nc.scalar.copy(aF[:, bass.ds(s, 1), 0:SEQ], psum[:, FB:FB + 1, :]).then_inc(fill_ev, 1)
                    keys_out(s, 2)
                    exponential(s, 1)
                    act.wait_ge(wf_used, s * 2 + 2)
                    nc.scalar.copy(aF[:, bass.ds(s, 1), SEQ:TOK], psum[:, FB:FB + 1, 0:NS]).then_inc(fill_ev, 1)
                    keys_out(s, 3)
                    exponential(s, 2)
                    exponential(s, 3)
                    act.wait_ge(mx, s * 5 + 5)
                    nc.scalar.activation(probs_n[:, 0:NS], psum[:, MB, M_S], ACT.Exp, bias=nmx[:, 4:5],
                                         accum_out=sums[:, 4:5]).then_inc(ex, 1)
                    act.wait_ge(wt_used, s * 2 + 1)
                    nc.scalar.copy(aT[:, 0:NT, bass.ds(s * P, P)],
                                   psum[:, FB, :].rearrange("p (t n) -> p t n", t=NT)).then_inc(fill_ev, 1)
                    act.wait_ge(wt_used, s * 2 + 2)
                    nc.scalar.copy(aT[0:NS, NT, bass.ds(s * P, P)], psum[0:NS, FB, 0:P]).then_inc(fill_ev, 1)
                    act.wait_ge(nm_ok, s + 1)
                    nc.scalar.activation(cexp, nmx, ACT.Exp, bias=nmax, scale=-1.0).then_inc(c_ok, 1)

            @block.vector
            def _(dve):
                me = Tally(dve, dve_own, dve_count[0])
                nc.vector.memset(psum[:, OB, :], 0.0).then_inc(banks_ok, 1)
                nc.vector.memset(psum[:, MB, :], 0.0).then_inc(banks_ok, 1)
                nc.vector.memset(probs_n, 0.0).then_inc(banks_ok, 1)
                nc.vector.memset(v_tok[NS:P, NT, :], 0.0).then_inc(banks_ok, 1)

                begin(dve, kg_dve, p_ev, o_ok)

                def keys_out(s, g):
                    for j in (0, 2):
                        dve.wait_ge(kg_tr, s * 16 + 4 * g + j + 1)
                        if j == 0:
                            after(dve, qk, s * 5 + g - 1 if g >= 2 else s * 5)
                        nc.vector.tensor_copy(kg[g % 2][:, j, :], psum[:, KB0, :]).then_inc(kg_dve, 1)

                def negmax(s, g):
                    after(dve, qk, s * 5 + g + 1)
                    src = psum[:, SB0 + g % 2, :] if g < 4 else psum[:, MB, M_S]
                    nc.vector.tensor_reduce(nmx[:, g:g + 1], src, AX.X, ALU.max, negate=True).then_inc(mx, 1)

                def probs_out(s, g):
                    after(dve, p_tr, s * 5 + g + 1)
                    dve.wait_ge(v_free, s * 4 + g + 1)
                    nc.vector.tensor_copy(pT[g % 2], psum[:, PTB, :]).then_inc(p_ev, 1)

                with dve.Fori(0, NSEQ) as s:
                    me.n = s * 7 + dve_count[0]
                    keys_out(s, 0)
                    keys_out(s, 1)
                    negmax(s, 0)
                    keys_out(s, 2)
                    negmax(s, 1)
                    probs_out(s, 0)
                    keys_out(s, 3)
                    negmax(s, 2)
                    probs_out(s, 1)
                    negmax(s, 3)
                    probs_out(s, 2)
                    negmax(s, 4)
                    probs_out(s, 3)
                    after(dve, p_tr, s * 5 + 5)
                    after(dve, pv, s)
                    nc.vector.tensor_copy(pT_n, psum[:, MB, M_P]).then_inc(p_ev, 1)
                    dve.wait_ge(mx, s * 5 + 5)
                    nc.vector.tensor_reduce(nmax, nmx, AX.X, ALU.min).then_inc(nm_ok, 1)
                    dve.wait_ge(c_ok, s + 1)
                    me.link(nc.vector.tensor_tensor_reduce(small[:, 32:37], cexp, sums, 1.0, 0.0, ALU.mult, ALU.add,
                                                           total))
                    me.link(nc.vector.reciprocal(rtotal, total))
                    me.link(nc.vector.tensor_scalar(cexp, cexp, rtotal, None, ALU.mult))
                    after(dve, pv, s + 1)
                    dve.wait_ge(v_free, s * 4 + 6)
                    me.link(nc.vector.tensor_scalar(acc, psum[:, OB, 0:P], cexp[:, 0:1], None, ALU.mult))
                    for g in (1, 2, 3):
                        me.link(nc.vector.scalar_tensor_tensor(acc, psum[:, OB, g * P:(g + 1) * P], cexp[:, g:g + 1],
                                                               acc, ALU.mult, ALU.add))
                    nc.vector.scalar_tensor_tensor(osb[:, bass.ds(s, 1), :], psum[:, MB:MB + 1, M_O], cexp[:, 4:5],
                                                   acc.unsqueeze(1), ALU.mult, ALU.add).then_inc(o_ok, 1)
                me.n = dve_count[0] + 7 * NSEQ
                dve_count[0] = me.n
        at[0] = KEEP2
        cum, dec, qE, kE = (carve(4 * TOK).rearrange("p (h n) -> p h n", h=HA) for _ in range(4))
        sc = carve(NT * 512).rearrange("p (c n) -> p c n", c=NT)
        sc_n = carve(HA * NS)[0:NS]
        levels = carve(len(LEVELS) * HA * P // 4).bitcast(U8).rearrange("p (l n) -> p l n", l=len(LEVELS))
        levels_f = qE.rearrange("p h n -> p (h n)")[:, 0:len(LEVELS) * P].rearrange("p (l n) -> p l n", l=len(LEVELS))
        state = carve(HA * P)
        seqcols = carve(NSEQ * NS)
        el_p, el_n = carve(HA * NT), carve(HA * NSEQ)
        lbl = carve(2 * HA).rearrange("p (a h) -> p a h", a=2)
        lb, lbc, lbt = carve(HA), carve(HA), carve(2 * HA).rearrange("p (a h) -> p a h", a=2)
        gn = carve(P)
        qa, ky = aF[:, 0:HA], aF[:, HA:2 * HA]
        ia, ga = aT[:, :, 0:W2], aT[:, :, W2:D]
        xflat = xT[:].rearrange("p c n -> p (c n)")
        lgt = [xflat[:, 512 * a:512 * a + 512] for a in range(2)]
        prb = [xflat[:, 1024 + 512 * a:1536 + 512 * a] for a in range(2)]
        prT = [xflat[:, 2048 + 512 * a:2560 + 512 * a] for a in range(2)]
        wo = wbuf[:].rearrange("p b c n -> p (b c n)").rearrange("p (c n) -> p c n", c=KC)
        nm4, rs4, ri4 = small[:, 40:44], small[:, 44:48], small[:, 48:52]

        par_in, wo_in, lev_in = sem("par_in"), sem("wo_in"), sem("lev_in")
        gate_ok, lb_ok, sig_ok, f_ok, ln_ok = sem("gate_ok"), sem("lb_ok"), sem("sig_ok"), sem("f_ok"), sem("ln_ok")
        ke_z = sem("ke_z")
        key_ok, q_ok, diff_ok, dec_ok, qe_ok, ke_ok = (sem("key_ok"), sem("q_ok"), sem("diff_ok"), sem("dec_ok"),
                                                       sem("qe_ok"), sem("ke_ok"))
        lv, lv_ev = sem("lv"), sem("lv_ev")
        lg, lmax, lex, ltr, ltr_ev, lpv, lout = (sem("lg"), sem("lmax"), sem("lex"), sem("ltr"), sem("ltr_ev"),
                                                 sem("lpv"), sem("lout"))
        NLEV = len(LEVELS)
        JOBS = [(l, c) for l in range(NLEV) for c in range(NT + (LEVELS[l] < NNEW))]
        FIRST = [min(n for n, j in enumerate(JOBS) if j[0] == l) for l in range(NLEV)] + [len(JOBS)]
        NA = HB * NT

        def jobs_of(a):
            l, c = a // 4, a % 4
            n0, n1 = FIRST[l], FIRST[l + 1]
            return range(n0, n0 + 3) if c == 0 else range(n0 + 3, n1) if c == 1 else range(0)

        def span(l):
            return TOK if LEVELS[l] < NNEW else SEQ

        def halves(x, l):
            b = LEVELS[l]
            v = x[:, :, 0:span(l)].rearrange("p h (n r) -> p h n r", r=2 * b)
            return v[:, :, :, 0:b], v[:, :, :, b:2 * b], v[:, :, :, b - 1:b]

        with nc.Block() as block:
            @block.sync
            def _(sp):
                sp.dma_start(levels_f, c_levels.rearrange("p (l n) -> p l n", l=NLEV)).then_inc(lev_in, 16)
                sp.dma_start(gn, hgrn_norm_g.partition_broadcast(P)).then_inc(par_in, 16)
                sp.dma_start(seqcols, c_seqcols).then_inc(par_in, 16)
                for a in range(2):
                    for h in range(HA):
                        sp.dma_start(lbl[:, a, h:h + 1], hgrn_lb_logits[a, h * P:(h + 1) * P].unsqueeze(1)).then_inc(par_in, 16)
                for c in range(2):
                    sp.dma_start(wo[:, 4 * c:4 * c + 4], wo_rows[:, 4 * c:4 * c + 4]).then_inc(wo_in, 16)
                sp.wait_ge(par_in, 160)
                sp.wait_ge(lev_in, 16)
                sp.wait_ge(wo_in, 32)

            @block.tensor
            def _(pe):
                def level_job(n):
                    l, c = JOBS[n]
                    if n >= 3:
                        pe.wait_ge(lv_ev, n - 2)
                    if l == 0:
                        pe.wait_ge(q_ok, 1)
                        pe.wait_ge(key_ok, 1)
                    else:
                        pe.wait_ge(qe_ok, l)
                        pe.wait_ge(ke_ok, l)
                    kk, qq = (ky, qa) if l == 0 else (kE, qE)
                    w, c0 = (P, c * P) if c < NT else (NS, SEQ)
                    for h in range(HA):
                        mm = pe.matmul(psum[0:w, n % 3, h * w:(h + 1) * w], kk[:, h, c0:c0 + w], qq[:, h, c0:c0 + w],
                                       start=True, stop=True, skip_group_check=True)
                    mm.then_inc(lv, 1)

                def prompt_logits(a):
                    h, b = a // NT, a % NT
                    if a >= 2:
                        pe.wait_ge(lmax, a - 1)
                    r = DH * (h % 2)
                    pe.matmul(psum[:, 3 + a % 2, 0:(b + 1) * P], qT[r:r + DH, h // 2, b * P:(b + 1) * P],
                              kT[r:r + DH, h // 2, 0:(b + 1) * P], start=True, stop=True).then_inc(lg, 1)

                def turn(a):
                    b = a % NT
                    pe.wait_ge(lex, a + 1)
                    if a >= 2:
                        pe.wait_ge(ltr_ev, a - 1)
                    for k in range(b + 1):
                        mm = pe.transpose(psum[:, 5 + a % 2, k * P:(k + 1) * P], prb[a % 2][:, k * P:(k + 1) * P], ident[:])
                    mm.then_inc(ltr, 1)

                def prompt_values(a):
                    h, b = a // NT, a % NT
                    pe.wait_ge(ltr_ev, a + 1)
                    if a >= 1:
                        pe.wait_ge(lout, a)
                    for k in range(b + 1):
                        mm = pe.matmul(psum[:, 7, 0:P], prT[a % 2][:, k * P:(k + 1) * P],
                                       v_tok[:, k, (h // 2) * P:(h // 2 + 1) * P], start=(k == 0), stop=(k == b))
                    mm.then_inc(lpv, 1)

                for a in range(NA + 2):
                    if a < NA:
                        prompt_logits(a)
                        for n in jobs_of(a):
                            level_job(n)
                    if 1 <= a <= NA:
                        turn(a - 1)
                    if a >= 2:
                        prompt_values(a - 2)

            @block.scalar
            def _(act):
                act.wait_ge(par_in, 160)
                act.wait_ge(lb_ok, 1)
                nc.scalar.activation(lbt, lbt, ACT.Exp).then_inc(lb_ok, 1)
                nc.scalar.activation(dec, ky, ACT.Sigmoid).then_inc(sig_ok, 1)
                act.wait_ge(sig_ok, 1)
                nc.scalar.activation(ky, ky, ACT.Sigmoid, scale=-1.0).then_inc(sig_ok, 1)
                nc.scalar.activation(qa, qa, ACT.Silu).then_inc(q_ok, 1)
                nc.scalar.activation(ga[:, 0:NT], ga[:, 0:NT], ACT.Silu).then_inc(gate_ok, 1)
                nc.scalar.activation(ga[0:NS, NT], ga[0:NS, NT], ACT.Silu).then_inc(gate_ok, 1)
                act.wait_ge(f_ok, HA)
                nc.scalar.activation(dec, dec, ACT.Ln).then_inc(ln_ok, 1)

                def exponential(a):
                    b = a % NT
                    act.wait_ge(lmax, a + 1)
                    if a >= 2:
                        act.wait_ge(ltr, a - 1)
                        act.wait_ge(lout, a - 3) if a >= 4 else None
                    w = (b + 1) * P
                    nc.scalar.activation(prb[a % 2][:, 0:w], lgt[a % 2][:, 0:w], ACT.Exp, bias=nm4[:, a % 4:a % 4 + 1],
                                         scale=-1.0, accum_out=rs4[:, a % 4:a % 4 + 1]).then_inc(lex, 1)

                def probs_out(a):
                    act.wait_ge(ltr, a + 1)
                    if a >= 2:
                        act.wait_ge(lpv, a - 1)
                    w = (a % NT + 1) * P
                    nc.scalar.copy(prT[a % 2][:, 0:w], psum[:, 5 + a % 2, 0:w]).then_inc(ltr_ev, 1)

                for a in range(NA + 1):
                    if a < NA:
                        l = a // 4 + 1
                        if a % 4 == 1 and l < NLEV:
                            act.wait_ge(diff_ok, 2 * l)
                            nc.scalar.activation(dec[:, :, 0:span(l)], dec[:, :, 0:span(l)], ACT.Exp).then_inc(dec_ok, 1)
                        exponential(a)
                    if a >= 1:
                        probs_out(a - 1)

            @block.gpsimd
            def _(pool):
                pool.wait_ge(par_in, 160)
                pool.wait_ge(gate_ok, 2)
                for t in range(NT + 1):
                    r = ROWS[t]
                    v = ga[0:r, t].rearrange("p (h n) -> p h n", h=HA)
                    nc.gpsimd.tensor_tensor(v, v, gn[0:r].unsqueeze(1).to_broadcast([r, HA, P]), ALU.mult).then_inc(gate_ok, 1)
                nc.gpsimd.memset(kE, 0.0).then_inc(ke_z, 1)
                pool.wait_ge(ke_z, 1)
                for l in range(1, NLEV):
                    pool.wait_ge(dec_ok, l)
                    pool.wait_ge(key_ok, 1)
                    if l > 1:
                        pool.wait_ge(lv, FIRST[l])
                    nc.gpsimd.tensor_tensor(halves(kE, l)[0], halves(ky, l)[0], halves(dec, l)[0], ALU.mult).then_inc(ke_ok, 1)

            @block.vector
            def _(dve):
                me = Tally(dve, dve_own, dve_count[0])
                dve.wait_ge(par_in, 160)
                me.link(nc.vector.tensor_tensor(lb, lbl[:, 0], lbl[:, 1], ALU.max))
                nc.vector.tensor_tensor(lbt, lbl, lb.unsqueeze(1).to_broadcast([P, 2, HA]), ALU.subtract).then_inc(lb_ok, 1)
                me.link(nc.vector.memset(sc, 0.0))
                me.link(nc.vector.memset(sc_n, 0.0))
                dve.wait_ge(lev_in, 16)
                for h in range(HA):
                    me.add(nc.vector.tensor_copy(levels[:, :, h * P:(h + 1) * P], levels_f))
                me.wait()
                me.link(nc.vector.memset(qE, 0.0))
                dve.wait_ge(lb_ok, 2)
                me.link(nc.vector.tensor_tensor(lbc, lbt[:, 0], lbt[:, 1], ALU.add))
                me.link(nc.vector.reciprocal(lbc, lbc))
                me.link(nc.vector.tensor_tensor(lb, lbt[:, 0], lbc, ALU.mult))
                me.link(nc.vector.tensor_scalar(lbc, lb, -1.0, 1.0, ALU.mult, ALU.add))
                dve.wait_ge(sig_ok, 1)
                for h in range(HA):
                    nc.vector.tensor_scalar(dec[:, h], dec[:, h], lbc[:, h:h + 1], lb[:, h:h + 1], ALU.mult, ALU.add).then_inc(f_ok, 1)
                dve.wait_ge(sig_ok, 2)
                for h in range(HA):
                    ins = nc.vector.tensor_scalar(ky[:, h], ky[:, h], lbc[:, h:h + 1], None, ALU.mult)
                ins.then_inc(key_ok, 1)
                dve.wait_ge(ln_ok, 1)
                for h in range(HA):
                    me.add(nc.vector.tensor_tensor_scan(cum[:, h], keep[:], dec[:, h], 0.0, ALU.mult, ALU.add))
                me.wait()

                def differences(l):
                    left, right, edge = halves(cum, l)
                    dl, dr, _ = halves(dec, l)
                    shape = list(left.shape)
                    if l > 1:
                        dve.wait_ge(ke_ok, l - 1)
                        dve.wait_ge(qe_ok, l - 1)
                    nc.vector.tensor_tensor(dl, edge.to_broadcast(shape), left, ALU.subtract).then_inc(diff_ok, 1)
                    nc.vector.tensor_tensor(dr, right, edge.to_broadcast(shape), ALU.subtract).then_inc(diff_ok, 1)

                def scores_out(n):
                    l, c = JOBS[n]
                    dve.wait_ge(lv, n + 1)
                    if c < NT:
                        out, mask, src = sc[:, c], levels[:, l], psum[:, n % 3, :]
                    else:
                        out = sc_n.rearrange("p (h n) -> p h n", h=HA)
                        mask = levels[0:NS, l].rearrange("p (h n) -> p h n", h=HA)[:, :, 0:NS]
                        src = psum[0:NS, n % 3, 0:HA * NS].rearrange("p (h n) -> p h n", h=HA)
                    nc.vector.copy_predicated(out, mask, src).then_inc(lv_ev, 1)

                def mask_and_max(a):
                    b = a % NT
                    w = (b + 1) * P
                    dve.wait_ge(lg, a + 1)
                    if a >= 2:
                        dve.wait_ge(lex, a - 1)
                    nc.vector.tensor_tensor_reduce(lgt[a % 2][:, 0:w], psum[:, 3 + a % 2, 0:w],
                                                   bias_p[:, POFF[b]:POFF[b] + w], -1.0, 3.0e38, ALU.add, ALU.min,
                                                   nm4[:, a % 4:a % 4 + 1]).then_inc(lmax, 1)

                def attended(a):
                    h, b = a // NT, a % NT
                    dve.wait_ge(lex, a + 1)
                    me.link(nc.vector.reciprocal(ri4[:, a % 4:a % 4 + 1], rs4[:, a % 4:a % 4 + 1]))
                    dve.wait_ge(lpv, a + 1)
                    g = gB[:, b, h * DH:(h + 1) * DH]
                    nc.vector.scalar_tensor_tensor(g, psum[:, 7, DH * (h % 2):DH * (h % 2) + DH], ri4[:, a % 4:a % 4 + 1],
                                                   g, ALU.mult, ALU.mult).then_inc(lout, 1)

                for a in range(NA + 2):
                    if a < NA:
                        l = a // 4 + 1
                        if a % 4 == 0 and l < NLEV:
                            differences(l)
                        mask_and_max(a)
                        for n in jobs_of(a):
                            scores_out(n)
                        if a % 4 == 2 and l < NLEV:
                            dve.wait_ge(dec_ok, l)
                            dve.wait_ge(lv, FIRST[l])
                            dve.wait_ge(q_ok, 1)
                            nc.vector.tensor_tensor(halves(qE, l)[1], halves(qa, l)[1], halves(dec, l)[1],
                                                    ALU.mult).then_inc(qe_ok, 1)
                    if a >= 2:
                        attended(a - 2)
                dve_count[0] = me.n

        kdT = arena[:, KEEP2:KEEP2 + (NT + 1) * W2].rearrange("p (t n) -> p t n", n=W2)
        oa = aF.rearrange("p c n -> p (c n)")[:, 0:(NT + 1) * W2].rearrange("p (t n) -> p t n", n=W2)
        s0 = xflat[:, 0:NSEQ * HA * P].rearrange("p (s h n) -> p s h n", s=NSEQ, h=HA)
        vflat = v_tok[:].rearrange("p t n -> p (t n)")
        vx = [vflat[0:NS, a * 1024:(a + 1) * 1024].rearrange("p (s n) -> p s n", s=NSEQ) for a in range(2)]
        qx = [bias_p[:, a * 512:(a + 1) * 512].rearrange("p (s n) -> p s n", s=NSEQ) for a in range(2)]
        sq = vflat[:, 2048:2048 + P]
        ss = small[:, 56:56 + 4 * (NT + 1)]
        state_st = sem("state_st")
        s0_in, e_ok, qc_ok, el_ok, dl_ok, dl_ex, kd_ok = (sem("s0_in"), sem("e_ok"), sem("qc_ok"), sem("el_ok"),
                                                          sem("dl_ok"), sem("dl_ex"), sem("kd_ok"))
        kt, kt_ev, kv, st_ok, oc, oc_ev = sem("kt"), sem("kt_ev"), sem("kv"), sem("st_ok"), sem("oc"), sem("oc_ev")
        qx_ok, vx_ok, dec_o, skv, skv_ev, sdec = (sem("qx_ok"), sem("vx_ok"), sem("dec_o"), sem("skv"), sem("skv_ev"),
                                                  sem("sdec"))
        ss_ok, ss_v, ss_r, mixed = sem("ss_ok"), sem("ss_v"), sem("ss_r"), sem("mixed")
        with nc.Block() as block:
            @block.sync
            def _(sp):
                sp.dma_start(s0, state_hgrn[0].rearrange("s h k v -> k s h v")).then_inc(s0_in, 16)
                sp.wait_ge(st_ok, HA * NT)
                sp.dma_start(st_prompt[0, 0].rearrange("h k v -> k h v"),
                             state.rearrange("p (h n) -> p h n", h=HA)).then_inc(state_st, 16)
                sp.wait_ge(skv_ev, HA)
                sp.dma_start(st_sample[0].rearrange("s h k v -> k s h v"), s0).then_inc(state_st, 16)
                sp.wait_ge(state_st, 32)

            @block.tensor
            def _(pe):
                pe.wait_ge(kd_ok, 1)
                for t in range(NT + 1):
                    r = ROWS[t]
                    if t >= 2:
                        pe.wait_ge(kt_ev, t - 1)
                    for h in range(HA):
                        mm = pe.transpose(psum[0:r, t % 2, h * P:(h + 1) * P], kE[:, h, t * P:t * P + r], ident[:])
                    mm.then_inc(kt, 1)
                pe.wait_ge(qc_ok, 1)
                for c in range(NT):
                    pe.wait_ge(kt_ev, c + 1)
                    if c >= 2:
                        pe.wait_ge(st_ok, HA * (c - 1))
                    for h in range(HA):
                        mm = pe.matmul(psum[:, 4 + c % 2, h * P:(h + 1) * P], kdT[:, c, h * P:(h + 1) * P],
                                       ia[:, c, h * P:(h + 1) * P], start=True, stop=True, skip_group_check=True)
                    mm.then_inc(kv, 1)
                    if c >= 2:
                        pe.wait_ge(oc_ev, c - 1)
                    for h in range(HA):
                        out = psum[:, 2 + c % 2, h * P:(h + 1) * P]
                        mm = pe.matmul(out, sc[:, c, h * P:(h + 1) * P], ia[:, c, h * P:(h + 1) * P],
                                       start=True, stop=(c == 0), skip_group_check=True)
                        if c:
                            pe.wait_ge(st_ok, HA * c)
                            mm = pe.matmul(out, qE[:, h, c * P:(c + 1) * P], state[:, h * P:(h + 1) * P],
                                           start=False, stop=True, skip_group_check=True)
                    mm.then_inc(oc, 1)
                pe.wait_ge(s0_in, 16)
                for h in range(HA):
                    out = psum[0:NS, 6, h * P:(h + 1) * P]
                    pe.matmul(out, sc_n[:, h * NS:(h + 1) * NS], ia[0:NS, NT, h * P:(h + 1) * P],
                              start=True, stop=False, skip_group_check=True)
                    pe.wait_ge(qx_ok, h + 1)
                    for s in range(NSEQ):
                        mm = pe.matmul(out, qx[h % 2][:, s, :], s0[:, s, h, :], start=False, stop=(s == NSEQ - 1),
                                       skip_group_check=True)
                    mm.then_inc(dec_o, 1)
                pe.wait_ge(kt_ev, NT + 1)
                for h in range(HA):
                    pe.wait_ge(vx_ok, h + 1)
                    if h:
                        pe.wait_ge(skv_ev, h)
                    for a in range(2):
                        mm = pe.matmul(psum[:, a, :], kdT[0:NS, NT, h * P:(h + 1) * P],
                                       vx[h % 2][:, 4 * a:4 * a + 4, :], start=True, stop=True)
                    mm.then_inc(skv, 1)

            @block.scalar
            def _(act):
                nc.scalar.activation(dec, cum, ACT.Exp).then_inc(e_ok, 1)
                act.wait_ge(dl_ok, 2)
                nc.scalar.activation(dec, dec, ACT.Exp).then_inc(dl_ex, 1)
                for t in range(NT + 1):
                    r = ROWS[t]
                    act.wait_ge(kt, t + 1)
                    nc.scalar.copy(kdT[0:r, t, :], psum[0:r, t % 2, :]).then_inc(kt_ev, 1)
                for t in range(NT + 1):
                    r = ROWS[t]
                    act.wait_ge(oc_ev, t + 1)
                    for h in range(HA):
                        n = t * HA + h
                        if n:
                            act.wait_ge(ss_ok, n)
                        nc.scalar.activation(sq[0:r], oa[0:r, t, h * P:(h + 1) * P], ACT.Square,
                                             accum_out=ss[0:r, n:n + 1]).then_inc(ss_ok, 1)
                act.wait_ge(ss_v, 1)
                nc.scalar.activation(ss, ss, ACT.Sqrt).then_inc(ss_v, 1)

            @block.gpsimd
            def _(pool):
                for h in range(HA):
                    pool.wait_ge(qc_ok, 1)
                    if h >= 2:
                        pool.wait_ge(dec_o, h - 1)
                    nc.gpsimd.tensor_tensor(qx[h % 2], seqcols.rearrange("p (s n) -> p s n", s=NSEQ),
                                            qE[:, h, SEQ:TOK].unsqueeze(1).to_broadcast([P, NSEQ, NS]),
                                            ALU.mult).then_inc(qx_ok, 1)
                for h in range(HA):
                    if h >= 2:
                        pool.wait_ge(skv, h - 1)
                    nc.gpsimd.tensor_tensor(vx[h % 2], ia[0:NS, NT, h * P:(h + 1) * P].unsqueeze(1).to_broadcast([NS, NSEQ, P]),
                                            ofseq[:].unsqueeze(2).to_broadcast([NS, NSEQ, P]), ALU.mult).then_inc(vx_ok, 1)
                    pool.wait_ge(dec_o, h + 1)
                    pool.wait_ge(el_ok, 2)
                    nc.gpsimd.tensor_tensor(s0[:, :, h, :], s0[:, :, h, :],
                                            el_n[:, h * NSEQ:(h + 1) * NSEQ].unsqueeze(2).to_broadcast([P, NSEQ, P]),
                                            ALU.mult).then_inc(sdec, 1)

            @block.vector
            def _(dve):
                me = Tally(dve, dve_own, dve_count[0])
                nc.vector.memset(ss, 1.0)
                dve.wait_ge(e_ok, 1)
                nc.vector.tensor_tensor(qE, qa, dec, ALU.mult).then_inc(qc_ok, 1)
                nc.vector.tensor_copy(el_p.rearrange("p (h n) -> p h n", h=HA), dec[:, :, P - 1:SEQ:P]).then_inc(el_ok, 1)
                nc.vector.tensor_copy(el_n.rearrange("p (h n) -> p h n", h=HA), dec[:, :, SEQ + NNEW - 1:TOK:NNEW]).then_inc(el_ok, 1)
                dve.wait_ge(el_ok, 2)
                dve.wait_ge(qc_ok, 1)
                for (a, b, w) in ((0, SEQ, P), (SEQ, TOK, NNEW)):
                    v = cum[:, :, a:b].rearrange("p h (n r) -> p h n r", r=w)
                    last = v[:, :, :, w - 1:w].to_broadcast(list(v.shape))
                    nc.vector.tensor_tensor(dec[:, :, a:b].rearrange("p h (n r) -> p h n r", r=w), last, v,
                                            ALU.subtract).then_inc(dl_ok, 1)
                dve.wait_ge(dl_ex, 1)
                nc.vector.tensor_tensor(kE, ky, dec, ALU.mult).then_inc(kd_ok, 1)
                for c in range(NT):
                    dve.wait_ge(kv, c + 1)
                    if c:
                        dve.wait_ge(oc, c + 1)
                    for h in range(HA):
                        st = state[:, h * P:(h + 1) * P]
                        src = psum[:, 4 + c % 2, h * P:(h + 1) * P]
                        if c == 0:
                            nc.vector.tensor_copy(st, src).then_inc(st_ok, 1)
                        else:
                            if h == 0:
                                dve.wait_ge(st_ok, HA * c)
                            nc.vector.scalar_tensor_tensor(st, st, el_p[:, h * NT + c:h * NT + c + 1], src,
                                                           ALU.mult, ALU.add).then_inc(st_ok, 1)
                    if c:
                        nc.vector.tensor_copy(oa[:, c - 1, :], psum[:, 2 + (c - 1) % 2, :]).then_inc(oc_ev, 1)
                dve.wait_ge(oc, NT)
                nc.vector.tensor_copy(oa[:, NT - 1, :], psum[:, 2 + (NT - 1) % 2, :]).then_inc(oc_ev, 1)
                dve.wait_ge(dec_o, HA)
                nc.vector.tensor_copy(oa[0:NS, NT, :], psum[0:NS, 6, :]).then_inc(oc_ev, 1)
                for h in range(HA):
                    dve.wait_ge(skv, h + 1)
                    dve.wait_ge(sdec, h + 1)
                    for a in range(2):
                        v = s0[:, 4 * a:4 * a + 4, h, :]
                        ins = nc.vector.tensor_tensor(v, v, psum[:, a, :].rearrange("p (s n) -> p s n", s=4), ALU.add)
                    ins.then_inc(skv_ev, 1)
                dve.wait_ge(ss_ok, HA * (NT + 1))
                nc.vector.tensor_scalar(ss[:], ss[:], 1.0 / P, EPS, ALU.mult, ALU.add).then_inc(ss_v, 1)
                dve.wait_ge(ss_v, 2)
                me.link(nc.vector.reciprocal(ss, ss))
                dve.wait_ge(gate_ok, NT + 3)
                for t in range(NT + 1):
                    r = ROWS[t]
                    for h in range(HA):
                        o = oa[0:r, t, h * P:(h + 1) * P]
                        ins = nc.vector.scalar_tensor_tensor(o, o, ss[0:r, t * HA + h:t * HA + h + 1],
                                                             ga[0:r, t, h * P:(h + 1) * P], ALU.mult, ALU.mult)
                    ins.then_inc(mixed, 1)
                dve_count[0] = me.n

        mixA, mixB = qT, kT
        at[0] = KEEP2 + 2 * 4 * TOK
        xr = [carve(D) for _ in range(2)]
        z = [carve(D) for _ in range(2)]
        lng, lnb = carve(D), carve(D)
        st2 = small[:, 80:92].rearrange("p (a n) -> p a n", a=2)
        mv2 = small[:, 92:94]
        sd = small[:, 94:95]
        ln_in, xr_in = sem("ln_in"), sems("xr_in", 2)
        mt, mt_ev, yb, zr, zv, zs, zn, zf = (sem("mt"), sem("mt_ev"), sem("yb"), sem("zr"), sem("zv"), sem("zs"),
                                             sem("zn"), sem("zf"))
        zg, y_st = sem("zg"), sems("y_st", 2)
        with nc.Block() as block:
            @block.sync
            def _(sp):
                sp.dma_start(lng, ln_g.partition_broadcast(P)).then_inc(ln_in, 16)
                sp.dma_start(lnb, ln_b.partition_broadcast(P)).then_inc(ln_in, 16)
                def store(t):
                    sp.wait_ge(zf, t + 1)
                    sp.dma_start(y_prompt[0].rearrange("(t p) d -> t p d", p=P)[t] if t < NT
                                 else y_sample.rearrange("s t d -> (s t) d"), z[t % 2][0:ROWS[t]]).then_inc(y_st[t % 2], 16)

                for t in range(NT + 1):
                    if t >= 2:
                        sp.wait_ge(zr, 2 * (t - 1))
                    sp.dma_start(xr[t % 2][0:ROWS[t]], xp_rows[t] if t < NT else xs_rows).then_inc(xr_in[t % 2], 16)
                    if t >= 2:
                        store(t - 2)
                store(NT - 1)
                store(NT)
                sp.wait_ge(y_st[0], 48)
                sp.wait_ge(y_st[1], 32)
                sp.wait_ge(stored, NSTORE[0])

            @block.tensor
            def _(pe):
                n = 0
                for t in range(NT + 1):
                    r = ROWS[t]
                    for src in (oa, gB):
                        if n >= 2:
                            pe.wait_ge(mt_ev, n - 1)
                        for c in range(4):
                            mm = pe.transpose(psum[:, n % 2, c * P:c * P + r], src[0:r, t, c * P:(c + 1) * P],
                                              ident[0:r, 0:r])
                        mm.then_inc(mt, 1)
                        n += 1
                for a in range(2):
                    pe.wait_ge(mt_ev, n - 1)
                    for s in range(4):
                        mm = pe.transpose(psum[:, n % 2, s * P:(s + 1) * P], osb[:, 4 * a + s, :], ident[:])
                    mm.then_inc(mt, 1)
                    n += 1
                pe.wait_ge(mt_ev, n)
                for t in range(NT + 1):
                    r = ROWS[t]
                    for a in range(2):
                        m = 2 * t + a
                        if m >= 4:
                            pe.wait_ge(zr, m - 3)
                        for c in range(KC):
                            src = (mixA, mixB)[c // 4][:, c % 4, t * P:t * P + r]
                            mm = pe.matmul(psum[0:r, 2 + m % 4, :], src, wo[:, c, a * 512:(a + 1) * 512],
                                           start=(c == 0), stop=(c == KC - 1))
                        mm.then_inc(yb, 1)

            @block.scalar
            def _(act):
                n = 0
                for t in range(NT + 1):
                    r = ROWS[t]
                    for dst in (mixA, mixB):
                        act.wait_ge(mt, n + 1)
                        nc.scalar.copy(dst[:, :, t * P:t * P + r],
                                       psum[:, n % 2, :].rearrange("p (c n) -> p c n", c=4)[:, :, 0:r]).then_inc(mt_ev, 1)
                        n += 1
                for t in range(NT + 1):
                    r = ROWS[t]
                    act.wait_ge(zv, t + 1)
                    nc.scalar.activation(sd[0:r], sd[0:r], ACT.Sqrt).then_inc(zs, 1)

            @block.gpsimd
            def _(pool):
                pool.wait_ge(ln_in, 32)
                for t in range(NT + 1):
                    r = ROWS[t]
                    zz = z[t % 2][0:r]
                    pool.wait_ge(zn, t + 1)
                    nc.gpsimd.tensor_tensor(zz, zz, lng[0:r], ALU.mult).then_inc(zg, 1)
                    pool.wait_ge(zg, t + 1)
                    nc.gpsimd.tensor_tensor(zz, zz, lnb[0:r], ALU.add).then_inc(zf, 1)

            @block.vector
            def _(dve):
                me = Tally(dve, dve_own, dve_count[0])
                n = 2 * (NT + 1)
                dve.wait_ge(mt_ev, n)
                for a in range(2):
                    dve.wait_ge(mt, n + 1)
                    for h in range(2):
                        g = mixB[DH * h:DH * h + DH, :, SEQ + 32 * a:SEQ + 32 * a + 32].rearrange(
                            "p j (s q) -> p j s q", q=NNEW)
                        src = psum[DH * h:DH * h + DH, n % 2, :].rearrange("p (s j x) -> p j s x", s=4, j=4)[
                            :, :, :, NNEW * h:NNEW * h + NNEW]
                        ins = nc.vector.tensor_tensor(g, src, g, ALU.mult)
                        if h == 0:
                            me.add(ins)
                    ins.then_inc(mt_ev, 1)
                    n += 1
                for t in range(NT + 1):
                    r = ROWS[t]
                    zz = z[t % 2][0:r]
                    dve.wait_ge(xr_in[t % 2], 16 * (t // 2 + 1))
                    if t >= 2:
                        dve.wait_ge(y_st[t % 2], 16 * (t // 2))
                    for a in range(2):
                        m = 2 * t + a
                        dve.wait_ge(yb, m + 1)
                        w = slice(a * 512, a * 512 + 512)
                        nc.vector.scalar_tensor_tensor(zz[:, w], xr[t % 2][0:r, w], ALPHA, psum[0:r, 2 + m % 4, :],
                                                       ALU.mult, ALU.add).then_inc(zr, 1)
                        dve.wait_ge(zr, m + 1)
                        me.add(nc.vector.bn_stats(st2[0:r, a], zz[:, w]))
                    me.wait()
                    me.link(nc.vector.bn_aggr(mv2[0:r], st2[0:r]))
                    nc.vector.tensor_scalar(sd[0:r], mv2[0:r, 1:2], EPS, None, ALU.add).then_inc(zv, 1)
                    dve.wait_ge(zs, t + 1)
                    me.link(nc.vector.reciprocal(sd[0:r], sd[0:r]))
                    nc.vector.tensor_scalar(zz, zz, mv2[0:r, 0:1], sd[0:r], ALU.subtract, ALU.mult).then_inc(zn, 1)
                dve_count[0] = me.n


_INS = ["x_prompt", "x_sample", "cache_k", "cache_v", "cache_kidx", "state_hgrn", "page_table", "w_in",
        "hgrn_lb_logits", "hgrn_norm_g", "idx_norm_g", "idx_norm_b", "w_out", "ln_g", "ln_b"]
_OUTS = [(1, SEQ, D), (NSEQ, NNEW, D), (1, NT, 1, PAGE, HB, DH), (1, NT, 1, PAGE, HB, DH), (1, NT, 1, PAGE, DH),
         (1, 1, HA, P, P), (NSEQ, 1, NNEW, HB, DH), (NSEQ, 1, NNEW, HB, DH), (NSEQ, 1, NNEW, DH),
         (1, NSEQ, HA, P, P)]


def kernel(**inputs):
    import numpy as _np
    import concourse.bacc as _bacc
    from concourse import mybir as _mybir
    from concourse.bass_utils import run_bass_kernel_spmd as _run

    nc = _bacc.Bacc("TRN2", target_bir_lowering=False, num_devices=1)
    arrays, args = {}, []
    given = {name: _np.ascontiguousarray(inputs[name]) for name in _INS}
    given.update({f"c_{name}": a for name, a in shape_constants().items()})
    for name, a in given.items():
        arrays[f"in_{name}"] = a
        args.append(nc.dram_tensor(f"in_{name}", a.shape, _mybir.dt.from_np(a.dtype), kind="ExternalInput").ap())
    for i, shape in enumerate(_OUTS):
        args.append(nc.dram_tensor(f"out_{i}", shape, F32, kind="ExternalOutput").ap())
    hybrid_step(nc, *args)
    r = _run(nc, [arrays], core_ids=[0])
    return tuple(r.results[0][f"out_{i}"] for i in range(len(_OUTS)))
```

```python
from contextlib import ExitStack

import numpy as np
import concourse.bass as bass
from concourse import mybir

ALU = mybir.AluOpType
ACT = mybir.ActivationFunctionType
F32 = mybir.dt.float32
BF16 = mybir.dt.bfloat16
I32 = mybir.dt.int32
U8 = mybir.dt.uint8
AX = mybir.AxisListType

P = 128
D = 1024
SEQ = 512
NSEQ, NNEW = 8, 8
NS = NSEQ * NNEW
TOK = SEQ + NS
NT = SEQ // P
KC = D // P
HA = 4
HB, DH = 8, 64
HI = 16
PAGE, NPG = 128, 16
PAST = PAGE * NPG
W2 = HB * DH
LS = PAST + NS
TOPK_P, TOPK_S = min(256, SEQ // 4), min(256, (PAST + NNEW) // 4)
G_QA, G_FA, G_IA, G_GA = 0, 512, 1024, 1536
G_QB, G_KB, G_VB, G_GB, G_QI, G_KI = 2048, 2560, 3072, 3584, 4096, 5120
EPS = 1e-5
ALPHA = 2.0 ** 0.25
ROT = 8
TAKEN = -3.0e38
MASKED = -1.0e30
LEVELS = [0, 1, 2, 4, 8, 16, 32, 64]
POFF = [0, 128, 384, 768]
PW = 1280


def shape_constants():
    c = {}
    c["ident"] = np.eye(P, dtype=np.float32)
    half = ROT
    inv = np.float32(500000.0) ** (-np.arange(half, dtype=np.float32) / np.float32(half))
    pos = np.concatenate([np.arange(SEQ), np.tile(PAST + np.arange(NNEW), NSEQ)]).astype(np.float32)
    ang = (pos[:, None] * inv[None, :]).astype(np.float32)
    cs = np.concatenate([np.cos(ang), np.sin(ang)], 1).astype(np.float32)
    rope = np.zeros((P, NT + 1, 2 * half), np.float32)
    for t in range(NT):
        rope[:, t] = cs[t * P:(t + 1) * P]
    rope[:NS, NT] = cs[SEQ:]
    c["rope"] = rope
    q, k = np.arange(P)[:, None], np.arange(P)[None, :]
    tri = (k <= q)
    c["tri"] = np.stack([tri.astype(np.float32), np.where(tri, 0, TAKEN).astype(np.float32),
                         np.where(tri, 0, MASKED).astype(np.float32)], 1)
    sq, sk = np.arange(NS)[:, None], np.arange(NS)[None, :]
    own = (sq // NNEW == sk // NNEW) & (sk % NNEW <= sq % NNEW)
    c["own"] = np.stack([own.astype(np.float32), np.where(own, 0, TAKEN).astype(np.float32),
                         np.where(own, 0, MASKED).astype(np.float32)], 1)
    pick = np.zeros((NS, NSEQ, 4, 32), np.float32)
    for s in range(NSEQ):
        for qq in range(NNEW):
            for hh in range(2):
                pick[s * NNEW + qq, s, :, hh * NNEW + qq] = 1
    c["pick"] = pick.reshape(NS, NSEQ * P)
    c["sameq"] = (np.arange(P)[:, None] % NNEW == np.arange(NS)[None, :] % NNEW).astype(np.float32)
    lv = np.zeros((P, len(LEVELS), P), np.float32)
    s, t = np.arange(P)[:, None], np.arange(P)[None, :]
    for i, b in enumerate(LEVELS):
        lv[:, i] = (s == t) if b == 0 else ((s // (2 * b) == t // (2 * b)) & (s % (2 * b) < b) & (t % (2 * b) >= b))
    c["levels"] = lv.reshape(P, len(LEVELS) * P)
    keep = np.ones((P, TOK), np.float32)
    keep[:, 0:SEQ:P] = 0
    keep[:, SEQ::NNEW] = 0
    c["keep"] = keep
    c["seqcols"] = np.broadcast_to(np.repeat(np.eye(NSEQ, dtype=np.float32), NNEW, 1).reshape(1, -1),
                                   (P, NSEQ * NS)).copy()
    c["ofseq"] = (np.arange(NS)[:, None] // NNEW == np.arange(NSEQ)[None, :]).astype(np.float32)
    return c


def begin(e, *given):
    for sem in given:
        e.sem_inc(sem, 1)


def after(e, sem, n):
    e.wait_ge(sem, n + 1)


class Tally:

    def __init__(self, eng, sem, n=0):
        self.eng, self.sem, self.n = eng, sem, n

    def add(self, ins):
        ins.then_inc(self.sem, 1)
        self.n = self.n + 1

    def wait(self):
        self.eng.wait_ge(self.sem, self.n)

    def link(self, ins):
        self.add(ins)
        self.wait()


def hybrid_step(nc, x_prompt, x_sample, cache_k, cache_v, cache_kidx, state_hgrn, page_table,
                w_in, hgrn_lb_logits, hgrn_norm_g, idx_norm_g, idx_norm_b, w_out, ln_g, ln_b,
                c_ident, c_rope, c_tri, c_own, c_pick, c_sameq, c_levels, c_keep, c_seqcols, c_ofseq,
                y_prompt, y_sample, k_prompt, v_prompt, ki_prompt, st_prompt,
                k_sample, v_sample, ki_sample, st_sample):
    w_rows = w_in[0].rearrange("(c p) n -> p c n", p=P)
    wo_rows = w_out[0].rearrange("(c p) n -> p c n", p=P)
    xp_rows = x_prompt[0].rearrange("(t p) d -> t p d", p=P)
    xs_rows = x_sample.rearrange("s t d -> (s t) d")

    with ExitStack() as ctx:
        def sb(name, shape, dt=F32):
            return ctx.enter_context(nc.sbuf_tensor(name, shape, dt))

        def sem(name):
            return ctx.enter_context(nc.semaphore(name))

        def sems(name, n):
            return [sem(f"{name}{i}") for i in range(n)]

        ident = sb("ident", [P, P])
        rope = sb("rope", [P, NT + 1, 2 * ROT])
        tri = sb("tri", [P, 3, P])
        own = sb("own", [NS, 3, NS])
        pick = sb("pick", [NS, NSEQ * P], BF16)
        sameq = sb("sameq", [P, NS])
        keep = sb("keep", [P, TOK])
        ofseq = sb("ofseq", [NS, NSEQ])
        gki = sb("gki", [P, 2, DH])
        pages = sb("pages", [1, NSEQ * NPG], I32)
        xT = sb("xT", [P, KC, TOK])
        late = sb("late", [P, 2 * 4 * TOK + (NT + 1) * W2 + PW])
        kT = late[:, 0:4 * TOK].rearrange("p (c n) -> p c n", c=4)
        qT = late[:, 4 * TOK:8 * TOK].rearrange("p (c n) -> p c n", c=4)
        gB = late[:, 8 * TOK:8 * TOK + (NT + 1) * W2].rearrange("p (t n) -> p t n", n=W2)
        bias_p = late[:, 8 * TOK + (NT + 1) * W2:]
        kidx = late[:, 0:NSEQ * NPG * DH].rearrange("p (s g n) -> p s g n", s=NSEQ, g=NPG)
        v_tok = sb("v_tok", [P, NT + 1, W2])
        bias_s = sb("bias_s", [NS, LS], BF16)
        small = sb("small", [P, 128])
        wbuf = sb("wbuf", [P, 2, KC, 512])
        ARENA = 25600
        arena = sb("arena", [P, ARENA])
        at = [0]

        def carve(n):
            a = at[0]
            at[0] += n
            assert at[0] <= ARENA, at[0]
            return arena[:, a:a + n]

        psum = ctx.enter_context(nc.psum_tensor("banks", [P, 8, 512], F32))

        at[0] = 0
        qi_tok = carve((NT + 1) * D).rearrange("p (t n) -> p t n", n=D)
        k_tok = qi_tok[:, :, 0:W2]
        q_tok = qi_tok[:, :, W2:D]
        qiT = carve(8 * SEQ).rearrange("p (c n) -> p c n", c=8)
        pick_f = qiT[0:NS, 0:2].rearrange("p c n -> p (c n)")
        qis = carve(NSEQ * P).rearrange("p (s h q) -> p s h q", s=NSEQ, h=HI)
        kxT = [carve(PAST // 2) for _ in range(2)]
        kiT = carve(TOK)
        relu_s = [carve(PAST) for _ in range(2)]
        relu_n = carve(NS)
        relu_p = carve(4 * 512).rearrange("p (b n) -> p b n", b=4)
        S = carve(LS)[0:NS]
        SP = {b: bias_p[:, POFF[b]:POFF[b] + (b + 1) * P] for b in (1, 2, 3)}
        kiwi = carve((NT + 1) * 80).rearrange("p (t n) -> p t n", n=80)
        kin = carve((NT + 1) * DH).rearrange("p (t n) -> p t n", n=DH)
        w_all = carve(NS)
        w_rep = carve(P)[0:NS]
        w_seq = carve(NSEQ * NS).rearrange("p (s n) -> p s n", s=NSEQ)
        rtmp = carve(4 * HI * ROT).rearrange("p (a n) -> p a n", a=4)
        stats = carve((NT + 1) * 6).rearrange("p (t n) -> p t n", n=6)
        mv = carve((NT + 1) * 2).rearrange("p (t n) -> p t n", n=2)
        rstd = carve(NT + 1)
        best = small[:, 96:128].rearrange("p (a n) -> p a n", a=4)
        newbias = carve(NS)[0:NS]
        xin = arena[:, ARENA - 5 * D:ARENA].rearrange("p (t n) -> p t n", n=D)
        assert at[0] <= ARENA

        const_in, pages_in, ki_par_in = sem("const_in"), sem("pages_in"), sem("ki_par_in")
        x_in = sems("x_in", NT + 1)
        x_tr, x_ev = sem("x_tr"), sem("x_ev")
        w_got = sems("w_got", 2)
        proj, proj_ev = sem("proj"), sem("proj_ev")
        var_ok, std_ok, kin_ok = sem("var_ok"), sem("std_ok"), sem("kin_ok")
        act_own, dve_own, pool_own = sem("act_own"), sem("dve_own"), sem("pool_own")
        roped = sem("roped")
        wrep_ok = sem("wrep_ok")
        tr, tr_ev = sem("tr"), sem("tr_ev")
        tr2, tr2_ev = sem("tr2"), sem("tr2_ev")
        kidx_in, kidx_tr, kidx_ev = sems("kidx_in", NSEQ), sem("kidx_tr"), sem("kidx_ev")
        wseq_ok, rel, relu_ok, comb, rel_n, relun_ok, comb_n = (sem("wseq_ok"), sem("rel"), sem("relu_ok"), sem("comb"),
                                                                sem("rel_n"), sem("relun_ok"), sem("comb_n"))
        ofseq_in = sem("ofseq_in")
        prel, prelu, pacc, weighed = sem("prel"), sem("prelu"), sem("pacc"), sem("weighed")
        s_ok, topk = sem("s_ok"), sem("topk")
        stored = sem("stored")
        NSTORE = [0]
        halves_out = [0]
        dve_count, pool_count = [0], [0]

        ROWS = [P] * NT + [NS]
        GROUPS = [(G_KI, 80), (G_QI, 512), (G_QI + 512, 512), (G_VB, 512), (G_KB, 512), (G_QB, 512), (G_GB, 512)]
        BEFORE = 3
        PB = 4
        TB = 4
        CB = 6

        NCONST = 7 * 16

        def hold(dve, value):
            dve.wait_ge(topk, value)
            nc.vector.memset(small[:, 95:96], 0.0)

        def kidx_loads(e, sequences):
            e.wait_ge(pages_in, 16)
            with e.Fori(0, NPG // 2) as g:
                for s in sequences:
                    for h in range(2):
                        pg = e.value_load(pages[0:1, bass.ds(g + s * NPG + h * (NPG // 2), 1)], min_val=0,
                                          max_val=cache_kidx.shape[0] - 1)
                        e.dma_start(kidx[:, s, bass.ds(g * 2 + h, 1), :],
                                    cache_kidx[bass.ds(pg, 1), 0].rearrange("a p d -> p a d")
                                    ).then_inc(kidx_in[s], 16)

        with nc.Block() as block:
            @block.sync
            def _(sp):
                sp.dma_start(pages[:], page_table.rearrange("s g -> (s g)").rearrange("(a n) -> a n", a=1)).then_inc(pages_in, 16)
                sp.dma_start(ident[:], c_ident).then_inc(const_in, 16)
                for t in range(NT + 1):
                    src = xp_rows[t] if t < NT else xs_rows
                    sp.dma_start(xin[0:ROWS[t], t, :], src).then_inc(x_in[t], 16)

                for dst, src in ((rope, c_rope), (tri, c_tri), (own, c_own),
                                 (sameq, c_sameq), (keep, c_keep), (pick_f, c_pick)):
                    sp.dma_start(dst[:], src).then_inc(const_in, 16)
                sp.dma_start(gki[:, 0, :], idx_norm_g.partition_broadcast(P)).then_inc(ki_par_in, 16)
                sp.dma_start(gki[:, 1, :], idx_norm_b.partition_broadcast(P)).then_inc(ki_par_in, 16)
                kidx_loads(sp, range(NSEQ // 2))

            def indexer_jobs(g, t):
                n = 4 * ((g - BEFORE) * (NT + 1) + t)
                return range(n, n + 4) if n < 3 * HI else range(0)

            def pe_project(pe, g, then=None):
                pe.wait_ge(w_got[g % 2], 16 * (g // 2 + 1))
                w = GROUPS[g][1]
                for t in range(NT + 1):
                    n = g * (NT + 1) + t
                    if n >= PB:
                        pe.wait_ge(proj_ev, n - PB + 1)
                    split = 2 if t == NT and w == 512 else 1
                    for c in range(KC):
                        for a in range(split):
                            mm = pe.matmul(psum[a * NS:a * NS + ROWS[t], n % PB, 0:w // split],
                                           xT[:, c, t * P:t * P + ROWS[t]],
                                           wbuf[:, g % 2, c, a * w // split:(a + 1) * w // split],
                                           start=(c == 0), stop=(c == KC - 1), skip_group_check=(split == 2))
                    mm.then_inc(proj, 1)
                    if then:
                        then(g, t)

            @block.tensor
            def _(pe):
                pe.wait_ge(const_in, 16)
                for t in range(NT + 1):
                    pe.wait_ge(x_in[t], 16)
                    for h in range(2):
                        n = 2 * t + h
                        if n >= PB:
                            pe.wait_ge(x_ev, n - PB + 1)
                        for c in range(4):
                            mm = pe.transpose(psum[:, n % PB, c * P:c * P + ROWS[t]],
                                              xin[0:ROWS[t], t, (4 * h + c) * P:(4 * h + c + 1) * P],
                                              ident[0:ROWS[t], 0:ROWS[t]])
                        mm.then_inc(x_tr, 1)
                pe.wait_ge(x_ev, 2 * (NT + 1))
                for g in range(BEFORE):
                    pe_project(pe, g)

                job = 0

                def take_bank():
                    if job >= 2:
                        pe.wait_ge(tr_ev, job - 1)
                    return TB + job % 2

                pe.wait_ge(roped, NT + 1)
                b = take_bank()
                for t in range(NT):
                    mm = pe.transpose(psum[0:DH, b, t * P:(t + 1) * P], kin[:, t, :], ident[:])
                mm.then_inc(tr, 1)
                job += 1
                b = take_bank()
                pe.transpose(psum[0:DH, b, 0:NS], kin[0:NS, NT, :], ident[0:NS, 0:NS]).then_inc(tr, 1)
                job += 1
                b = take_bank()
                pe.wait_ge(wrep_ok, 1)
                pe.matmul(psum[:, b, 0:NS], w_rep, ident[0:NS, 0:NS], start=True, stop=True).then_inc(tr, 1)
                job += 1
                for t in range(NT):
                    pe.wait_ge(roped, NT + 1 + t + 1)
                    for h in range(2):
                        b = take_bank()
                        for c in range(4):
                            mm = pe.transpose(psum[:, b, c * P:(c + 1) * P],
                                              qi_tok[:, t, (4 * h + c) * P:(4 * h + c + 1) * P], ident[:])
                        mm.then_inc(tr, 1)
                        job += 1
                pe.wait_ge(roped, 2 * (NT + 1))
                for h in range(2):
                    b = take_bank()
                    for c in range(8):
                        mm = pe.transpose(psum[0:DH, b, c * NS:(c + 1) * NS],
                                          qi_tok[0:NS, NT, (8 * h + c) * DH:(8 * h + c + 1) * DH],
                                          ident[0:NS, 0:NS])
                    mm.then_inc(tr, 1)
                    job += 1
                NJ = job
                pe.wait_ge(tr_ev, NJ)
                pe.wait_ge(proj_ev, BEFORE * (NT + 1))

                def keys(s):
                    pe.wait_ge(kidx_in[s], 16 * NPG)
                    if s:
                        pe.wait_ge(kidx_ev, 2 * s)
                    for b in range(2):
                        for c in range(4):
                            mm = pe.transpose(psum[:, TB + b, c * P:(c + 1) * P],
                                              kidx[:, s, 8 * b + 2 * c:8 * b + 2 * c + 2, :], ident[:])
                        mm.then_inc(kidx_tr, 1)

                def relevance(s):
                    pe.wait_ge(kidx_ev, 2 * s + 2)
                    for k in range(4):
                        h, b = k % 2, k // 2
                        if s:
                            pe.wait_ge(relu_ok, 4 * s - 3 + k)
                        pe.matmul(psum[:, k, :], qis[DH * h:DH * h + DH, s].rearrange("p h q -> p (h q)"),
                                  kxT[s % 2][DH * h:DH * h + DH, b * 512:(b + 1) * 512],
                                  start=True, stop=True).then_inc(rel, 1)

                def combine(s):
                    for k in range(4):
                        h, b = k % 2, k // 2
                        pe.wait_ge(relu_ok, 4 * s + k + 1)
                        mm = pe.matmul(psum[NS * b:NS * b + NS, CB + h, :], w_seq[:, s, :],
                                       relu_s[s % 2][:, k * 512:(k + 1) * 512], start=(s == 0), stop=(s == NSEQ - 1),
                                       skip_group_check=True)
                    mm.then_inc(comb, 1)

                keys(0)
                pe.wait_ge(wseq_ok, NSEQ)
                for s in range(NSEQ):
                    relevance(s)
                    if s + 1 < NSEQ:
                        keys(s + 1)
                    if s:
                        combine(s - 1)
                for s in range(NSEQ):
                    mm = pe.matmul(psum[:, TB, s * NNEW:(s + 1) * NNEW], qis[0:DH, s].rearrange("p h q -> p (h q)"),
                                   kiT[0:DH, SEQ + s * NNEW:SEQ + (s + 1) * NNEW], start=True, stop=True,
                                   skip_group_check=True)
                mm.then_inc(rel_n, 1)
                combine(NSEQ - 1)
                pe.wait_ge(relun_ok, 1)
                for s in range(NSEQ):
                    mm = pe.matmul(psum[0:NS, TB + 1, s * NNEW:(s + 1) * NNEW], w_seq[:, s, :],
                                   relu_n[:, s * NNEW:(s + 1) * NNEW], start=True, stop=True, skip_group_check=True)
                mm.then_inc(comb_n, 1)

                def prompt_relevance(g, t):
                    for n in indexer_jobs(g, t):
                        b, h = n // HI + 1, n % HI
                        if n >= 4:
                            pe.wait_ge(prelu, n - 3)
                        r = DH * (h % 2)
                        pe.matmul(psum[:, TB + n % 4, 0:(b + 1) * P], qiT[r:r + DH, h // 2, b * P:(b + 1) * P],
                                  kiT[r:r + DH, 0:(b + 1) * P], start=True, stop=True).then_inc(prel, 1)

                job = 0

                def turn(src, t):
                    nonlocal job
                    if job >= 2:
                        pe.wait_ge(tr2_ev, job - 1)
                    for c in range(4):
                        mm = pe.transpose(psum[:, TB + job % 2, c * P:c * P + ROWS[t]],
                                          src[0:ROWS[t], t, c * P:(c + 1) * P],
                                          ident[0:ROWS[t], 0:ROWS[t]])
                    mm.then_inc(tr2, 1)
                    job += 1

                pe.wait_ge(relu_ok, 4 * NSEQ)
                pe.wait_ge(s_ok, 5)
                pe_project(pe, 3, prompt_relevance)
                pe_project(pe, 4, prompt_relevance)
                pe_project(pe, 5, prompt_relevance)
                pe.wait_ge(prelu, 3 * HI)
                for t in range(NT + 1):
                    pe.wait_ge(roped, 2 * (NT + 1) + t + 1)
                    turn(k_tok, t)
                pe_project(pe, 6)
                for t in range(NT + 1):
                    pe.wait_ge(roped, 3 * (NT + 1) + t + 1)
                    turn(q_tok, t)


            def load_w(act, g):
                c0, w = GROUPS[g]
                act.dma_start(wbuf[:, g % 2, :, 0:w], w_rows[:, :, c0:c0 + w]).then_inc(w_got[g % 2], 16)

            def act_evac(act, g, then=None):
                dest = (kiwi, qi_tok[:, :, 0:512], qi_tok[:, :, 512:1024], v_tok, k_tok, q_tok, gB)[g]
                w = GROUPS[g][1]
                for t in range(NT + 1):
                    n = g * (NT + 1) + t
                    act.wait_ge(proj, n + 1)
                    if g == 4 and t == 0:
                        act.wait_ge(tr, 13)
                    split = 2 if t == NT and w == 512 else 1
                    for a in range(split):
                        o = dest[0:ROWS[t], t, a * w // split:(a + 1) * w // split]
                        i_ = psum[a * NS:a * NS + ROWS[t], n % PB, 0:w // split]
                        if g == 6:
                            ins = nc.scalar.activation(o, i_, ACT.Silu)
                        elif g == 5:
                            ins = nc.scalar.mul(o, i_, DH ** -0.5)
                        else:
                            ins = nc.scalar.copy(o, i_)
                        if split == 2 and a == 0:
                            ins.then_inc(act_own, 1)
                    if split == 2:
                        halves_out[0] += 1
                        act.wait_ge(act_own, halves_out[0])
                    ins.then_inc(proj_ev, 1)
                    if then:
                        then(g, t)
                if g + 2 < len(GROUPS):
                    load_w(act, g + 2)

            @block.scalar
            def _(act):
                load_w(act, 0)
                load_w(act, 1)
                for n in range(2 * (NT + 1)):
                    t, h = n // 2, n % 2
                    act.wait_ge(x_tr, n + 1)
                    nc.scalar.copy(xT[:, 4 * h:4 * h + 4, t * P:t * P + ROWS[t]],
                                   psum[:, n % PB, :].rearrange("p (c n) -> p c n", c=4)[:, :, 0:ROWS[t]]
                                   ).then_inc(x_ev, 1)
                act_evac(act, 0)
                act_evac(act, 1)
                act.wait_ge(var_ok, 1)
                nc.scalar.activation(rstd[:, :], mv[:, :, 1], ACT.Sqrt).then_inc(std_ok, 1)
                act_evac(act, 2)
                for s in range(NSEQ):
                    if s >= 2:
                        act.wait_ge(comb, s - 1)
                    for k in range(4):
                        act.wait_ge(rel, 4 * s + k + 1)
                        nc.scalar.activation(relu_s[s % 2][:, k * 512:(k + 1) * 512], psum[:, k, :],
                                             ACT.Relu).then_inc(relu_ok, 1)
                act.wait_ge(rel_n, 1)
                nc.scalar.activation(relu_n, psum[:, TB, 0:NS], ACT.Relu).then_inc(relun_ok, 1)
                act.wait_ge(comb, NSEQ)
                for h in range(2):
                    for b in range(2):
                        g = 2 * h + b
                        nc.scalar.copy(S[:, g * 512:(g + 1) * 512], psum[NS * b:NS * b + NS, CB + h, :]).then_inc(s_ok, 1)
                act.wait_ge(comb_n, 1)
                nc.scalar.copy(S[:, PAST:], psum[0:NS, TB + 1, 0:NS]).then_inc(s_ok, 1)

                def prompt_relu(g, t):
                    for n in indexer_jobs(g, t):
                        w = (n // HI + 2) * P
                        act.wait_ge(prel, n + 1)
                        if n >= 4:
                            act.wait_ge(pacc, n - 3)
                        nc.scalar.activation(relu_p[:, n % 4, 0:w], psum[:, TB + n % 4, 0:w], ACT.Relu).then_inc(prelu, 1)
                    for n in indexer_jobs(g, t):
                        b, h = n // HI + 1, n % HI
                        act.wait_ge(prelu, n + 1)
                        nc.scalar.mul(relu_p[:, n % 4, 0:(b + 1) * P], relu_p[:, n % 4, 0:(b + 1) * P],
                                      kiwi[:, b, DH + h:DH + h + 1]).then_inc(weighed, 1)

                act_evac(act, 3, prompt_relu)
                act_evac(act, 4, prompt_relu)
                act_evac(act, 5, prompt_relu)

                def evac(dst, t, job):
                    act.wait_ge(tr2, job + 1)
                    nc.scalar.copy(dst[:, :, t * P:t * P + ROWS[t]],
                                   psum[:, TB + job % 2, :].rearrange("p (c n) -> p c n", c=4)[:, :, 0:ROWS[t]]
                                   ).then_inc(tr2_ev, 1)

                for t in range(NT + 1):
                    evac(kT, t, t)
                act_evac(act, 6)
                for t in range(NT + 1):
                    evac(qT, t, NT + 1 + t)

            @block.vector
            def _(dve):
                me = Tally(dve, dve_own)
                dve.wait_ge(x_ev, 2 * (NT + 1))
                me.link(nc.vector.memset(mv[:], 1.0))
                for t in range(NT + 1):
                    dve.wait_ge(proj_ev, t + 1)
                    me.add(nc.vector.bn_stats(stats[0:ROWS[t], t, :], kiwi[0:ROWS[t], t, 0:DH]))
                me.wait()
                for t in range(NT + 1):
                    me.add(nc.vector.bn_aggr(mv[0:ROWS[t], t, :], stats[0:ROWS[t], t, :]))
                me.wait()
                nc.vector.tensor_scalar(mv[:, :, 1], mv[:, :, 1], EPS, None, ALU.add).then_inc(var_ok, 1)
                nc.vector.tensor_scalar(w_rep.rearrange("p (h q) -> p h q", h=HI),
                                        kiwi[0:NS, NT, DH:DH + HI].unsqueeze(2).to_broadcast([NS, HI, NNEW]),
                                        (HI * DH) ** -0.5, None, ALU.mult).then_inc(wrep_ok, 1)
                me.add(nc.vector.tensor_scalar(kiwi[:, 0:NT, DH:DH + HI], kiwi[:, 0:NT, DH:DH + HI],
                                               (HI * DH) ** -0.5, None, ALU.mult))
                me.add(nc.vector.memset(w_seq, 0.0))
                dve.wait_ge(std_ok, 1)
                me.link(nc.vector.reciprocal(rstd[:, :], rstd[:, :]))
                dve.wait_ge(ki_par_in, 32)
                for t in range(NT + 1):
                    r = ROWS[t]
                    me.link(nc.vector.tensor_scalar(kin[0:r, t, :], kiwi[0:r, t, 0:DH], mv[0:r, t, 0:1],
                                                    rstd[0:r, t:t + 1], ALU.subtract, ALU.mult))
                    me.link(nc.vector.tensor_tensor(kin[0:r, t, :], kin[0:r, t, :], gki[0:r, 0, :], ALU.mult))
                    nc.vector.tensor_tensor(kin[0:r, t, :], kin[0:r, t, :], gki[0:r, 1, :], ALU.add).then_inc(kin_ok, 1)
                dve.wait_ge(const_in, NCONST)
                me.link(nc.vector.tensor_copy(pick[:], pick_f))
                job = 0

                def both(cols, view):
                    for h in range(2):
                        ins = nc.vector.tensor_copy(cols(h), view)
                        if h == 0:
                            me.add(ins)
                    ins.then_inc(tr_ev, 1)

                dve.wait_ge(tr, 1)
                both(lambda h: kiT[DH * h:DH * h + DH, 0:SEQ], psum[0:DH, TB, :])
                dve.wait_ge(tr, 2)
                both(lambda h: kiT[DH * h:DH * h + DH, SEQ:TOK], psum[0:DH, TB + 1, 0:NS])
                dve.wait_ge(tr, 3)
                dve.wait_ge(const_in, NCONST)
                nc.vector.tensor_tensor(w_all, psum[:, TB, 0:NS], sameq[:], ALU.mult).then_inc(tr_ev, 1)
                job = 3
                dve.wait_ge(tr_ev, 3)
                for s in range(NSEQ):
                    nc.vector.tensor_copy(w_seq[:, s, s * NNEW:(s + 1) * NNEW],
                                          w_all[:, s * NNEW:(s + 1) * NNEW]).then_inc(wseq_ok, 1)
                for t in range(NT):
                    for h in range(2):
                        dve.wait_ge(tr, job + 1)
                        nc.vector.tensor_copy(qiT[:, 4 * h:4 * h + 4, t * P:(t + 1) * P],
                                              psum[:, TB + job % 2, :].rearrange("p (c n) -> p c n", c=4)
                                              ).then_inc(tr_ev, 1)
                        job += 1
                for h in range(2):
                    dve.wait_ge(tr, job + 1)
                    both(lambda a: qis[DH * a:DH * a + DH, :, 8 * h:8 * h + 8, :].rearrange("p s h q -> p h s q"),
                         psum[0:DH, TB + job % 2, :].rearrange("p (h s q) -> p h s q", h=8, s=NSEQ))
                    job += 1
                me.wait()
                for s in range(NSEQ):
                    for b in range(2):
                        dve.wait_ge(kidx_tr, 2 * s + b + 1)
                        if s >= 2 and b == 0:
                            dve.wait_ge(rel, 4 * (s - 1))
                        nc.vector.tensor_copy(kxT[s % 2][:, b * 512:(b + 1) * 512],
                                              psum[:, TB + b, :]).then_inc(kidx_ev, 1)
                dve.wait_ge(s_ok, 5)
                me.link(nc.vector.tensor_tensor(S[:, PAST:], S[:, PAST:], own[:, 0, :], ALU.mult))
                nc.vector.tensor_tensor(S[:, PAST:], S[:, PAST:], own[:, 1, :], ALU.add).then_inc(topk, 1)

                with dve.Fori(0, TOPK_S // 8) as r:
                    hold(dve, r * 2 + 1)
                    nc.vector.max(best[0:NS, 0, :], S).then_inc(topk, 1)
                    hold(dve, r * 2 + 2)
                    nc.vector.match_replace(S, best[0:NS, 0, :], S, TAKEN).then_inc(topk, 1)
                dve.wait_ge(topk, 2 * (TOPK_S // 8) + 1)
                me.add(nc.vector.tensor_scalar(bias_s[:, 0:PAST], S[:, 0:PAST], 0.9 * TAKEN, MASKED, ALU.is_gt, ALU.mult))
                me.link(nc.vector.tensor_scalar(newbias, S[:, PAST:], 0.9 * TAKEN, MASKED, ALU.is_gt, ALU.mult))
                me.link(nc.vector.tensor_tensor(bias_s[:, PAST:], newbias, own[:, 2, :], ALU.add))
                dve_count[0] = me.n

            @block.gpsimd
            def _(pool):
                me = Tally(pool, pool_own)
                pool.dma_start(ofseq[:], c_ofseq).then_inc(ofseq_in, 16)
                kidx_loads(pool, range(NSEQ // 2, NSEQ))
                pool.wait_ge(const_in, NCONST)

                def rotate(view, r, t, heads, scaled=False):
                    x1, x2 = view[:, :, 0:ROT], view[:, :, ROT:2 * ROT]
                    shape = [r, heads, ROT]
                    cos = rope[0:r, t, 0:ROT].unsqueeze(1).to_broadcast(shape)
                    sin = rope[0:r, t, ROT:2 * ROT].unsqueeze(1).to_broadcast(shape)
                    tmp = [rtmp[0:r, a, 0:heads * ROT].rearrange("p (h n) -> p h n", h=heads) for a in range(4)]
                    for a, (x, w) in enumerate(((x1, cos), (x2, sin), (x1, sin), (x2, cos))):
                        me.add(nc.gpsimd.tensor_tensor(tmp[a], x, w, ALU.mult))
                    me.wait()
                    me.add(nc.gpsimd.tensor_tensor(x1, tmp[0], tmp[1], ALU.subtract))
                    me.wait()
                    nc.gpsimd.tensor_tensor(x2, tmp[2], tmp[3], ALU.add).then_inc(roped, 1)

                def store(dst, src):
                    pool.dma_start(dst, src).then_inc(stored, 16)
                    NSTORE[0] += 16

                n = 0
                for t in range(NT + 1):
                    r = ROWS[t]
                    pool.wait_ge(kin_ok, t + 1)
                    if n:
                        pool.wait_ge(roped, n)
                    rotate(kin[0:r, t, :].unsqueeze(1), r, t, 1)
                    n += 1
                pool.wait_ge(roped, n)
                for t in range(NT):
                    store(ki_prompt[0, t, 0], kin[:, t, :])
                store(ki_sample[:, 0].rearrange("s t d -> (s t) d"), kin[0:NS, NT, :])
                for t in range(NT + 1):
                    r = ROWS[t]
                    pool.wait_ge(proj_ev, 2 * (NT + 1) + t + 1)
                    pool.wait_ge(roped, n)
                    rotate(qi_tok[0:r, t, :].rearrange("p (h d) -> p h d", h=HI), r, t, HI)
                    n += 1

                def weigh(g, t):
                    for m in indexer_jobs(g, t):
                        b, h = m // HI + 1, m % HI
                        src = relu_p[:, m % 4, 0:(b + 1) * P]
                        pool.wait_ge(weighed, m + 1)
                        if h == 0:
                            nc.gpsimd.tensor_copy(SP[b], src).then_inc(pacc, 1)
                        else:
                            pool.wait_ge(pacc, m)
                            nc.gpsimd.tensor_tensor(SP[b], SP[b], src, ALU.add).then_inc(pacc, 1)
                        if h == HI - 1:
                            d = SP[b][:, b * P:]
                            pool.wait_ge(pacc, m + 1)
                            me.link(nc.gpsimd.tensor_tensor(d, d, tri[:, 0, :], ALU.mult))
                            me.link(nc.gpsimd.tensor_tensor(d, d, tri[:, 1, :], ALU.add))

                for g, view in ((3, v_tok), (4, k_tok), (5, q_tok)):
                    for t in range(NT + 1):
                        r = ROWS[t]
                        pool.wait_ge(proj_ev, g * (NT + 1) + t + 1)
                        if g > 3:
                            pool.wait_ge(roped, n)
                            rotate(view[0:r, t, :].rearrange("p (h d) -> p h d", h=HB), r, t, HB)
                            n += 1
                        weigh(g, t)
                    out_p, out_s = {3: (v_prompt, v_sample), 4: (k_prompt, k_sample), 5: (None, None)}[g]
                    if out_p is not None:
                        pool.wait_ge(roped, n)
                        for t in range(NT):
                            store(out_p[0, t, 0].rearrange("p h d -> p (h d)"), view[:, t, :])
                        store(out_s[:, 0].rearrange("s t h d -> (s t) (h d)"), view[0:NS, NT, :])
                pool.wait_ge(ofseq_in, 16)
                pool_count[0] = me.n
        at[0] = 0
        aF = carve(8 * TOK).rearrange("p (c n) -> p c n", c=8)
        aT = carve((NT + 1) * D).rearrange("p (t n) -> p t n", n=D)
        osb = carve(NSEQ * P).rearrange("p (s n) -> p s n", n=P)
        KEEP2 = at[0]
        k_buf = [carve(4 * W2).rearrange("p (g n) -> p g n", n=W2) for _ in range(2)]
        v_buf = [carve(4 * W2).rearrange("p (g n) -> p g n", n=W2) for _ in range(2)]
        probs = [carve(512) for _ in range(2)]
        probs_n = carve(P)
        pT = [carve(512) for _ in range(2)]
        pT_n = carve(P)
        qbd = carve(NSEQ * P)
        q_now = carve(P)
        acc = carve(P)
        pick_now = carve(P // 2)
        w_f = carve(KC * P).rearrange("p (c n) -> p c n", c=KC)
        w_t = carve(KC * P).rearrange("p (c n) -> p c n", c=KC)
        nmx, sums, cexp = small[:, 0:5], small[:, 8:13], small[:, 16:21]
        nmax, total, rtotal = small[:, 24:25], small[:, 25:26], small[:, 26:27]
        pick_now = pick_now[0:NS].bitcast(BF16)
        qbd_v = qbd.rearrange("p (s j n) -> p s j n", s=NSEQ, j=4)
        kg = [wbuf[:, b].rearrange("p c n -> p (c n)")[:, 0:4 * 512].rearrange("p (j n) -> p j n", j=4)
              for b in range(2)]

        k_in, v_in = sems("k_in", 2), sems("v_in", 2)
        v_free = sem("v_free")
        wf_in, wt_in = sem("wf_in"), sem("wt_in")
        wf_used, wt_used = sem("wf_used"), sem("wt_used")
        kg_tr, kg_dve, kg_act = sem("kg_tr"), sem("kg_dve"), sem("kg_act")
        qk, mx, ex = sem("qk"), sem("mx"), sem("ex")
        p_tr, p_ev, pv = sem("p_tr"), sem("p_ev"), sem("pv")
        fill, fill_ev = sem("fill"), sem("fill_ev")
        nm_ok, c_ok, o_ok = sem("nm_ok"), sem("c_ok"), sem("o_ok")
        now_ok, qbd_ok, banks_ok = sem("now_ok"), sem("qbd_ok"), sem("banks_ok")
        FB, KB0, SB0, PTB, OB, MB = 0, 1, 3, 5, 6, 7
        M_S, M_O, M_P = slice(64, 128), slice(128, 256), slice(256, 384)
        NPAGES = cache_k.shape[0]

        with nc.Block() as block:
            def page_loads(e, cache, buf, arrived, s, g):
                for n in range(4):
                    pg = e.value_load(pages[0:1, bass.ds(s * NPG + 4 * g + n, 1)], min_val=0, max_val=NPAGES - 1)
                    e.dma_start(buf[g % 2][:, n, :],
                                cache[bass.ds(pg, 1), 0].rearrange("a p h d -> p (a h d)")).then_inc(arrived[g % 2], 16)

            @block.sync
            def _(sp):
                def load_wf(s):
                    sp.dma_start(w_f, w_rows[:, :, bass.ds(s * P, P)]).then_inc(wf_in, 16)

                def load_wt(s):
                    sp.dma_start(w_t, w_rows[:, :, bass.ds(s * P + G_IA, P)]).then_inc(wt_in, 16)

                def keys(s, g, after=None):
                    if after is not None:
                        sp.wait_ge(kg_tr, after)
                    page_loads(sp, cache_k, k_buf, k_in, s, g)

                load_wf(0)
                keys(0, 0)
                keys(0, 1)
                load_wt(0)

                def sequence(s, last):
                    keys(s, 2, s * 16 + 4)
                    keys(s, 3, s * 16 + 8)
                    if not last:
                        keys(s + 1, 0, s * 16 + 12)
                        sp.wait_ge(wf_used, s * 2 + 2)
                        load_wf(s + 1)
                        keys(s + 1, 1, s * 16 + 16)
                        sp.wait_ge(wt_used, s * 2 + 2)
                        load_wt(s + 1)

                with sp.Fori(0, NSEQ - 1) as s:
                    sequence(s, False)
                sequence(NSEQ - 1, True)

            @block.gpsimd
            def _(pool):
                def now(s):
                    nc.gpsimd.tensor_copy(q_now.unsqueeze(1), qbd.rearrange("p (s n) -> p s n", s=NSEQ)[:, bass.ds(s, 1), :]
                                          ).then_inc(now_ok, 1)
                    nc.gpsimd.tensor_copy(pick_now, pick[:, bass.ds(s * P, P)]).then_inc(now_ok, 1)

                me = Tally(pool, pool_own, pool_count[0])
                me.link(nc.gpsimd.memset(qbd, 0.0))
                for h in range(2):
                    nc.gpsimd.tensor_copy(
                        qbd_v[DH * h:DH * h + DH, :, :, NNEW * h:NNEW * h + NNEW],
                        qT[DH * h:DH * h + DH, :, SEQ:TOK].rearrange("p j (s q) -> p s j q", s=NSEQ)).then_inc(qbd_ok, 1)
                pool.wait_ge(qbd_ok, 2)
                with pool.Fori(0, NSEQ) as s:
                    after(pool, qk, s * 5)
                    now(s)
                    for g in range(4):
                        pool.wait_ge(v_free, s * 4 + g + 1)
                        page_loads(pool, cache_v, v_buf, v_in, s, g)
                pool_count[0] = me.n

            @block.tensor
            def _(pe):
                pe.sem_inc(v_free, 2)
                begin(pe, qk, p_tr, pv)
                pe.wait_ge(banks_ok, 4)

                def turn_keys(s, g):
                    pe.wait_ge(k_in[g % 2], s * 128 + 64 * (g // 2) + 64)
                    for j in range(4):
                        if j % 2 == 0:
                            after(pe, kg_dve, s * 8 + 2 * g + j // 2)
                        else:
                            after(pe, kg_act, s * 8 + 2 * g + j // 2)
                        for n in range(4):
                            mm = pe.transpose(psum[:, KB0 + j % 2, n * P:(n + 1) * P],
                                              k_buf[g % 2][:, n, j * P:(j + 1) * P], ident[:])
                        mm.then_inc(kg_tr, 1)

                def logits(s, g):
                    pe.wait_ge(now_ok, s * 2 + 2)
                    after(pe, kg_dve, s * 8 + 2 * g + 2)
                    after(pe, kg_act, s * 8 + 2 * g + 2)
                    after(pe, ex, s * 5 + g - 1 if g >= 2 else s * 5)
                    bank = psum[:, SB0 + g % 2, :]
                    pe.matmul(bank, pick_now, bias_s[:, g * 512:(g + 1) * 512], start=True, stop=False,
                              skip_group_check=True)
                    for j in range(4):
                        mm = pe.matmul(bank[32 * j:32 * j + 32, :], q_now[:, 32 * j:32 * j + 32], kg[g % 2][:, j, :],
                                       start=False, stop=(j == 3), skip_group_check=True)
                    mm.then_inc(qk, 1)

                def logits_new(s):
                    bank = psum[:, MB, M_S]
                    pe.matmul(bank, pick_now, bias_s[:, PAST:LS], start=True, stop=False, skip_group_check=True)
                    for j in range(4):
                        mm = pe.matmul(bank[32 * j:32 * j + 32, :], q_now[:, 32 * j:32 * j + 32], kT[:, j, SEQ:TOK],
                                       start=False, stop=(j == 3), skip_group_check=True)
                    mm.then_inc(qk, 1)

                def turn_probs(s, g):
                    after(pe, ex, s * 5 + g + 1)
                    after(pe, p_ev, s * 5 + g)
                    for n in range(4):
                        mm = pe.transpose(psum[:, PTB, n * P:(n + 1) * P], probs[g % 2][:, n * P:(n + 1) * P], ident[:])
                    mm.then_inc(p_tr, 1)

                def values(s, g):
                    after(pe, p_ev, s * 5 + g + 1)
                    pe.wait_ge(v_in[g % 2], s * 128 + 64 * (g // 2) + 64)
                    if g == 0:
                        after(pe, o_ok, s)
                    for j in range(4):
                        for n in range(4):
                            mm = pe.matmul(psum[32 * j:32 * j + 16, OB, g * P:(g + 1) * P],
                                           pT[g % 2][:, n * P + 32 * j:n * P + 32 * j + 16],
                                           v_buf[g % 2][:, n, j * P:(j + 1) * P], start=(n == 0), stop=(n == 3),
                                           skip_group_check=True)
                    mm.then_inc(v_free, 1)

                def feature_tile(s, half):
                    if half == 0:
                        pe.wait_ge(wf_in, s * 16 + 16)
                        after(pe, fill_ev, s * 4)
                    for c in range(4 * half, 4 * half + 4):
                        mm = pe.matmul(psum[:, FB, :], w_f[:, c, :], xT[:, c, 0:SEQ], start=(c == 0), stop=(c == KC - 1),
                                       skip_group_check=True)
                    if half:
                        mm.then_inc(wf_used, 1)

                def feature_new(s):
                    after(pe, fill_ev, s * 4 + 1)
                    for c in range(KC):
                        mm = pe.matmul(psum[:, FB, 0:P], w_f[:, c, :], xT[:, c, TOK - P:TOK], start=(c == 0),
                                       stop=(c == KC - 1), skip_group_check=True)
                    mm.then_inc(wf_used, 1)

                def token_tile(s, t):
                    if t == 0:
                        pe.wait_ge(wt_in, s * 16 + 16)
                        after(pe, fill_ev, s * 4 + 2)
                    if t == NT:
                        after(pe, fill_ev, s * 4 + 3)
                    r = ROWS[t]
                    out = psum[0:r, FB, (t % NT) * P:(t % NT + 1) * P]
                    for c in range(KC):
                        mm = pe.matmul(out, xT[:, c, t * P:t * P + r], w_t[:, c, :], start=(c == 0),
                                       stop=(c == KC - 1), skip_group_check=True)
                    if t >= NT - 1:
                        mm.then_inc(wt_used, 1)

                with pe.Fori(0, NSEQ) as s:
                    turn_keys(s, 0)
                    feature_tile(s, 0)
                    turn_keys(s, 1)
                    logits(s, 0)
                    feature_tile(s, 1)
                    turn_keys(s, 2)
                    logits(s, 1)
                    turn_probs(s, 0)
                    feature_new(s)
                    values(s, 0)
                    turn_keys(s, 3)
                    logits(s, 2)
                    turn_probs(s, 1)
                    token_tile(s, 0)
                    values(s, 1)
                    logits(s, 3)
                    turn_probs(s, 2)
                    logits_new(s)
                    token_tile(s, 1)
                    values(s, 2)
                    token_tile(s, 2)
                    turn_probs(s, 3)
                    token_tile(s, 3)
                    after(pe, ex, s * 5 + 5)
                    pe.transpose(psum[:, MB, M_P], probs_n, ident[:]).then_inc(p_tr, 1)
                    values(s, 3)
                    token_tile(s, 4)
                    after(pe, p_ev, s * 5 + 5)
                    for j in range(4):
                        mm = pe.matmul(psum[32 * j:32 * j + 16, MB, M_O], pT_n[:, 32 * j:32 * j + 16],
                                       v_tok[:, NT, j * P:(j + 1) * P], start=True, stop=True, skip_group_check=True)
                    mm.then_inc(pv, 1)

            @block.scalar
            def _(act):
                def keys_out(s, g):
                    for j in (1, 3):
                        act.wait_ge(kg_tr, s * 16 + 4 * g + j + 1)
                        if j == 1:
                            after(act, qk, s * 5 + g - 1 if g >= 2 else s * 5)
                        nc.scalar.copy(kg[g % 2][:, j, :], psum[:, KB0 + 1, :]).then_inc(kg_act, 1)

                def exponential(s, g):
                    act.wait_ge(mx, s * 5 + g + 1)
                    after(act, p_tr, s * 5 + g - 1 if g >= 2 else s * 5)
                    nc.scalar.activation(probs[g % 2], psum[:, SB0 + g % 2, :], ACT.Exp, bias=nmx[:, g:g + 1],
                                         accum_out=sums[:, g:g + 1]).then_inc(ex, 1)

                act.wait_ge(banks_ok, 4)
                begin(act, kg_act, ex, fill_ev)
                with act.Fori(0, NSEQ) as s:
                    keys_out(s, 0)
                    keys_out(s, 1)
                    exponential(s, 0)
                    act.wait_ge(wf_used, s * 2 + 1)
                    nc.scalar.copy(aF[:, bass.ds(s, 1), 0:SEQ], psum[:, FB:FB + 1, :]).then_inc(fill_ev, 1)
                    keys_out(s, 2)
                    exponential(s, 1)
                    act.wait_ge(wf_used, s * 2 + 2)
                    nc.scalar.copy(aF[:, bass.ds(s, 1), SEQ:TOK], psum[:, FB:FB + 1, P - NS:P]).then_inc(fill_ev, 1)
                    keys_out(s, 3)
                    exponential(s, 2)
                    exponential(s, 3)
                    act.wait_ge(mx, s * 5 + 5)
                    nc.scalar.activation(probs_n[:, 0:NS], psum[:, MB, M_S], ACT.Exp, bias=nmx[:, 4:5],
                                         accum_out=sums[:, 4:5]).then_inc(ex, 1)
                    act.wait_ge(wt_used, s * 2 + 1)
                    nc.scalar.copy(aT[:, 0:NT, bass.ds(s * P, P)],
                                   psum[:, FB, :].rearrange("p (t n) -> p t n", t=NT)).then_inc(fill_ev, 1)
                    act.wait_ge(wt_used, s * 2 + 2)
                    nc.scalar.copy(aT[0:NS, NT, bass.ds(s * P, P)], psum[0:NS, FB, 0:P]).then_inc(fill_ev, 1)
                    act.wait_ge(nm_ok, s + 1)
                    nc.scalar.activation(cexp, nmx, ACT.Exp, bias=nmax, scale=-1.0).then_inc(c_ok, 1)

            @block.vector
            def _(dve):
                me = Tally(dve, dve_own, dve_count[0])
                nc.vector.memset(psum[:, OB, :], 0.0).then_inc(banks_ok, 1)
                nc.vector.memset(psum[:, MB, :], 0.0).then_inc(banks_ok, 1)
                nc.vector.memset(probs_n, 0.0).then_inc(banks_ok, 1)
                nc.vector.memset(v_tok[NS:P, NT, :], 0.0).then_inc(banks_ok, 1)

                begin(dve, kg_dve, p_ev, o_ok)

                def keys_out(s, g):
                    for j in (0, 2):
                        dve.wait_ge(kg_tr, s * 16 + 4 * g + j + 1)
                        if j == 0:
                            after(dve, qk, s * 5 + g - 1 if g >= 2 else s * 5)
                        nc.vector.tensor_copy(kg[g % 2][:, j, :], psum[:, KB0, :]).then_inc(kg_dve, 1)

                def negmax(s, g):
                    after(dve, qk, s * 5 + g + 1)
                    src = psum[:, SB0 + g % 2, :] if g < 4 else psum[:, MB, M_S]
                    nc.vector.tensor_reduce(nmx[:, g:g + 1], src, AX.X, ALU.max, negate=True).then_inc(mx, 1)

                def probs_out(s, g):
                    after(dve, p_tr, s * 5 + g + 1)
                    dve.wait_ge(v_free, s * 4 + g + 1)
                    nc.vector.tensor_copy(pT[g % 2], psum[:, PTB, :]).then_inc(p_ev, 1)

                base = 2 * (TOPK_S // 8) + 1
                ROUNDS = TOPK_P // 8 // NSEQ

                def strike(s, step):
                    hold(dve, s * (6 * ROUNDS) + (base + 3 * step))
                    for b in (1, 2, 3):
                        if step % 2 == 0:
                            nc.vector.max(best[:, b, :], SP[b]).then_inc(topk, 1)
                        else:
                            nc.vector.match_replace(SP[b], best[:, b, :], SP[b], TAKEN).then_inc(topk, 1)

                with dve.Fori(0, NSEQ) as s:
                    me.n = s * 7 + dve_count[0]
                    keys_out(s, 0)
                    strike(s, 0)
                    keys_out(s, 1)
                    negmax(s, 0)
                    keys_out(s, 2)
                    negmax(s, 1)
                    probs_out(s, 0)
                    strike(s, 1)
                    keys_out(s, 3)
                    negmax(s, 2)
                    probs_out(s, 1)
                    strike(s, 2)
                    negmax(s, 3)
                    probs_out(s, 2)
                    negmax(s, 4)
                    strike(s, 3)
                    probs_out(s, 3)
                    after(dve, p_tr, s * 5 + 5)
                    after(dve, pv, s)
                    nc.vector.tensor_copy(pT_n, psum[:, MB, M_P]).then_inc(p_ev, 1)
                    dve.wait_ge(mx, s * 5 + 5)
                    nc.vector.tensor_reduce(nmax, nmx, AX.X, ALU.min).then_inc(nm_ok, 1)
                    dve.wait_ge(c_ok, s + 1)
                    me.link(nc.vector.tensor_tensor_reduce(small[:, 32:37], cexp, sums, 1.0, 0.0, ALU.mult, ALU.add,
                                                           total))
                    me.link(nc.vector.reciprocal(rtotal, total))
                    me.link(nc.vector.tensor_scalar(cexp, cexp, rtotal, None, ALU.mult))
                    after(dve, pv, s + 1)
                    dve.wait_ge(v_free, s * 4 + 6)
                    me.link(nc.vector.tensor_scalar(acc, psum[:, OB, 0:P], cexp[:, 0:1], None, ALU.mult))
                    for g in (1, 2, 3):
                        me.link(nc.vector.scalar_tensor_tensor(acc, psum[:, OB, g * P:(g + 1) * P], cexp[:, g:g + 1],
                                                               acc, ALU.mult, ALU.add))
                    nc.vector.scalar_tensor_tensor(osb[:, bass.ds(s, 1), :], psum[:, MB:MB + 1, M_O], cexp[:, 4:5],
                                                   acc.unsqueeze(1), ALU.mult, ALU.add).then_inc(o_ok, 1)
                me.n = dve_count[0] + 7 * NSEQ
                dve.wait_ge(topk, base + 6 * ROUNDS * NSEQ)
                me.add(nc.vector.tensor_copy(bias_p[:, 0:P], tri[:, 2, :]))
                for b in (1, 2, 3):
                    me.add(nc.vector.tensor_scalar(SP[b], SP[b], 0.9 * TAKEN, MASKED, ALU.is_gt, ALU.mult))
                me.wait()
                for b in (1, 2, 3):
                    d = SP[b][:, b * P:]
                    me.add(nc.vector.tensor_tensor(d, d, tri[:, 2, :], ALU.add))
                me.wait()
                dve_count[0] = me.n
        at[0] = KEEP2
        cum, dec, qE, kE = (carve(4 * TOK).rearrange("p (h n) -> p h n", h=HA) for _ in range(4))
        sc = carve(NT * 512).rearrange("p (c n) -> p c n", c=NT)
        sc_n = carve(HA * NS)[0:NS]
        levels = carve(len(LEVELS) * HA * P // 4).bitcast(U8).rearrange("p (l n) -> p l n", l=len(LEVELS))
        levels_f = qE.rearrange("p h n -> p (h n)")[:, 0:len(LEVELS) * P].rearrange("p (l n) -> p l n", l=len(LEVELS))
        state = carve(HA * P)
        seqcols = carve(NSEQ * NS)
        el_p, el_n = carve(HA * NT), carve(HA * NSEQ)
        lbl = carve(2 * HA).rearrange("p (a h) -> p a h", a=2)
        lb, lbc, lbt = carve(HA), carve(HA), carve(2 * HA).rearrange("p (a h) -> p a h", a=2)
        gn = carve(P)
        qa, ky = aF[:, 0:HA], aF[:, HA:2 * HA]
        ia, ga = aT[:, :, 0:W2], aT[:, :, W2:D]
        xflat = xT[:].rearrange("p c n -> p (c n)")
        lgt = [xflat[:, 512 * a:512 * a + 512] for a in range(2)]
        prb = [xflat[:, 1024 + 512 * a:1536 + 512 * a] for a in range(2)]
        prT = [xflat[:, 2048 + 512 * a:2560 + 512 * a] for a in range(2)]
        wo = wbuf[:].rearrange("p b c n -> p (b c n)").rearrange("p (c n) -> p c n", c=KC)
        nm4, rs4, ri4 = small[:, 40:44], small[:, 44:48], small[:, 48:52]

        par_in, wo_in, lev_in = sem("par_in"), sem("wo_in"), sem("lev_in")
        gate_ok, lb_ok, sig_ok, f_ok, ln_ok = sem("gate_ok"), sem("lb_ok"), sem("sig_ok"), sem("f_ok"), sem("ln_ok")
        ke_z = sem("ke_z")
        key_ok, q_ok, diff_ok, dec_ok, qe_ok, ke_ok = (sem("key_ok"), sem("q_ok"), sem("diff_ok"), sem("dec_ok"),
                                                       sem("qe_ok"), sem("ke_ok"))
        lv, lv_ev = sem("lv"), sem("lv_ev")
        lg, lmax, lex, ltr, ltr_ev, lpv, lout = (sem("lg"), sem("lmax"), sem("lex"), sem("ltr"), sem("ltr_ev"),
                                                 sem("lpv"), sem("lout"))
        NLEV = len(LEVELS)
        JOBS = [(l, c) for l in range(NLEV) for c in range(NT + (LEVELS[l] < NNEW))]
        FIRST = [min(n for n, j in enumerate(JOBS) if j[0] == l) for l in range(NLEV)] + [len(JOBS)]
        NA = HB * NT

        def jobs_of(a):
            l, c = a // 4, a % 4
            n0, n1 = FIRST[l], FIRST[l + 1]
            return range(n0, n0 + 3) if c == 0 else range(n0 + 3, n1) if c == 1 else range(0)

        def span(l):
            return TOK if LEVELS[l] < NNEW else SEQ

        def halves(x, l):
            b = LEVELS[l]
            v = x[:, :, 0:span(l)].rearrange("p h (n r) -> p h n r", r=2 * b)
            return v[:, :, :, 0:b], v[:, :, :, b:2 * b], v[:, :, :, b - 1:b]

        with nc.Block() as block:
            @block.sync
            def _(sp):
                sp.dma_start(levels_f, c_levels.rearrange("p (l n) -> p l n", l=NLEV)).then_inc(lev_in, 16)
                sp.dma_start(gn, hgrn_norm_g.partition_broadcast(P)).then_inc(par_in, 16)
                sp.dma_start(seqcols, c_seqcols).then_inc(par_in, 16)
                for a in range(2):
                    for h in range(HA):
                        sp.dma_start(lbl[:, a, h:h + 1], hgrn_lb_logits[a, h * P:(h + 1) * P].unsqueeze(1)).then_inc(par_in, 16)
                for c in range(2):
                    sp.dma_start(wo[:, 4 * c:4 * c + 4], wo_rows[:, 4 * c:4 * c + 4]).then_inc(wo_in, 16)
                sp.wait_ge(par_in, 160)
                sp.wait_ge(lev_in, 16)
                sp.wait_ge(wo_in, 32)

            @block.tensor
            def _(pe):
                def level_job(n):
                    l, c = JOBS[n]
                    if n >= 3:
                        pe.wait_ge(lv_ev, n - 2)
                    if l == 0:
                        pe.wait_ge(q_ok, 1)
                        pe.wait_ge(key_ok, 1)
                    else:
                        pe.wait_ge(qe_ok, l)
                        pe.wait_ge(ke_ok, l)
                    kk, qq = (ky, qa) if l == 0 else (kE, qE)
                    w, c0 = (P, c * P) if c < NT else (NS, SEQ)
                    for h in range(HA):
                        mm = pe.matmul(psum[0:w, n % 3, h * w:(h + 1) * w], kk[:, h, c0:c0 + w], qq[:, h, c0:c0 + w],
                                       start=True, stop=True, skip_group_check=True)
                    mm.then_inc(lv, 1)

                def prompt_logits(a):
                    h, b = a // NT, a % NT
                    if a >= 2:
                        pe.wait_ge(lmax, a - 1)
                    r = DH * (h % 2)
                    pe.matmul(psum[:, 3 + a % 2, 0:(b + 1) * P], qT[r:r + DH, h // 2, b * P:(b + 1) * P],
                              kT[r:r + DH, h // 2, 0:(b + 1) * P], start=True, stop=True).then_inc(lg, 1)

                def turn(a):
                    b = a % NT
                    pe.wait_ge(lex, a + 1)
                    if a >= 2:
                        pe.wait_ge(ltr_ev, a - 1)
                    for k in range(b + 1):
                        mm = pe.transpose(psum[:, 5 + a % 2, k * P:(k + 1) * P], prb[a % 2][:, k * P:(k + 1) * P], ident[:])
                    mm.then_inc(ltr, 1)

                def prompt_values(a):
                    h, b = a // NT, a % NT
                    pe.wait_ge(ltr_ev, a + 1)
                    if a >= 1:
                        pe.wait_ge(lout, a)
                    for k in range(b + 1):
                        mm = pe.matmul(psum[:, 7, 0:P], prT[a % 2][:, k * P:(k + 1) * P],
                                       v_tok[:, k, (h // 2) * P:(h // 2 + 1) * P], start=(k == 0), stop=(k == b))
                    mm.then_inc(lpv, 1)

                for a in range(NA + 2):
                    if a < NA:
                        prompt_logits(a)
                        for n in jobs_of(a):
                            level_job(n)
                    if 1 <= a <= NA:
                        turn(a - 1)
                    if a >= 2:
                        prompt_values(a - 2)

            @block.scalar
            def _(act):
                act.wait_ge(par_in, 160)
                act.wait_ge(lb_ok, 1)
                nc.scalar.activation(lbt, lbt, ACT.Exp).then_inc(lb_ok, 1)
                nc.scalar.activation(dec, ky, ACT.Sigmoid).then_inc(sig_ok, 1)
                act.wait_ge(sig_ok, 1)
                nc.scalar.activation(ky, ky, ACT.Sigmoid, scale=-1.0).then_inc(sig_ok, 1)
                nc.scalar.activation(qa, qa, ACT.Silu).then_inc(q_ok, 1)
                nc.scalar.activation(ga[:, 0:NT], ga[:, 0:NT], ACT.Silu).then_inc(gate_ok, 1)
                nc.scalar.activation(ga[0:NS, NT], ga[0:NS, NT], ACT.Silu).then_inc(gate_ok, 1)
                act.wait_ge(f_ok, HA)
                nc.scalar.activation(dec, dec, ACT.Ln).then_inc(ln_ok, 1)

                def exponential(a):
                    b = a % NT
                    act.wait_ge(lmax, a + 1)
                    if a >= 2:
                        act.wait_ge(ltr, a - 1)
                        act.wait_ge(lout, a - 3) if a >= 4 else None
                    w = (b + 1) * P
                    nc.scalar.activation(prb[a % 2][:, 0:w], lgt[a % 2][:, 0:w], ACT.Exp, bias=nm4[:, a % 4:a % 4 + 1],
                                         scale=-1.0, accum_out=rs4[:, a % 4:a % 4 + 1]).then_inc(lex, 1)

                def probs_out(a):
                    act.wait_ge(ltr, a + 1)
                    if a >= 2:
                        act.wait_ge(lpv, a - 1)
                    w = (a % NT + 1) * P
                    nc.scalar.copy(prT[a % 2][:, 0:w], psum[:, 5 + a % 2, 0:w]).then_inc(ltr_ev, 1)

                for a in range(NA + 1):
                    if a < NA:
                        l = a // 4 + 1
                        if a % 4 == 1 and l < NLEV:
                            act.wait_ge(diff_ok, 2 * l)
                            nc.scalar.activation(dec[:, :, 0:span(l)], dec[:, :, 0:span(l)], ACT.Exp).then_inc(dec_ok, 1)
                        exponential(a)
                    if a >= 1:
                        probs_out(a - 1)

            @block.gpsimd
            def _(pool):
                pool.wait_ge(par_in, 160)
                pool.wait_ge(gate_ok, 2)
                for t in range(NT + 1):
                    r = ROWS[t]
                    v = ga[0:r, t].rearrange("p (h n) -> p h n", h=HA)
                    nc.gpsimd.tensor_tensor(v, v, gn[0:r].unsqueeze(1).to_broadcast([r, HA, P]), ALU.mult).then_inc(gate_ok, 1)
                nc.gpsimd.memset(kE, 0.0).then_inc(ke_z, 1)
                pool.wait_ge(ke_z, 1)
                for l in range(1, NLEV):
                    pool.wait_ge(dec_ok, l)
                    pool.wait_ge(key_ok, 1)
                    if l > 1:
                        pool.wait_ge(lv, FIRST[l])
                    nc.gpsimd.tensor_tensor(halves(kE, l)[0], halves(ky, l)[0], halves(dec, l)[0], ALU.mult).then_inc(ke_ok, 1)

            @block.vector
            def _(dve):
                me = Tally(dve, dve_own, dve_count[0])
                dve.wait_ge(par_in, 160)
                me.link(nc.vector.tensor_tensor(lb, lbl[:, 0], lbl[:, 1], ALU.max))
                nc.vector.tensor_tensor(lbt, lbl, lb.unsqueeze(1).to_broadcast([P, 2, HA]), ALU.subtract).then_inc(lb_ok, 1)
                me.link(nc.vector.memset(sc, 0.0))
                me.link(nc.vector.memset(sc_n, 0.0))
                dve.wait_ge(lev_in, 16)
                for h in range(HA):
                    me.add(nc.vector.tensor_copy(levels[:, :, h * P:(h + 1) * P], levels_f))
                me.wait()
                me.link(nc.vector.memset(qE, 0.0))
                dve.wait_ge(lb_ok, 2)
                me.link(nc.vector.tensor_tensor(lbc, lbt[:, 0], lbt[:, 1], ALU.add))
                me.link(nc.vector.reciprocal(lbc, lbc))
                me.link(nc.vector.tensor_tensor(lb, lbt[:, 0], lbc, ALU.mult))
                me.link(nc.vector.tensor_scalar(lbc, lb, -1.0, 1.0, ALU.mult, ALU.add))
                dve.wait_ge(sig_ok, 1)
                for h in range(HA):
                    nc.vector.tensor_scalar(dec[:, h], dec[:, h], lbc[:, h:h + 1], lb[:, h:h + 1], ALU.mult, ALU.add).then_inc(f_ok, 1)
                dve.wait_ge(sig_ok, 2)
                for h in range(HA):
                    ins = nc.vector.tensor_scalar(ky[:, h], ky[:, h], lbc[:, h:h + 1], None, ALU.mult)
                ins.then_inc(key_ok, 1)
                dve.wait_ge(ln_ok, 1)
                for h in range(HA):
                    me.add(nc.vector.tensor_tensor_scan(cum[:, h], keep[:], dec[:, h], 0.0, ALU.mult, ALU.add))
                me.wait()

                def differences(l):
                    left, right, edge = halves(cum, l)
                    dl, dr, _ = halves(dec, l)
                    shape = list(left.shape)
                    if l > 1:
                        dve.wait_ge(ke_ok, l - 1)
                        dve.wait_ge(qe_ok, l - 1)
                    nc.vector.tensor_tensor(dl, edge.to_broadcast(shape), left, ALU.subtract).then_inc(diff_ok, 1)
                    nc.vector.tensor_tensor(dr, right, edge.to_broadcast(shape), ALU.subtract).then_inc(diff_ok, 1)

                def scores_out(n):
                    l, c = JOBS[n]
                    dve.wait_ge(lv, n + 1)
                    if c < NT:
                        out, mask, src = sc[:, c], levels[:, l], psum[:, n % 3, :]
                    else:
                        out = sc_n.rearrange("p (h n) -> p h n", h=HA)
                        mask = levels[0:NS, l].rearrange("p (h n) -> p h n", h=HA)[:, :, 0:NS]
                        src = psum[0:NS, n % 3, 0:HA * NS].rearrange("p (h n) -> p h n", h=HA)
                    nc.vector.copy_predicated(out, mask, src).then_inc(lv_ev, 1)

                def mask_and_max(a):
                    b = a % NT
                    w = (b + 1) * P
                    dve.wait_ge(lg, a + 1)
                    if a >= 2:
                        dve.wait_ge(lex, a - 1)
                    nc.vector.tensor_tensor_reduce(lgt[a % 2][:, 0:w], psum[:, 3 + a % 2, 0:w],
                                                   bias_p[:, POFF[b]:POFF[b] + w], -1.0, 3.0e38, ALU.add, ALU.min,
                                                   nm4[:, a % 4:a % 4 + 1]).then_inc(lmax, 1)

                def attended(a):
                    h, b = a // NT, a % NT
                    dve.wait_ge(lex, a + 1)
                    me.link(nc.vector.reciprocal(ri4[:, a % 4:a % 4 + 1], rs4[:, a % 4:a % 4 + 1]))
                    dve.wait_ge(lpv, a + 1)
                    g = gB[:, b, h * DH:(h + 1) * DH]
                    nc.vector.scalar_tensor_tensor(g, psum[:, 7, DH * (h % 2):DH * (h % 2) + DH], ri4[:, a % 4:a % 4 + 1],
                                                   g, ALU.mult, ALU.mult).then_inc(lout, 1)

                for a in range(NA + 2):
                    if a < NA:
                        l = a // 4 + 1
                        if a % 4 == 0 and l < NLEV:
                            differences(l)
                        mask_and_max(a)
                        for n in jobs_of(a):
                            scores_out(n)
                        if a % 4 == 2 and l < NLEV:
                            dve.wait_ge(dec_ok, l)
                            dve.wait_ge(lv, FIRST[l])
                            dve.wait_ge(q_ok, 1)
                            nc.vector.tensor_tensor(halves(qE, l)[1], halves(qa, l)[1], halves(dec, l)[1],
                                                    ALU.mult).then_inc(qe_ok, 1)
                    if a >= 2:
                        attended(a - 2)
                dve_count[0] = me.n

        kdT = arena[:, KEEP2:KEEP2 + (NT + 1) * W2].rearrange("p (t n) -> p t n", n=W2)
        oa = aF.rearrange("p c n -> p (c n)")[:, 0:(NT + 1) * W2].rearrange("p (t n) -> p t n", n=W2)
        s0 = xflat[:, 0:NSEQ * HA * P].rearrange("p (s h n) -> p s h n", s=NSEQ, h=HA)
        vflat = v_tok[:].rearrange("p t n -> p (t n)")
        vx = [vflat[0:NS, a * 1024:(a + 1) * 1024].rearrange("p (s n) -> p s n", s=NSEQ) for a in range(2)]
        qx = [bias_p[:, a * 512:(a + 1) * 512].rearrange("p (s n) -> p s n", s=NSEQ) for a in range(2)]
        sq = vflat[:, 2048:2048 + P]
        ss = small[:, 56:56 + 4 * (NT + 1)]
        state_st = sem("state_st")
        s0_in, e_ok, qc_ok, el_ok, dl_ok, dl_ex, kd_ok = (sem("s0_in"), sem("e_ok"), sem("qc_ok"), sem("el_ok"),
                                                          sem("dl_ok"), sem("dl_ex"), sem("kd_ok"))
        kt, kt_ev, kv, st_ok, oc, oc_ev = sem("kt"), sem("kt_ev"), sem("kv"), sem("st_ok"), sem("oc"), sem("oc_ev")
        qx_ok, vx_ok, dec_o, skv, skv_ev, sdec = (sem("qx_ok"), sem("vx_ok"), sem("dec_o"), sem("skv"), sem("skv_ev"),
                                                  sem("sdec"))
        ss_ok, ss_v, ss_r, mixed = sem("ss_ok"), sem("ss_v"), sem("ss_r"), sem("mixed")
        with nc.Block() as block:
            @block.sync
            def _(sp):
                sp.dma_start(s0, state_hgrn[0].rearrange("s h k v -> k s h v")).then_inc(s0_in, 16)
                sp.wait_ge(st_ok, HA * NT)
                sp.dma_start(st_prompt[0, 0].rearrange("h k v -> k h v"),
                             state.rearrange("p (h n) -> p h n", h=HA)).then_inc(state_st, 16)
                sp.wait_ge(skv_ev, HA)
                sp.dma_start(st_sample[0].rearrange("s h k v -> k s h v"), s0).then_inc(state_st, 16)
                sp.wait_ge(state_st, 32)

            @block.tensor
            def _(pe):
                pe.wait_ge(kd_ok, 1)
                for t in range(NT + 1):
                    r = ROWS[t]
                    if t >= 2:
                        pe.wait_ge(kt_ev, t - 1)
                    for h in range(HA):
                        mm = pe.transpose(psum[0:r, t % 2, h * P:(h + 1) * P], kE[:, h, t * P:t * P + r], ident[:])
                    mm.then_inc(kt, 1)
                pe.wait_ge(qc_ok, 1)
                for c in range(NT):
                    pe.wait_ge(kt_ev, c + 1)
                    if c >= 2:
                        pe.wait_ge(st_ok, HA * (c - 1))
                    for h in range(HA):
                        mm = pe.matmul(psum[:, 4 + c % 2, h * P:(h + 1) * P], kdT[:, c, h * P:(h + 1) * P],
                                       ia[:, c, h * P:(h + 1) * P], start=True, stop=True, skip_group_check=True)
                    mm.then_inc(kv, 1)
                    if c >= 2:
                        pe.wait_ge(oc_ev, c - 1)
                    for h in range(HA):
                        out = psum[:, 2 + c % 2, h * P:(h + 1) * P]
                        mm = pe.matmul(out, sc[:, c, h * P:(h + 1) * P], ia[:, c, h * P:(h + 1) * P],
                                       start=True, stop=(c == 0), skip_group_check=True)
                        if c:
                            pe.wait_ge(st_ok, HA * c)
                            mm = pe.matmul(out, qE[:, h, c * P:(c + 1) * P], state[:, h * P:(h + 1) * P],
                                           start=False, stop=True, skip_group_check=True)
                    mm.then_inc(oc, 1)
                pe.wait_ge(s0_in, 16)
                for h in range(HA):
                    out = psum[0:NS, 6, h * P:(h + 1) * P]
                    pe.matmul(out, sc_n[:, h * NS:(h + 1) * NS], ia[0:NS, NT, h * P:(h + 1) * P],
                              start=True, stop=False, skip_group_check=True)
                    pe.wait_ge(qx_ok, h + 1)
                    for s in range(NSEQ):
                        mm = pe.matmul(out, qx[h % 2][:, s, :], s0[:, s, h, :], start=False, stop=(s == NSEQ - 1),
                                       skip_group_check=True)
                    mm.then_inc(dec_o, 1)
                pe.wait_ge(kt_ev, NT + 1)
                for h in range(HA):
                    pe.wait_ge(vx_ok, h + 1)
                    if h:
                        pe.wait_ge(skv_ev, h)
                    for a in range(2):
                        mm = pe.matmul(psum[:, a, :], kdT[0:NS, NT, h * P:(h + 1) * P],
                                       vx[h % 2][:, 4 * a:4 * a + 4, :], start=True, stop=True)
                    mm.then_inc(skv, 1)

            @block.scalar
            def _(act):
                nc.scalar.activation(dec, cum, ACT.Exp).then_inc(e_ok, 1)
                act.wait_ge(dl_ok, 2)
                nc.scalar.activation(dec, dec, ACT.Exp).then_inc(dl_ex, 1)
                for t in range(NT + 1):
                    r = ROWS[t]
                    act.wait_ge(kt, t + 1)
                    nc.scalar.copy(kdT[0:r, t, :], psum[0:r, t % 2, :]).then_inc(kt_ev, 1)
                for t in range(NT + 1):
                    r = ROWS[t]
                    act.wait_ge(oc_ev, t + 1)
                    for h in range(HA):
                        n = t * HA + h
                        if n:
                            act.wait_ge(ss_ok, n)
                        nc.scalar.activation(sq[0:r], oa[0:r, t, h * P:(h + 1) * P], ACT.Square,
                                             accum_out=ss[0:r, n:n + 1]).then_inc(ss_ok, 1)
                act.wait_ge(ss_v, 1)
                nc.scalar.activation(ss, ss, ACT.Sqrt).then_inc(ss_v, 1)

            @block.gpsimd
            def _(pool):
                for h in range(HA):
                    pool.wait_ge(qc_ok, 1)
                    if h >= 2:
                        pool.wait_ge(dec_o, h - 1)
                    nc.gpsimd.tensor_tensor(qx[h % 2], seqcols.rearrange("p (s n) -> p s n", s=NSEQ),
                                            qE[:, h, SEQ:TOK].unsqueeze(1).to_broadcast([P, NSEQ, NS]),
                                            ALU.mult).then_inc(qx_ok, 1)
                for h in range(HA):
                    if h >= 2:
                        pool.wait_ge(skv, h - 1)
                    nc.gpsimd.tensor_tensor(vx[h % 2], ia[0:NS, NT, h * P:(h + 1) * P].unsqueeze(1).to_broadcast([NS, NSEQ, P]),
                                            ofseq[:].unsqueeze(2).to_broadcast([NS, NSEQ, P]), ALU.mult).then_inc(vx_ok, 1)
                    pool.wait_ge(dec_o, h + 1)
                    pool.wait_ge(el_ok, 2)
                    nc.gpsimd.tensor_tensor(s0[:, :, h, :], s0[:, :, h, :],
                                            el_n[:, h * NSEQ:(h + 1) * NSEQ].unsqueeze(2).to_broadcast([P, NSEQ, P]),
                                            ALU.mult).then_inc(sdec, 1)

            @block.vector
            def _(dve):
                me = Tally(dve, dve_own, dve_count[0])
                nc.vector.memset(ss, 1.0)
                dve.wait_ge(e_ok, 1)
                nc.vector.tensor_tensor(qE, qa, dec, ALU.mult).then_inc(qc_ok, 1)
                nc.vector.tensor_copy(el_p.rearrange("p (h n) -> p h n", h=HA), dec[:, :, P - 1:SEQ:P]).then_inc(el_ok, 1)
                nc.vector.tensor_copy(el_n.rearrange("p (h n) -> p h n", h=HA), dec[:, :, SEQ + NNEW - 1:TOK:NNEW]).then_inc(el_ok, 1)
                dve.wait_ge(el_ok, 2)
                dve.wait_ge(qc_ok, 1)
                for (a, b, w) in ((0, SEQ, P), (SEQ, TOK, NNEW)):
                    v = cum[:, :, a:b].rearrange("p h (n r) -> p h n r", r=w)
                    last = v[:, :, :, w - 1:w].to_broadcast(list(v.shape))
                    nc.vector.tensor_tensor(dec[:, :, a:b].rearrange("p h (n r) -> p h n r", r=w), last, v,
                                            ALU.subtract).then_inc(dl_ok, 1)
                dve.wait_ge(dl_ex, 1)
                nc.vector.tensor_tensor(kE, ky, dec, ALU.mult).then_inc(kd_ok, 1)
                for c in range(NT):
                    dve.wait_ge(kv, c + 1)
                    if c:
                        dve.wait_ge(oc, c + 1)
                    for h in range(HA):
                        st = state[:, h * P:(h + 1) * P]
                        src = psum[:, 4 + c % 2, h * P:(h + 1) * P]
                        if c == 0:
                            nc.vector.tensor_copy(st, src).then_inc(st_ok, 1)
                        else:
                            if h == 0:
                                dve.wait_ge(st_ok, HA * c)
                            nc.vector.scalar_tensor_tensor(st, st, el_p[:, h * NT + c:h * NT + c + 1], src,
                                                           ALU.mult, ALU.add).then_inc(st_ok, 1)
                    if c:
                        nc.vector.tensor_copy(oa[:, c - 1, :], psum[:, 2 + (c - 1) % 2, :]).then_inc(oc_ev, 1)
                dve.wait_ge(oc, NT)
                nc.vector.tensor_copy(oa[:, NT - 1, :], psum[:, 2 + (NT - 1) % 2, :]).then_inc(oc_ev, 1)
                dve.wait_ge(dec_o, HA)
                nc.vector.tensor_copy(oa[0:NS, NT, :], psum[0:NS, 6, :]).then_inc(oc_ev, 1)
                for h in range(HA):
                    dve.wait_ge(skv, h + 1)
                    dve.wait_ge(sdec, h + 1)
                    for a in range(2):
                        v = s0[:, 4 * a:4 * a + 4, h, :]
                        ins = nc.vector.tensor_tensor(v, v, psum[:, a, :].rearrange("p (s n) -> p s n", s=4), ALU.add)
                    ins.then_inc(skv_ev, 1)
                dve.wait_ge(ss_ok, HA * (NT + 1))
                nc.vector.tensor_scalar(ss[:], ss[:], 1.0 / P, EPS, ALU.mult, ALU.add).then_inc(ss_v, 1)
                dve.wait_ge(ss_v, 2)
                me.link(nc.vector.reciprocal(ss, ss))
                dve.wait_ge(gate_ok, NT + 3)
                for t in range(NT + 1):
                    r = ROWS[t]
                    for h in range(HA):
                        o = oa[0:r, t, h * P:(h + 1) * P]
                        ins = nc.vector.scalar_tensor_tensor(o, o, ss[0:r, t * HA + h:t * HA + h + 1],
                                                             ga[0:r, t, h * P:(h + 1) * P], ALU.mult, ALU.mult)
                    ins.then_inc(mixed, 1)
                dve_count[0] = me.n

        mixA, mixB = qT, kT
        at[0] = KEEP2 + 2 * 4 * TOK
        xr = [carve(D) for _ in range(2)]
        z = [carve(D) for _ in range(2)]
        lng, lnb = carve(D), carve(D)
        st2 = small[:, 80:92].rearrange("p (a n) -> p a n", a=2)
        mv2 = small[:, 92:94]
        sd = small[:, 94:95]
        ln_in, xr_in = sem("ln_in"), sems("xr_in", 2)
        mt, mt_ev, yb, zr, zv, zs, zn, zf = (sem("mt"), sem("mt_ev"), sem("yb"), sem("zr"), sem("zv"), sem("zs"),
                                             sem("zn"), sem("zf"))
        zg, y_st = sem("zg"), sems("y_st", 2)
        with nc.Block() as block:
            @block.sync
            def _(sp):
                sp.dma_start(lng, ln_g.partition_broadcast(P)).then_inc(ln_in, 16)
                sp.dma_start(lnb, ln_b.partition_broadcast(P)).then_inc(ln_in, 16)
                def store(t):
                    sp.wait_ge(zf, t + 1)
                    sp.dma_start(y_prompt[0].rearrange("(t p) d -> t p d", p=P)[t] if t < NT
                                 else y_sample.rearrange("s t d -> (s t) d"), z[t % 2][0:ROWS[t]]).then_inc(y_st[t % 2], 16)

                for t in range(NT + 1):
                    if t >= 2:
                        sp.wait_ge(zr, 2 * (t - 1))
                    sp.dma_start(xr[t % 2][0:ROWS[t]], xp_rows[t] if t < NT else xs_rows).then_inc(xr_in[t % 2], 16)
                    if t >= 2:
                        store(t - 2)
                store(NT - 1)
                store(NT)
                sp.wait_ge(y_st[0], 48)
                sp.wait_ge(y_st[1], 32)
                sp.wait_ge(stored, NSTORE[0])

            @block.tensor
            def _(pe):
                n = 0
                for t in range(NT + 1):
                    r = ROWS[t]
                    for src in (oa, gB):
                        if n >= 2:
                            pe.wait_ge(mt_ev, n - 1)
                        for c in range(4):
                            mm = pe.transpose(psum[:, n % 2, c * P:c * P + r], src[0:r, t, c * P:(c + 1) * P],
                                              ident[0:r, 0:r])
                        mm.then_inc(mt, 1)
                        n += 1
                for a in range(2):
                    pe.wait_ge(mt_ev, n - 1)
                    for s in range(4):
                        mm = pe.transpose(psum[:, n % 2, s * P:(s + 1) * P], osb[:, 4 * a + s, :], ident[:])
                    mm.then_inc(mt, 1)
                    n += 1
                pe.wait_ge(mt_ev, n)
                for t in range(NT + 1):
                    r = ROWS[t]
                    for a in range(2):
                        m = 2 * t + a
                        if m >= 4:
                            pe.wait_ge(zr, m - 3)
                        for c in range(KC):
                            src = (mixA, mixB)[c // 4][:, c % 4, t * P:t * P + r]
                            mm = pe.matmul(psum[0:r, 2 + m % 4, :], src, wo[:, c, a * 512:(a + 1) * 512],
                                           start=(c == 0), stop=(c == KC - 1))
                        mm.then_inc(yb, 1)

            @block.scalar
            def _(act):
                n = 0
                for t in range(NT + 1):
                    r = ROWS[t]
                    for dst in (mixA, mixB):
                        act.wait_ge(mt, n + 1)
                        nc.scalar.copy(dst[:, :, t * P:t * P + r],
                                       psum[:, n % 2, :].rearrange("p (c n) -> p c n", c=4)[:, :, 0:r]).then_inc(mt_ev, 1)
                        n += 1
                for t in range(NT + 1):
                    r = ROWS[t]
                    act.wait_ge(zv, t + 1)
                    nc.scalar.activation(sd[0:r], sd[0:r], ACT.Sqrt).then_inc(zs, 1)

            @block.gpsimd
            def _(pool):
                pool.wait_ge(ln_in, 32)
                for t in range(NT + 1):
                    r = ROWS[t]
                    zz = z[t % 2][0:r]
                    pool.wait_ge(zn, t + 1)
                    nc.gpsimd.tensor_tensor(zz, zz, lng[0:r], ALU.mult).then_inc(zg, 1)
                    pool.wait_ge(zg, t + 1)
                    nc.gpsimd.tensor_tensor(zz, zz, lnb[0:r], ALU.add).then_inc(zf, 1)

            @block.vector
            def _(dve):
                me = Tally(dve, dve_own, dve_count[0])
                n = 2 * (NT + 1)
                dve.wait_ge(mt_ev, n)
                for a in range(2):
                    dve.wait_ge(mt, n + 1)
                    for h in range(2):
                        g = mixB[DH * h:DH * h + DH, :, SEQ + 32 * a:SEQ + 32 * a + 32].rearrange(
                            "p j (s q) -> p j s q", q=NNEW)
                        src = psum[DH * h:DH * h + DH, n % 2, :].rearrange("p (s j x) -> p j s x", s=4, j=4)[
                            :, :, :, NNEW * h:NNEW * h + NNEW]
                        ins = nc.vector.tensor_tensor(g, src, g, ALU.mult)
                        if h == 0:
                            me.add(ins)
                    ins.then_inc(mt_ev, 1)
                    n += 1
                for t in range(NT + 1):
                    r = ROWS[t]
                    zz = z[t % 2][0:r]
                    dve.wait_ge(xr_in[t % 2], 16 * (t // 2 + 1))
                    if t >= 2:
                        dve.wait_ge(y_st[t % 2], 16 * (t // 2))
                    for a in range(2):
                        m = 2 * t + a
                        dve.wait_ge(yb, m + 1)
                        w = slice(a * 512, a * 512 + 512)
                        nc.vector.scalar_tensor_tensor(zz[:, w], xr[t % 2][0:r, w], ALPHA, psum[0:r, 2 + m % 4, :],
                                                       ALU.mult, ALU.add).then_inc(zr, 1)
                        dve.wait_ge(zr, m + 1)
                        me.add(nc.vector.bn_stats(st2[0:r, a], zz[:, w]))
                    me.wait()
                    me.link(nc.vector.bn_aggr(mv2[0:r], st2[0:r]))
                    nc.vector.tensor_scalar(sd[0:r], mv2[0:r, 1:2], EPS, None, ALU.add).then_inc(zv, 1)
                    dve.wait_ge(zs, t + 1)
                    me.link(nc.vector.reciprocal(sd[0:r], sd[0:r]))
                    nc.vector.tensor_scalar(zz, zz, mv2[0:r, 0:1], sd[0:r], ALU.subtract, ALU.mult).then_inc(zn, 1)
                dve_count[0] = me.n


_INS = ["x_prompt", "x_sample", "cache_k", "cache_v", "cache_kidx", "state_hgrn", "page_table", "w_in",
        "hgrn_lb_logits", "hgrn_norm_g", "idx_norm_g", "idx_norm_b", "w_out", "ln_g", "ln_b"]
_OUTS = [(1, SEQ, D), (NSEQ, NNEW, D), (1, NT, 1, PAGE, HB, DH), (1, NT, 1, PAGE, HB, DH), (1, NT, 1, PAGE, DH),
         (1, 1, HA, P, P), (NSEQ, 1, NNEW, HB, DH), (NSEQ, 1, NNEW, HB, DH), (NSEQ, 1, NNEW, DH),
         (1, NSEQ, HA, P, P)]


def kernel(**inputs):
    import numpy as _np
    import concourse.bacc as _bacc
    from concourse import mybir as _mybir
    from concourse.bass_utils import run_bass_kernel_spmd as _run

    nc = _bacc.Bacc("TRN2", target_bir_lowering=False, num_devices=1)
    arrays, args = {}, []
    given = {name: _np.ascontiguousarray(inputs[name]) for name in _INS}
    given.update({f"c_{name}": a for name, a in shape_constants().items()})
    for name, a in given.items():
        arrays[f"in_{name}"] = a
        args.append(nc.dram_tensor(f"in_{name}", a.shape, _mybir.dt.from_np(a.dtype), kind="ExternalInput").ap())
    for i, shape in enumerate(_OUTS):
        args.append(nc.dram_tensor(f"out_{i}", shape, F32, kind="ExternalOutput").ap())
    hybrid_step(nc, *args)
    r = _run(nc, [arrays], core_ids=[0])
    return tuple(r.results[0][f"out_{i}"] for i in range(len(_OUTS)))
```

```python
from contextlib import ExitStack

import numpy as np
import concourse.bass as bass
from concourse import mybir

ALU = mybir.AluOpType
ACT = mybir.ActivationFunctionType
F32 = mybir.dt.float32
BF16 = mybir.dt.bfloat16
I32 = mybir.dt.int32
U8 = mybir.dt.uint8
AX = mybir.AxisListType

P = 128
D = 1024
SEQ = 512
NSEQ, NNEW = 8, 8
NS = NSEQ * NNEW
TOK = SEQ + NS
NT = SEQ // P
KC = D // P
HA = 4
HB, DH = 8, 64
HI = 16
PAGE, NPG = 128, 16
PAST = PAGE * NPG
W2 = HB * DH
LS = PAST + NS
TOPK_P, TOPK_S = min(256, SEQ // 4), min(256, (PAST + NNEW) // 4)
G_QA, G_FA, G_IA, G_GA = 0, 512, 1024, 1536
G_QB, G_KB, G_VB, G_GB, G_QI, G_KI = 2048, 2560, 3072, 3584, 4096, 5120
EPS = 1e-5
ALPHA = 2.0 ** 0.25
ROT = 8
TAKEN = -3.0e38
MASKED = -1.0e30
LEVELS = [0, 1, 2, 4, 8, 16, 32, 64]
POFF = [0, 128, 384, 768]
PW = 1280


def shape_constants():
    c = {}
    c["ident"] = np.eye(P, dtype=np.float32)
    half = ROT
    inv = np.float32(500000.0) ** (-np.arange(half, dtype=np.float32) / np.float32(half))
    pos = np.concatenate([np.arange(SEQ), np.tile(PAST + np.arange(NNEW), NSEQ)]).astype(np.float32)
    ang = (pos[:, None] * inv[None, :]).astype(np.float32)
    cs = np.concatenate([np.cos(ang), np.sin(ang)], 1).astype(np.float32)
    rope = np.zeros((P, NT + 1, 2 * half), np.float32)
    for t in range(NT):
        rope[:, t] = cs[t * P:(t + 1) * P]
    rope[:NS, NT] = cs[SEQ:]
    c["rope"] = rope
    q, k = np.arange(P)[:, None], np.arange(P)[None, :]
    tri = (k <= q)
    c["tri"] = np.stack([tri.astype(np.float32), np.where(tri, 0, TAKEN).astype(np.float32),
                         np.where(tri, 0, MASKED).astype(np.float32)], 1)
    sq, sk = np.arange(NS)[:, None], np.arange(NS)[None, :]
    own = (sq // NNEW == sk // NNEW) & (sk % NNEW <= sq % NNEW)
    c["own"] = np.stack([own.astype(np.float32), np.where(own, 0, TAKEN).astype(np.float32),
                         np.where(own, 0, MASKED).astype(np.float32)], 1)
    pick = np.zeros((NS, NSEQ, 4, 32), np.float32)
    for s in range(NSEQ):
        for qq in range(NNEW):
            for hh in range(2):
                pick[s * NNEW + qq, s, :, hh * NNEW + qq] = 1
    c["pick"] = pick.reshape(NS, NSEQ * P)
    c["sameq"] = (np.arange(P)[:, None] % NNEW == np.arange(NS)[None, :] % NNEW).astype(np.float32)
    lv = np.zeros((P, len(LEVELS), P), np.float32)
    s, t = np.arange(P)[:, None], np.arange(P)[None, :]
    for i, b in enumerate(LEVELS):
        lv[:, i] = (s == t) if b == 0 else ((s // (2 * b) == t // (2 * b)) & (s % (2 * b) < b) & (t % (2 * b) >= b))
    c["levels"] = lv.reshape(P, len(LEVELS) * P)
    keep = np.ones((P, TOK), np.float32)
    keep[:, 0:SEQ:P] = 0
    keep[:, SEQ::NNEW] = 0
    c["keep"] = keep
    c["seqcols"] = np.broadcast_to(np.repeat(np.eye(NSEQ, dtype=np.float32), NNEW, 1).reshape(1, -1),
                                   (P, NSEQ * NS)).copy()
    c["ofseq"] = (np.arange(NS)[:, None] // NNEW == np.arange(NSEQ)[None, :]).astype(np.float32)
    return c


def begin(e, *given):
    for sem in given:
        e.sem_inc(sem, 1)


def after(e, sem, n):
    e.wait_ge(sem, n + 1)


class Tally:

    def __init__(self, eng, sem, n=0):
        self.eng, self.sem, self.n = eng, sem, n

    def add(self, ins):
        ins.then_inc(self.sem, 1)
        self.n = self.n + 1

    def wait(self):
        self.eng.wait_ge(self.sem, self.n)

    def link(self, ins):
        self.add(ins)
        self.wait()


def hybrid_step(nc, x_prompt, x_sample, cache_k, cache_v, cache_kidx, state_hgrn, page_table,
                w_in, hgrn_lb_logits, hgrn_norm_g, idx_norm_g, idx_norm_b, w_out, ln_g, ln_b,
                c_ident, c_rope, c_tri, c_own, c_pick, c_sameq, c_levels, c_keep, c_seqcols, c_ofseq,
                y_prompt, y_sample, k_prompt, v_prompt, ki_prompt, st_prompt,
                k_sample, v_sample, ki_sample, st_sample):
    w_rows = w_in[0].rearrange("(c p) n -> p c n", p=P)
    wo_rows = w_out[0].rearrange("(c p) n -> p c n", p=P)
    xp_rows = x_prompt[0].rearrange("(t p) d -> t p d", p=P)
    xs_rows = x_sample.rearrange("s t d -> (s t) d")

    with ExitStack() as ctx:
        def sb(name, shape, dt=F32):
            return ctx.enter_context(nc.sbuf_tensor(name, shape, dt))

        def sem(name):
            return ctx.enter_context(nc.semaphore(name))

        def sems(name, n):
            return [sem(f"{name}{i}") for i in range(n)]

        ident = sb("ident", [P, P])
        rope = sb("rope", [P, NT + 1, 2 * ROT])
        tri = sb("tri", [P, 3, P])
        own = sb("own", [NS, 3, NS])
        pick = sb("pick", [NS, NSEQ * P], BF16)
        sameq = sb("sameq", [P, NS])
        keep = sb("keep", [P, TOK])
        ofseq = sb("ofseq", [NS, NSEQ])
        gki = sb("gki", [P, 2, DH])
        pages = sb("pages", [1, NSEQ * NPG], I32)
        xT = sb("xT", [P, KC, TOK])
        late = sb("late", [P, 2 * 4 * TOK + (NT + 1) * W2 + PW])
        kT = late[:, 0:4 * TOK].rearrange("p (c n) -> p c n", c=4)
        qT = late[:, 4 * TOK:8 * TOK].rearrange("p (c n) -> p c n", c=4)
        gB = late[:, 8 * TOK:8 * TOK + (NT + 1) * W2].rearrange("p (t n) -> p t n", n=W2)
        bias_p = late[:, 8 * TOK + (NT + 1) * W2:]
        kidx = late[:, 0:NSEQ * NPG * DH].rearrange("p (s g n) -> p s g n", s=NSEQ, g=NPG)
        v_tok = sb("v_tok", [P, NT + 1, W2])
        bias_s = sb("bias_s", [NS, LS], BF16)
        small = sb("small", [P, 160])
        gn = sb("gn", [P, P])
        wbuf = sb("wbuf", [P, 2, KC, 512])
        ARENA = 25600
        arena = sb("arena", [P, ARENA])
        at = [0]

        def carve(n):
            a = at[0]
            at[0] += n
            assert at[0] <= ARENA, at[0]
            return arena[:, a:a + n]

        psum = ctx.enter_context(nc.psum_tensor("banks", [P, 8, 512], F32))

        at[0] = 0
        qi_tok = carve((NT + 1) * D).rearrange("p (t n) -> p t n", n=D)
        k_tok = qi_tok[:, :, 0:W2]
        q_tok = qi_tok[:, :, W2:D]
        qiT = carve(8 * SEQ).rearrange("p (c n) -> p c n", c=8)
        pick_f = qiT[0:NS, 0:2].rearrange("p c n -> p (c n)")
        qis = carve(NSEQ * P).rearrange("p (s h q) -> p s h q", s=NSEQ, h=HI)
        kxT = [carve(PAST // 2) for _ in range(2)]
        kiT = carve(TOK)
        relu_s = [carve(PAST) for _ in range(2)]
        relu_n = carve(NS)
        relu_p = carve(4 * 512).rearrange("p (b n) -> p b n", b=4)
        S = carve(LS)[0:NS]
        SP = {b: bias_p[:, POFF[b]:POFF[b] + (b + 1) * P] for b in (1, 2, 3)}
        kiwi = carve((NT + 1) * 80).rearrange("p (t n) -> p t n", n=80)
        kin = carve((NT + 1) * DH).rearrange("p (t n) -> p t n", n=DH)
        w_all = carve(NS)
        w_rep = carve(P)[0:NS]
        w_seq = carve(NSEQ * NS).rearrange("p (s n) -> p s n", s=NSEQ)
        rtmp = carve(4 * HI * ROT).rearrange("p (a n) -> p a n", a=4)
        stats = carve((NT + 1) * 6).rearrange("p (t n) -> p t n", n=6)
        mv = carve((NT + 1) * 2).rearrange("p (t n) -> p t n", n=2)
        rstd = carve(NT + 1)
        best = small[:, 96:128].rearrange("p (a n) -> p a n", a=4)
        newbias = carve(NS)[0:NS]
        xin = arena[:, ARENA - 5 * D:ARENA].rearrange("p (t n) -> p t n", n=D)
        assert at[0] <= ARENA

        const_in, pages_in, ki_par_in = sem("const_in"), sem("pages_in"), sem("ki_par_in")
        lbl, lbt = (small[:, a:a + 2 * HA].rearrange("p (a h) -> p a h", a=2) for a in (128, 136))
        lb, lbc = small[:, 144:148], small[:, 148:152]
        lb_in, lb_ok, gn_in = sem("lb_in"), sem("lb_ok"), sem("gn_in")
        x_in, x_half = sems("x_in", NT + 1), sems("x_half", 2)
        x_tr, x_ev = sem("x_tr"), sem("x_ev")
        w_got = sems("w_got", 2)
        proj, proj_ev = sem("proj"), sem("proj_ev")
        var_ok, std_ok, kin_ok = sem("var_ok"), sem("std_ok"), sem("kin_ok")
        act_own, dve_own, pool_own = sem("act_own"), sem("dve_own"), sem("pool_own")
        roped = sem("roped")
        wrep_ok = sem("wrep_ok")
        tr, tr_ev = sem("tr"), sem("tr_ev")
        qi_tr, qi_tr_ev = sem("qi_tr"), sem("qi_tr_ev")
        qs_tr, qs_dve, qs_act = sem("qs_tr"), sem("qs_dve"), sem("qs_act")
        tr2, tr2_act, tr2_dve = sem("tr2"), sem("tr2_act"), sem("tr2_dve")
        kidx_in, kidx_tr, kidx_ev = sems("kidx_in", NSEQ), sem("kidx_tr"), sem("kidx_ev")
        wseq_ok, rel, relu_ok, comb, rel_n, relun_ok, comb_n = (sem("wseq_ok"), sem("rel"), sem("relu_ok"), sem("comb"),
                                                                sem("rel_n"), sem("relun_ok"), sem("comb_n"))
        ofseq_in = sem("ofseq_in")
        prel, prelu, pacc, weighed = sem("prel"), sem("prelu"), sem("pacc"), sem("weighed")
        s_ok, topk = sem("s_ok"), sem("topk")
        stored = sem("stored")
        NSTORE = [0]
        halves_out = [0]
        dve_count, pool_count = [0], [0]

        ROWS = [P] * NT + [NS]
        GROUPS = [(G_KI, 80), (G_QI, 512), (G_QI + 512, 512), (G_VB, 512), (G_KB, 512), (G_QB, 512), (G_GB, 512)]
        BEFORE = 3
        PB = 4
        TB = 4
        CB = 6

        NCONST = 7 * 16

        def tiles_of(g):
            return [NT] + list(range(NT)) if g == BEFORE - 1 else list(range(NT + 1))

        at[0] = 0
        aF = carve(8 * TOK).rearrange("p (c n) -> p c n", c=8)
        aT = carve((NT + 1) * D).rearrange("p (t n) -> p t n", n=D)
        osb = carve(NSEQ * P).rearrange("p (s n) -> p s n", n=P)
        KEEP2 = at[0]
        qa, ky = aF[:, 0:HA], aF[:, HA:2 * HA]
        dec = arena[:, KEEP2 + HA * TOK:KEEP2 + 2 * HA * TOK].rearrange("p (h n) -> p h n", h=HA)
        k_buf = [carve(4 * W2).rearrange("p (g n) -> p g n", n=W2) for _ in range(2)]
        w_f = carve(KC * P).rearrange("p (c n) -> p c n", c=KC)
        w_t = carve(KC * P).rearrange("p (c n) -> p c n", c=KC)
        v_buf = [carve(4 * W2).rearrange("p (g n) -> p g n", n=W2) for _ in range(2)]
        probs = [carve(512) for _ in range(2)]
        probs_n = carve(P)
        pT = [carve(512) for _ in range(2)]
        pT_n = carve(P)
        qbd = carve(NSEQ * P)
        q_now = carve(P)
        acc = carve(P)
        pick_now = carve(P // 2)
        nmx, sums, cexp = small[:, 0:5], small[:, 8:13], small[:, 16:21]
        nmax, total, rtotal = small[:, 24:25], small[:, 25:26], small[:, 26:27]
        pick_now = pick_now[0:NS].bitcast(BF16)
        qbd_v = qbd.rearrange("p (s j n) -> p s j n", s=NSEQ, j=4)
        kg = [wbuf[:, b].rearrange("p c n -> p (c n)")[:, 0:4 * 512].rearrange("p (j n) -> p j n", j=4)
              for b in range(2)]

        k_in, v_in = sems("k_in", 2), sems("v_in", 2)
        v_free = sem("v_free")
        wf_in, wt_in = sem("wf_in"), sem("wt_in")
        wf_used, wt_used = sem("wf_used"), sem("wt_used")
        sig_ok = sem("sig_ok")
        kg_tr, kg_dve, kg_act = sem("kg_tr"), sem("kg_dve"), sem("kg_act")
        qk, mx, ex = sem("qk"), sem("mx"), sem("ex")
        p_tr, p_ev, pv = sem("p_tr"), sem("p_ev"), sem("pv")
        fill_ev = sem("fill_ev")
        nm_ok, c_ok, o_ok = sem("nm_ok"), sem("c_ok"), sem("o_ok")
        now_ok, qbd_ok, banks_ok = sem("now_ok"), sem("qbd_ok"), sem("banks_ok")
        FB, KB0, SB0, PTB, OB, MB = 0, 1, 3, 5, 6, 7
        M_S, M_O, M_P = slice(64, 128), slice(128, 256), slice(256, 384)
        NPAGES = cache_k.shape[0]
        HALF = TOK // 2

        def page_loads(e, cache, buf, arrived, s, g):
            for n in range(4):
                pg = e.value_load(pages[0:1, bass.ds(s * NPG + 4 * g + n, 1)], min_val=0, max_val=NPAGES - 1)
                e.dma_start(buf[g % 2][:, n, :],
                            cache[bass.ds(pg, 1), 0].rearrange("a p h d -> p (a h d)")).then_inc(arrived[g % 2], 16)

        def load_wf(sp, s):
            sp.dma_start(w_f, w_rows[:, :, bass.ds(s * P, P)]).then_inc(wf_in, 16)

        def load_wt(sp, s):
            sp.dma_start(w_t, w_rows[:, :, bass.ds(s * P + G_IA, P)]).then_inc(wt_in, 16)

        def hold(dve, value):
            dve.wait_ge(topk, value)
            nc.vector.memset(small[:, 95:96], 0.0)

        def kidx_loads(e, sequences):
            e.wait_ge(pages_in, 16)
            with e.Fori(0, NPG // 2) as g:
                for s in sequences:
                    for h in range(2):
                        pg = e.value_load(pages[0:1, bass.ds(g + s * NPG + h * (NPG // 2), 1)], min_val=0,
                                          max_val=cache_kidx.shape[0] - 1)
                        e.dma_start(kidx[:, s, bass.ds(g * 2 + h, 1), :],
                                    cache_kidx[bass.ds(pg, 1), 0].rearrange("a p d -> p a d")
                                    ).then_inc(kidx_in[s], 16)

        with nc.Block() as block:
            @block.sync
            def _(sp):
                sp.dma_start(pages[:], page_table.rearrange("s g -> (s g)").rearrange("(a n) -> a n", a=1)).then_inc(pages_in, 16)
                sp.dma_start(ident[:], c_ident).then_inc(const_in, 16)
                for t in range(NT + 1):
                    src = xp_rows[t] if t < NT else xs_rows
                    for h in range(2):
                        w = slice(h * W2, (h + 1) * W2)
                        sp.dma_start(xin[0:ROWS[t], t, w], src[:, w]).then_inc(x_half[h] if t == 0 else x_in[t], 16)

                for dst, src in ((rope, c_rope), (tri, c_tri), (own, c_own),
                                 (sameq, c_sameq), (keep, c_keep), (pick_f, c_pick)):
                    sp.dma_start(dst[:], src).then_inc(const_in, 16)
                sp.dma_start(gki[:, 0, :], idx_norm_g.partition_broadcast(P)).then_inc(ki_par_in, 16)
                sp.dma_start(gki[:, 1, :], idx_norm_b.partition_broadcast(P)).then_inc(ki_par_in, 16)
                kidx_loads(sp, (0, 1, 2, 3))
                kidx_loads(sp, (7,))
                for a in range(2):
                    for h in range(HA):
                        sp.dma_start(lbl[:, a, h:h + 1], hgrn_lb_logits[a, h * P:(h + 1) * P].unsqueeze(1)).then_inc(lb_in, 16)
                sp.dma_start(gn[:], hgrn_norm_g.partition_broadcast(P)).then_inc(gn_in, 16)
                sp.wait_ge(prelu, 3 * HI)
                load_wf(sp, 0)
                for g in range(2):
                    page_loads(sp, cache_k, k_buf, k_in, 0, g)
                load_wt(sp, 0)

            def indexer_jobs(g, t):
                n = 4 * ((g - BEFORE - 1) * (NT + 1) + t)
                return range(n, n + 4) if g > BEFORE and n < 3 * HI else range(0)

            def pe_project(pe, g, then=None):
                pe.wait_ge(w_got[g % 2], 16 * (g // 2 + 1))
                w = GROUPS[g][1]
                for i, t in enumerate(tiles_of(g)):
                    n = g * (NT + 1) + i
                    if n >= PB:
                        pe.wait_ge(proj_ev, n - PB + 1)
                    split = 2 if t == NT and w == 512 else 1
                    for c in range(KC):
                        for a in range(split):
                            mm = pe.matmul(psum[a * NS:a * NS + ROWS[t], n % PB, 0:w // split],
                                           xT[:, c, t * P:t * P + ROWS[t]],
                                           wbuf[:, g % 2, c, a * w // split:(a + 1) * w // split],
                                           start=(c == 0), stop=(c == KC - 1), skip_group_check=(split == 2))
                    mm.then_inc(proj, 1)
                    if then:
                        then(g, t)

            @block.tensor
            def _(pe):
                pe.wait_ge(const_in, 16)
                for t in range(NT + 1):
                    if t:
                        pe.wait_ge(x_in[t], 32)
                    for h in range(2):
                        if t == 0:
                            pe.wait_ge(x_half[h], 16)
                        n = 2 * t + h
                        if n >= PB:
                            pe.wait_ge(x_ev, n - PB + 1)
                        for c in range(4):
                            mm = pe.transpose(psum[:, n % PB, c * P:c * P + ROWS[t]],
                                              xin[0:ROWS[t], t, (4 * h + c) * P:(4 * h + c + 1) * P],
                                              ident[0:ROWS[t], 0:ROWS[t]])
                        mm.then_inc(x_tr, 1)
                pe.wait_ge(x_ev, 2 * (NT + 1))
                def turn_indexer_keys(g, i):
                    if i != NT - 1:
                        return
                    pe.wait_ge(roped, NT + 1)
                    for t in range(NT):
                        mm = pe.transpose(psum[0:DH, TB, t * P:(t + 1) * P], kin[:, t, :], ident[:])
                    mm.then_inc(tr, 1)
                    pe.transpose(psum[0:DH, TB + 1, 0:NS], kin[0:NS, NT, :], ident[0:NS, 0:NS]).then_inc(tr, 1)
                    pe.wait_ge(wrep_ok, 1)
                    pe.matmul(psum[:, CB, 0:NS], w_rep, ident[0:NS, 0:NS], start=True, stop=True).then_inc(tr, 1)

                pe_project(pe, 0)
                pe_project(pe, 1)
                pe_project(pe, 2, turn_indexer_keys)

                pe.wait_ge(roped, NT + 1 + 1)
                pe.wait_ge(tr_ev, 3)
                for h in range(2):
                    for c in range(8):
                        mm = pe.transpose(psum[0:DH, CB + h, c * NS:(c + 1) * NS],
                                          qi_tok[0:NS, NT, (8 * h + c) * DH:(8 * h + c + 1) * DH],
                                          ident[0:NS, 0:NS])
                    mm.then_inc(qs_tr, 1)
                pe.wait_ge(proj_ev, BEFORE * (NT + 1))

                def keys(s):
                    pe.wait_ge(kidx_in[s], 16 * NPG)
                    if s:
                        pe.wait_ge(kidx_ev, 2 * s)
                    for b in range(2):
                        for c in range(4):
                            mm = pe.transpose(psum[:, TB + b, c * P:(c + 1) * P],
                                              kidx[:, s, 8 * b + 2 * c:8 * b + 2 * c + 2, :], ident[:])
                        mm.then_inc(kidx_tr, 1)

                def relevance(s):
                    pe.wait_ge(kidx_ev, 2 * s + 2)
                    for k in range(4):
                        h, b = k % 2, k // 2
                        if s:
                            pe.wait_ge(relu_ok, 4 * s - 3 + k)
                        pe.matmul(psum[:, k, :], qis[DH * h:DH * h + DH, s].rearrange("p h q -> p (h q)"),
                                  kxT[s % 2][DH * h:DH * h + DH, b * 512:(b + 1) * 512],
                                  start=True, stop=True).then_inc(rel, 1)

                def combine(s):
                    for k in range(4):
                        h, b = k % 2, k // 2
                        pe.wait_ge(relu_ok, 4 * s + k + 1)
                        mm = pe.matmul(psum[NS * b:NS * b + NS, CB + h, :], w_seq[:, s, :],
                                       relu_s[s % 2][:, k * 512:(k + 1) * 512], start=(s == 0), stop=(s == NSEQ - 1),
                                       skip_group_check=True)
                    mm.then_inc(comb, 1)

                keys(0)
                pe.wait_ge(wseq_ok, NSEQ)
                pe.wait_ge(qs_dve, 1)
                pe.wait_ge(qs_act, 1)
                for s in range(NSEQ):
                    relevance(s)
                    if s + 1 < NSEQ:
                        keys(s + 1)
                    if s:
                        combine(s - 1)
                for s in range(NSEQ):
                    mm = pe.matmul(psum[:, TB, s * NNEW:(s + 1) * NNEW], qis[0:DH, s].rearrange("p h q -> p (h q)"),
                                   kiT[0:DH, SEQ + s * NNEW:SEQ + (s + 1) * NNEW], start=True, stop=True,
                                   skip_group_check=True)
                mm.then_inc(rel_n, 1)
                combine(NSEQ - 1)
                pe.wait_ge(relun_ok, 1)
                for s in range(NSEQ):
                    mm = pe.matmul(psum[0:NS, TB + 1, s * NNEW:(s + 1) * NNEW], w_seq[:, s, :],
                                   relu_n[:, s * NNEW:(s + 1) * NNEW], start=True, stop=True, skip_group_check=True)
                mm.then_inc(comb_n, 1)

                def turn_queries(g, t):
                    if t == 0:
                        pe.wait_ge(s_ok, 5)
                        pe.wait_ge(roped, 2 * (NT + 1))
                    for job in (2 * t, 2 * t + 1) if t < NT else ():
                        if job >= 2:
                            pe.wait_ge(qi_tr_ev, job - 1)
                        for c in range(4):
                            c0 = (4 * (job % 2) + c) * P
                            mm = pe.transpose(psum[:, TB + job % 2, c * P:(c + 1) * P], qi_tok[:, t, c0:c0 + P], ident[:])
                        mm.then_inc(qi_tr, 1)

                def prompt_relevance(g, t):
                    pe.wait_ge(qi_tr_ev, 2 * NT)
                    for n in indexer_jobs(g, t):
                        b, h = n // HI + 1, n % HI
                        if n >= 4:
                            pe.wait_ge(prelu, n - 3)
                        r = DH * (h % 2)
                        pe.matmul(psum[:, TB + n % 4, 0:(b + 1) * P], qiT[r:r + DH, h // 2, b * P:(b + 1) * P],
                                  kiT[r:r + DH, 0:(b + 1) * P], start=True, stop=True).then_inc(prel, 1)

                job = 0

                def turn(src, t):
                    nonlocal job
                    if job >= 2:
                        pe.wait_ge((tr2_act, tr2_dve)[job % 2], job // 2)
                    for c in range(4):
                        mm = pe.transpose(psum[:, TB + job % 2, c * P:c * P + ROWS[t]],
                                          src[0:ROWS[t], t, c * P:(c + 1) * P],
                                          ident[0:ROWS[t], 0:ROWS[t]])
                    mm.then_inc(tr2, 1)
                    job += 1

                pe.wait_ge(relu_ok, 4 * NSEQ)
                pe_project(pe, 3, turn_queries)
                pe_project(pe, 4, prompt_relevance)
                pe_project(pe, 5, prompt_relevance)
                pe_project(pe, 6, prompt_relevance)
                pe.wait_ge(prelu, 3 * HI)
                for t in range(NT + 1):
                    pe.wait_ge(roped, 2 * (NT + 1) + t + 1)
                    turn(k_tok, t)
                for t in range(NT + 1):
                    pe.wait_ge(roped, 3 * (NT + 1) + t + 1)
                    turn(q_tok, t)

            def queries_apart(copy, h, a):
                return copy(qis[DH * a:DH * a + DH, :, 8 * h:8 * h + 8, :].rearrange("p s h q -> p h s q"),
                            psum[0:DH, CB + h, :].rearrange("p (h s q) -> p h s q", h=8, s=NSEQ))

            def turned_out(e, copy, done, job):
                dst, t = (kT, qT)[job // (NT + 1)], job % (NT + 1)
                e.wait_ge(tr2, job + 1)
                copy(dst[:, :, t * P:t * P + ROWS[t]],
                     psum[:, TB + job % 2, :].rearrange("p (c n) -> p c n", c=4)[:, :, 0:ROWS[t]]).then_inc(done, 1)

            def load_w(act, g):
                c0, w = GROUPS[g]
                act.dma_start(wbuf[:, g % 2, :, 0:w], w_rows[:, :, c0:c0 + w]).then_inc(w_got[g % 2], 16)

            def act_evac(act, g, then=None):
                dest = (kiwi, qi_tok[:, :, 0:512], qi_tok[:, :, 512:1024], v_tok, k_tok, q_tok, gB)[g]
                w = GROUPS[g][1]
                for i, t in enumerate(tiles_of(g)):
                    n = g * (NT + 1) + i
                    act.wait_ge(proj, n + 1)
                    split = 2 if t == NT and w == 512 else 1
                    for a in range(split):
                        o = dest[0:ROWS[t], t, a * w // split:(a + 1) * w // split]
                        i_ = psum[a * NS:a * NS + ROWS[t], n % PB, 0:w // split]
                        if g == 6:
                            ins = nc.scalar.activation(o, i_, ACT.Silu)
                        elif g == 5:
                            ins = nc.scalar.mul(o, i_, DH ** -0.5)
                        else:
                            ins = nc.scalar.copy(o, i_)
                        if split == 2 and a == 0:
                            ins.then_inc(act_own, 1)
                    if split == 2:
                        halves_out[0] += 1
                        act.wait_ge(act_own, halves_out[0])
                    ins.then_inc(proj_ev, 1)
                    if then:
                        then(g, t)
                if g + 2 < len(GROUPS):
                    load_w(act, g + 2)

            @block.scalar
            def _(act):
                load_w(act, 0)
                for n in range(2 * (NT + 1)):
                    if n == 4:
                        load_w(act, 1)
                    t, h = n // 2, n % 2
                    act.wait_ge(x_tr, n + 1)
                    nc.scalar.copy(xT[:, 4 * h:4 * h + 4, t * P:t * P + ROWS[t]],
                                   psum[:, n % PB, :].rearrange("p (c n) -> p c n", c=4)[:, :, 0:ROWS[t]]
                                   ).then_inc(x_ev, 1)
                act_evac(act, 0)
                act_evac(act, 1)
                act.wait_ge(var_ok, 1)
                nc.scalar.activation(rstd[:, :], mv[:, :, 1], ACT.Sqrt).then_inc(std_ok, 1)
                act_evac(act, 2)
                act.wait_ge(qs_tr, 2)
                for a in range(2):
                    ins = queries_apart(nc.scalar.copy, 1, a)
                    if a == 0:
                        ins.then_inc(act_own, 1)
                halves_out[0] += 1
                act.wait_ge(act_own, halves_out[0])
                ins.then_inc(qs_act, 1)
                for s in range(NSEQ):
                    if s >= 2:
                        act.wait_ge(comb, s - 1)
                    for k in range(4):
                        act.wait_ge(rel, 4 * s + k + 1)
                        nc.scalar.activation(relu_s[s % 2][:, k * 512:(k + 1) * 512], psum[:, k, :],
                                             ACT.Relu).then_inc(relu_ok, 1)
                act.wait_ge(rel_n, 1)
                nc.scalar.activation(relu_n, psum[:, TB, 0:NS], ACT.Relu).then_inc(relun_ok, 1)
                act.wait_ge(comb, NSEQ)
                for h in range(2):
                    for b in range(2):
                        g = 2 * h + b
                        nc.scalar.copy(S[:, g * 512:(g + 1) * 512], psum[NS * b:NS * b + NS, CB + h, :]).then_inc(s_ok, 1)
                act.wait_ge(comb_n, 1)
                nc.scalar.copy(S[:, PAST:], psum[0:NS, TB + 1, 0:NS]).then_inc(s_ok, 1)

                def queries_out(g, t):
                    for job in (2 * t, 2 * t + 1) if t < NT else ():
                        h = job % 2
                        act.wait_ge(qi_tr, job + 1)
                        nc.scalar.copy(qiT[:, 4 * h:4 * h + 4, t * P:(t + 1) * P],
                                       psum[:, TB + h, :].rearrange("p (c n) -> p c n", c=4)).then_inc(qi_tr_ev, 1)

                def prompt_relu(g, t):
                    def weigh(n):
                        b, h = n // HI + 1, n % HI
                        act.wait_ge(prelu, n + 1)
                        nc.scalar.mul(relu_p[:, n % 4, 0:(b + 1) * P], relu_p[:, n % 4, 0:(b + 1) * P],
                                      kiwi[:, b, DH + h:DH + h + 1]).then_inc(weighed, 1)

                    jobs = indexer_jobs(g, t)
                    for n in jobs:
                        w = (n // HI + 2) * P
                        act.wait_ge(prel, n + 1)
                        if n >= 4:
                            act.wait_ge(pacc, n - 3)
                        nc.scalar.activation(relu_p[:, n % 4, 0:w], psum[:, TB + n % 4, 0:w], ACT.Relu).then_inc(prelu, 1)
                        if n > jobs[0]:
                            weigh(n - 1)
                    if jobs:
                        weigh(jobs[-1])

                act_evac(act, 3, queries_out)
                act_evac(act, 4, prompt_relu)
                act_evac(act, 5, prompt_relu)
                act_evac(act, 6, prompt_relu)
                act.wait_ge(lb_ok, 1)
                nc.scalar.activation(lbt, lbt, ACT.Exp).then_inc(lb_ok, 1)

                for job in range(0, 2 * (NT + 1), 2):
                    turned_out(act, nc.scalar.copy, tr2_act, job)

            @block.vector
            def _(dve):
                me = Tally(dve, dve_own)
                dve.wait_ge(x_ev, 2 * (NT + 1))
                me.link(nc.vector.memset(mv[:], 1.0))
                for t in range(NT + 1):
                    dve.wait_ge(proj_ev, t + 1)
                    me.add(nc.vector.bn_stats(stats[0:ROWS[t], t, :], kiwi[0:ROWS[t], t, 0:DH]))
                me.wait()
                for t in range(NT + 1):
                    me.add(nc.vector.bn_aggr(mv[0:ROWS[t], t, :], stats[0:ROWS[t], t, :]))
                me.wait()
                nc.vector.tensor_scalar(mv[:, :, 1], mv[:, :, 1], EPS, None, ALU.add).then_inc(var_ok, 1)
                nc.vector.tensor_scalar(w_rep.rearrange("p (h q) -> p h q", h=HI),
                                        kiwi[0:NS, NT, DH:DH + HI].unsqueeze(2).to_broadcast([NS, HI, NNEW]),
                                        (HI * DH) ** -0.5, None, ALU.mult).then_inc(wrep_ok, 1)
                me.add(nc.vector.tensor_scalar(kiwi[:, 0:NT, DH:DH + HI], kiwi[:, 0:NT, DH:DH + HI],
                                               (HI * DH) ** -0.5, None, ALU.mult))
                me.add(nc.vector.memset(w_seq, 0.0))
                dve.wait_ge(std_ok, 1)
                me.link(nc.vector.reciprocal(rstd[:, :], rstd[:, :]))
                dve.wait_ge(ki_par_in, 32)
                for t in range(NT + 1):
                    r = ROWS[t]
                    me.link(nc.vector.tensor_scalar(kin[0:r, t, :], kiwi[0:r, t, 0:DH], mv[0:r, t, 0:1],
                                                    rstd[0:r, t:t + 1], ALU.subtract, ALU.mult))
                    me.link(nc.vector.tensor_tensor(kin[0:r, t, :], kin[0:r, t, :], gki[0:r, 0, :], ALU.mult))
                    nc.vector.tensor_tensor(kin[0:r, t, :], kin[0:r, t, :], gki[0:r, 1, :], ALU.add).then_inc(kin_ok, 1)
                dve.wait_ge(const_in, NCONST)
                me.link(nc.vector.tensor_copy(pick[:], pick_f))
                def both(cols, view):
                    for h in range(2):
                        ins = nc.vector.tensor_copy(cols(h), view)
                        if h == 0:
                            me.add(ins)
                    ins.then_inc(tr_ev, 1)

                dve.wait_ge(tr, 1)
                both(lambda h: kiT[DH * h:DH * h + DH, 0:SEQ], psum[0:DH, TB, :])
                dve.wait_ge(tr, 2)
                both(lambda h: kiT[DH * h:DH * h + DH, SEQ:TOK], psum[0:DH, TB + 1, 0:NS])
                dve.wait_ge(tr, 3)
                dve.wait_ge(const_in, NCONST)
                nc.vector.tensor_tensor(w_all, psum[:, CB, 0:NS], sameq[:], ALU.mult).then_inc(tr_ev, 1)
                dve.wait_ge(tr_ev, 3)
                for s in range(NSEQ):
                    nc.vector.tensor_copy(w_seq[:, s, s * NNEW:(s + 1) * NNEW],
                                          w_all[:, s * NNEW:(s + 1) * NNEW]).then_inc(wseq_ok, 1)
                dve.wait_ge(qs_tr, 1)
                for a in range(2):
                    queries_apart(nc.vector.tensor_copy, 0, a).then_inc(dve_own if a == 0 else qs_dve, 1)
                me.n = me.n + 1
                me.wait()
                for s in range(NSEQ):
                    for b in range(2):
                        dve.wait_ge(kidx_tr, 2 * s + b + 1)
                        if s >= 2 and b == 0:
                            dve.wait_ge(rel, 4 * (s - 1))
                        nc.vector.tensor_copy(kxT[s % 2][:, b * 512:(b + 1) * 512],
                                              psum[:, TB + b, :]).then_inc(kidx_ev, 1)
                dve.wait_ge(s_ok, 5)
                me.link(nc.vector.tensor_tensor(S[:, PAST:], S[:, PAST:], own[:, 0, :], ALU.mult))
                nc.vector.tensor_tensor(S[:, PAST:], S[:, PAST:], own[:, 1, :], ALU.add).then_inc(topk, 1)

                dve.wait_ge(lb_in, 2 * HA * 16)
                me.link(nc.vector.tensor_tensor(lb, lbl[:, 0], lbl[:, 1], ALU.max))
                nc.vector.tensor_tensor(lbt, lbl, lb.unsqueeze(1).to_broadcast([P, 2, HA]), ALU.subtract).then_inc(lb_ok, 1)
                with dve.Fori(0, TOPK_S // 8) as r:
                    hold(dve, r * 2 + 1)
                    nc.vector.max(best[0:NS, 0, :], S).then_inc(topk, 1)
                    hold(dve, r * 2 + 2)
                    nc.vector.match_replace(S, best[0:NS, 0, :], S, TAKEN).then_inc(topk, 1)
                dve.wait_ge(topk, 2 * (TOPK_S // 8) + 1)
                me.add(nc.vector.tensor_scalar(bias_s[:, 0:PAST], S[:, 0:PAST], 0.9 * TAKEN, MASKED, ALU.is_gt, ALU.mult))
                me.link(nc.vector.tensor_scalar(newbias, S[:, PAST:], 0.9 * TAKEN, MASKED, ALU.is_gt, ALU.mult))
                me.link(nc.vector.tensor_tensor(bias_s[:, PAST:], newbias, own[:, 2, :], ALU.add))
                dve.wait_ge(lb_ok, 2)
                me.link(nc.vector.tensor_tensor(lbc, lbt[:, 0], lbt[:, 1], ALU.add))
                me.link(nc.vector.reciprocal(lbc, lbc))
                me.link(nc.vector.tensor_tensor(lb, lbt[:, 0], lbc, ALU.mult))
                me.link(nc.vector.tensor_scalar(lbc, lb, -1.0, 1.0, ALU.mult, ALU.add))
                for job in range(1, 2 * (NT + 1), 2):
                    turned_out(dve, nc.vector.tensor_copy, tr2_dve, job)
                dve_count[0] = me.n

            @block.gpsimd
            def _(pool):
                me = Tally(pool, pool_own)
                pool.dma_start(ofseq[:], c_ofseq).then_inc(ofseq_in, 16)
                kidx_loads(pool, (4, 5, 6))
                pool.wait_ge(const_in, NCONST)

                def rotate(view, r, t, heads, scaled=False):
                    x1, x2 = view[:, :, 0:ROT], view[:, :, ROT:2 * ROT]
                    shape = [r, heads, ROT]
                    cos = rope[0:r, t, 0:ROT].unsqueeze(1).to_broadcast(shape)
                    sin = rope[0:r, t, ROT:2 * ROT].unsqueeze(1).to_broadcast(shape)
                    tmp = [rtmp[0:r, a, 0:heads * ROT].rearrange("p (h n) -> p h n", h=heads) for a in range(4)]
                    for a, (x, w) in enumerate(((x1, cos), (x2, sin), (x1, sin), (x2, cos))):
                        me.add(nc.gpsimd.tensor_tensor(tmp[a], x, w, ALU.mult))
                    me.wait()
                    me.add(nc.gpsimd.tensor_tensor(x1, tmp[0], tmp[1], ALU.subtract))
                    me.wait()
                    nc.gpsimd.tensor_tensor(x2, tmp[2], tmp[3], ALU.add).then_inc(roped, 1)

                def store(dst, src):
                    pool.dma_start(dst, src).then_inc(stored, 16)
                    NSTORE[0] += 16

                n = 0
                for t in range(NT + 1):
                    r = ROWS[t]
                    pool.wait_ge(kin_ok, t + 1)
                    if n:
                        pool.wait_ge(roped, n)
                    rotate(kin[0:r, t, :].unsqueeze(1), r, t, 1)
                    n += 1
                pool.wait_ge(roped, n)
                for i, t in enumerate(tiles_of(BEFORE - 1)):
                    r = ROWS[t]
                    pool.wait_ge(proj_ev, 2 * (NT + 1) + i + 1)
                    pool.wait_ge(roped, n)
                    rotate(qi_tok[0:r, t, :].rearrange("p (h d) -> p h d", h=HI), r, t, HI)
                    n += 1
                for t in range(NT):
                    store(ki_prompt[0, t, 0], kin[:, t, :])
                store(ki_sample[:, 0].rearrange("s t d -> (s t) d"), kin[0:NS, NT, :])

                def weigh(g, t):
                    for m in indexer_jobs(g, t):
                        b, h = m // HI + 1, m % HI
                        src = relu_p[:, m % 4, 0:(b + 1) * P]
                        pool.wait_ge(weighed, m + 1)
                        if h == 0:
                            nc.gpsimd.tensor_copy(SP[b], src).then_inc(pacc, 1)
                        else:
                            pool.wait_ge(pacc, m)
                            nc.gpsimd.tensor_tensor(SP[b], SP[b], src, ALU.add).then_inc(pacc, 1)
                        if h == HI - 1:
                            d = SP[b][:, b * P:]
                            pool.wait_ge(pacc, m + 1)
                            me.link(nc.gpsimd.tensor_tensor(d, d, tri[:, 0, :], ALU.mult))
                            me.link(nc.gpsimd.tensor_tensor(d, d, tri[:, 1, :], ALU.add))

                for g, view in ((3, v_tok), (4, k_tok), (5, q_tok), (6, None)):
                    for t in range(NT + 1):
                        r = ROWS[t]
                        pool.wait_ge(proj_ev, g * (NT + 1) + t + 1)
                        if g in (4, 5):
                            pool.wait_ge(roped, n)
                            rotate(view[0:r, t, :].rearrange("p (h d) -> p h d", h=HB), r, t, HB)
                            n += 1
                        weigh(g, t)
                    out_p, out_s = {3: (v_prompt, v_sample), 4: (k_prompt, k_sample)}.get(g, (None, None))
                    if out_p is not None:
                        pool.wait_ge(roped, n)
                        for t in range(NT):
                            store(out_p[0, t, 0].rearrange("p h d -> p (h d)"), view[:, t, :])
                        store(out_s[:, 0].rearrange("s t h d -> (s t) (h d)"), view[0:NS, NT, :])
                pool.wait_ge(ofseq_in, 16)
                pool.wait_ge(gn_in, 16)
                pool_count[0] = me.n
        with nc.Block() as block:
            @block.sync
            def _(sp):
                def keys(s, g, after=None):
                    if after is not None:
                        sp.wait_ge(kg_tr, after)
                    page_loads(sp, cache_k, k_buf, k_in, s, g)

                def sequence(s, last):
                    keys(s, 2, s * 16 + 4)
                    keys(s, 3, s * 16 + 8)
                    if not last:
                        keys(s + 1, 0, s * 16 + 12)
                        sp.wait_ge(wf_used, s * 2 + 2)
                        load_wf(sp, s + 1)
                        keys(s + 1, 1, s * 16 + 16)
                        sp.wait_ge(wt_used, s * 2 + 2)
                        load_wt(sp, s + 1)

                with sp.Fori(0, NSEQ - 1) as s:
                    sequence(s, False)
                sequence(NSEQ - 1, True)

            @block.gpsimd
            def _(pool):
                def now(s):
                    nc.gpsimd.tensor_copy(q_now.unsqueeze(1), qbd.rearrange("p (s n) -> p s n", s=NSEQ)[:, bass.ds(s, 1), :]
                                          ).then_inc(now_ok, 1)
                    nc.gpsimd.tensor_copy(pick_now, pick[:, bass.ds(s * P, P)]).then_inc(now_ok, 1)

                me = Tally(pool, pool_own, pool_count[0])
                me.link(nc.gpsimd.memset(qbd, 0.0))
                for h in range(2):
                    nc.gpsimd.tensor_copy(
                        qbd_v[DH * h:DH * h + DH, :, :, NNEW * h:NNEW * h + NNEW],
                        qT[DH * h:DH * h + DH, :, SEQ:TOK].rearrange("p j (s q) -> p s j q", s=NSEQ)).then_inc(qbd_ok, 1)
                pool.wait_ge(qbd_ok, 2)
                with pool.Fori(0, NSEQ) as s:
                    after(pool, qk, s * 5)
                    now(s)
                    for g in range(4):
                        pool.wait_ge(v_free, s * 4 + g + 1)
                        page_loads(pool, cache_v, v_buf, v_in, s, g)
                pool_count[0] = me.n

            @block.tensor
            def _(pe):
                pe.sem_inc(v_free, 2)
                begin(pe, qk, p_tr, pv)
                pe.wait_ge(banks_ok, 4)

                def turn_keys(s, g, half):
                    if half == 0:
                        pe.wait_ge(k_in[g % 2], s * 128 + 64 * (g // 2) + 64)
                    for j in (2 * half, 2 * half + 1):
                        if j % 2 == 0:
                            after(pe, kg_dve, s * 8 + 2 * g + j // 2)
                        else:
                            after(pe, kg_act, s * 8 + 2 * g + j // 2)
                        for n in range(4):
                            mm = pe.transpose(psum[:, KB0 + j % 2, n * P:(n + 1) * P],
                                              k_buf[g % 2][:, n, j * P:(j + 1) * P], ident[:])
                        mm.then_inc(kg_tr, 1)

                def logits(s, g):
                    pe.wait_ge(now_ok, s * 2 + 2)
                    after(pe, kg_dve, s * 8 + 2 * g + 2)
                    after(pe, kg_act, s * 8 + 2 * g + 2)
                    after(pe, ex, s * 5 + g - 1 if g >= 2 else s * 5)
                    bank = psum[:, SB0 + g % 2, :]
                    pe.matmul(bank, pick_now, bias_s[:, g * 512:(g + 1) * 512], start=True, stop=False,
                              skip_group_check=True)
                    for j in range(4):
                        mm = pe.matmul(bank[32 * j:32 * j + 32, :], q_now[:, 32 * j:32 * j + 32], kg[g % 2][:, j, :],
                                       start=False, stop=(j == 3), skip_group_check=True)
                    mm.then_inc(qk, 1)

                def logits_new(s):
                    bank = psum[:, MB, M_S]
                    pe.matmul(bank, pick_now, bias_s[:, PAST:LS], start=True, stop=False, skip_group_check=True)
                    for j in range(4):
                        mm = pe.matmul(bank[32 * j:32 * j + 32, :], q_now[:, 32 * j:32 * j + 32], kT[:, j, SEQ:TOK],
                                       start=False, stop=(j == 3), skip_group_check=True)
                    mm.then_inc(qk, 1)

                def turn_probs(s, g):
                    after(pe, ex, s * 5 + g + 1)
                    after(pe, p_ev, s * 5 + g)
                    for n in range(4):
                        mm = pe.transpose(psum[:, PTB, n * P:(n + 1) * P], probs[g % 2][:, n * P:(n + 1) * P], ident[:])
                    mm.then_inc(p_tr, 1)

                def values(s, g):
                    after(pe, p_ev, s * 5 + g + 1)
                    pe.wait_ge(v_in[g % 2], s * 128 + 64 * (g // 2) + 64)
                    if g == 0:
                        after(pe, o_ok, s)
                    for j in range(4):
                        for n in range(4):
                            mm = pe.matmul(psum[32 * j:32 * j + 16, OB, g * P:(g + 1) * P],
                                           pT[g % 2][:, n * P + 32 * j:n * P + 32 * j + 16],
                                           v_buf[g % 2][:, n, j * P:(j + 1) * P], start=(n == 0), stop=(n == 3),
                                           skip_group_check=True)
                    mm.then_inc(v_free, 1)

                def feature_tile(s, half, chunks):
                    if half == 0:
                        pe.wait_ge(wf_in, s * 16 + 16)
                    if chunks[0] == 0:
                        after(pe, fill_ev, s * 4 + half)
                    for c in chunks:
                        mm = pe.matmul(psum[:, FB, 0:HALF], w_f[:, c, :], xT[:, c, half * HALF:(half + 1) * HALF],
                                       start=(c == 0), stop=(c == KC - 1), skip_group_check=True)
                    if chunks[-1] == KC - 1:
                        mm.then_inc(wf_used, 1)

                def token_tile(s, t):
                    if t == 0:
                        pe.wait_ge(wt_in, s * 16 + 16)
                        after(pe, fill_ev, s * 4 + 2)
                    if t == NT:
                        after(pe, fill_ev, s * 4 + 3)
                    r = ROWS[t]
                    out = psum[0:r, FB, (t % NT) * P:(t % NT + 1) * P]
                    for c in range(KC):
                        mm = pe.matmul(out, xT[:, c, t * P:t * P + r], w_t[:, c, :], start=(c == 0),
                                       stop=(c == KC - 1), skip_group_check=True)
                    if t >= NT - 1:
                        mm.then_inc(wt_used, 1)

                all_chunks, first_chunks, last_chunks = range(KC), range(KC // 2), range(KC // 2, KC)
                with pe.Fori(0, NSEQ) as s:
                    turn_keys(s, 0, 0)
                    feature_tile(s, 0, all_chunks)
                    turn_keys(s, 0, 1)
                    feature_tile(s, 1, first_chunks)
                    turn_keys(s, 1, 0)
                    feature_tile(s, 1, last_chunks)
                    turn_keys(s, 1, 1)
                    logits(s, 0)
                    turn_keys(s, 2, 0)
                    token_tile(s, 0)
                    turn_keys(s, 2, 1)
                    logits(s, 1)
                    turn_probs(s, 0)
                    token_tile(s, 1)
                    values(s, 0)
                    turn_keys(s, 3, 0)
                    logits(s, 2)
                    turn_keys(s, 3, 1)
                    turn_probs(s, 1)
                    token_tile(s, 2)
                    values(s, 1)
                    logits(s, 3)
                    turn_probs(s, 2)
                    logits_new(s)
                    token_tile(s, 3)
                    values(s, 2)
                    turn_probs(s, 3)
                    after(pe, ex, s * 5 + 5)
                    pe.transpose(psum[:, MB, M_P], probs_n, ident[:]).then_inc(p_tr, 1)
                    token_tile(s, 4)
                    values(s, 3)
                    after(pe, p_ev, s * 5 + 5)
                    for j in range(4):
                        mm = pe.matmul(psum[32 * j:32 * j + 16, MB, M_O], pT_n[:, 32 * j:32 * j + 16],
                                       v_tok[:, NT, j * P:(j + 1) * P], start=True, stop=True, skip_group_check=True)
                    mm.then_inc(pv, 1)

            @block.scalar
            def _(act):
                def keys_out(s, g, pieces=(1, 3)):
                    for j in pieces:
                        act.wait_ge(kg_tr, s * 16 + 4 * g + j + 1)
                        if j == 1:
                            after(act, qk, s * 5 + g - 1 if g >= 2 else s * 5)
                        nc.scalar.copy(kg[g % 2][:, j, :], psum[:, KB0 + 1, :]).then_inc(kg_act, 1)

                def exponential(s, g):
                    act.wait_ge(mx, s * 5 + g + 1)
                    after(act, p_tr, s * 5 + g - 1 if g >= 2 else s * 5)
                    nc.scalar.activation(probs[g % 2], psum[:, SB0 + g % 2, :], ACT.Exp, bias=nmx[:, g:g + 1],
                                         accum_out=sums[:, g:g + 1]).then_inc(ex, 1)

                act.wait_ge(banks_ok, 4)
                begin(act, kg_act, ex, fill_ev)
                with act.Fori(0, NSEQ) as s:
                    keys_out(s, 0, (1,))
                    act.wait_ge(wf_used, s * 2 + 1)
                    nc.scalar.copy(aF[:, bass.ds(s, 1), 0:HALF], psum[:, FB:FB + 1, 0:HALF]).then_inc(fill_ev, 1)
                    keys_out(s, 0, (3,))
                    keys_out(s, 1, (1,))
                    act.wait_ge(wf_used, s * 2 + 2)
                    nc.scalar.copy(aF[:, bass.ds(s, 1), HALF:TOK], psum[:, FB:FB + 1, 0:HALF]).then_inc(fill_ev, 1)
                    keys_out(s, 1, (3,))
                    exponential(s, 0)
                    keys_out(s, 2)
                    exponential(s, 1)
                    keys_out(s, 3)
                    exponential(s, 2)
                    exponential(s, 3)
                    act.wait_ge(mx, s * 5 + 5)
                    nc.scalar.activation(probs_n[:, 0:NS], psum[:, MB, M_S], ACT.Exp, bias=nmx[:, 4:5],
                                         accum_out=sums[:, 4:5]).then_inc(ex, 1)
                    act.wait_ge(wt_used, s * 2 + 1)
                    nc.scalar.copy(aT[:, 0:NT, bass.ds(s * P, P)],
                                   psum[:, FB, :].rearrange("p (t n) -> p t n", t=NT)).then_inc(fill_ev, 1)
                    act.wait_ge(wt_used, s * 2 + 2)
                    nc.scalar.copy(aT[0:NS, NT, bass.ds(s * P, P)], psum[0:NS, FB, 0:P]).then_inc(fill_ev, 1)
                    act.wait_ge(nm_ok, s + 1)
                    nc.scalar.activation(cexp, nmx, ACT.Exp, bias=nmax, scale=-1.0).then_inc(c_ok, 1)
                act.wait_ge(kg_tr, 16 * NSEQ)
                act.wait_ge(wf_used, 2 * NSEQ)
                nc.scalar.activation(dec, ky, ACT.Sigmoid).then_inc(sig_ok, 1)
                act.wait_ge(sig_ok, 1)
                nc.scalar.activation(ky, ky, ACT.Sigmoid, scale=-1.0).then_inc(sig_ok, 1)

            @block.vector
            def _(dve):
                me = Tally(dve, dve_own, dve_count[0])
                nc.vector.memset(psum[:, OB, :], 0.0).then_inc(banks_ok, 1)
                nc.vector.memset(psum[:, MB, :], 0.0).then_inc(banks_ok, 1)
                nc.vector.memset(probs_n, 0.0).then_inc(banks_ok, 1)
                nc.vector.memset(v_tok[NS:P, NT, :], 0.0).then_inc(banks_ok, 1)

                begin(dve, kg_dve, p_ev, o_ok)

                def keys_out(s, g):
                    for j in (0, 2):
                        dve.wait_ge(kg_tr, s * 16 + 4 * g + j + 1)
                        if j == 0:
                            after(dve, qk, s * 5 + g - 1 if g >= 2 else s * 5)
                        nc.vector.tensor_copy(kg[g % 2][:, j, :], psum[:, KB0, :]).then_inc(kg_dve, 1)

                def negmax(s, g):
                    after(dve, qk, s * 5 + g + 1)
                    src = psum[:, SB0 + g % 2, :] if g < 4 else psum[:, MB, M_S]
                    nc.vector.tensor_reduce(nmx[:, g:g + 1], src, AX.X, ALU.max, negate=True).then_inc(mx, 1)

                def probs_out(s, g):
                    after(dve, p_tr, s * 5 + g + 1)
                    dve.wait_ge(v_free, s * 4 + g + 1)
                    nc.vector.tensor_copy(pT[g % 2], psum[:, PTB, :]).then_inc(p_ev, 1)

                base = 2 * (TOPK_S // 8) + 1
                ROUNDS = TOPK_P // 8 // NSEQ

                def strike(s, step):
                    hold(dve, s * (6 * ROUNDS) + (base + 3 * step))
                    for b in (1, 2, 3):
                        if step % 2 == 0:
                            nc.vector.max(best[:, b, :], SP[b]).then_inc(topk, 1)
                        else:
                            nc.vector.match_replace(SP[b], best[:, b, :], SP[b], TAKEN).then_inc(topk, 1)

                with dve.Fori(0, NSEQ) as s:
                    me.n = s * 7 + dve_count[0]
                    keys_out(s, 0)
                    strike(s, 0)
                    keys_out(s, 1)
                    negmax(s, 0)
                    keys_out(s, 2)
                    negmax(s, 1)
                    probs_out(s, 0)
                    strike(s, 1)
                    keys_out(s, 3)
                    negmax(s, 2)
                    probs_out(s, 1)
                    strike(s, 2)
                    negmax(s, 3)
                    probs_out(s, 2)
                    negmax(s, 4)
                    strike(s, 3)
                    probs_out(s, 3)
                    after(dve, p_tr, s * 5 + 5)
                    after(dve, pv, s)
                    nc.vector.tensor_copy(pT_n, psum[:, MB, M_P]).then_inc(p_ev, 1)
                    dve.wait_ge(mx, s * 5 + 5)
                    nc.vector.tensor_reduce(nmax, nmx, AX.X, ALU.min).then_inc(nm_ok, 1)
                    dve.wait_ge(c_ok, s + 1)
                    me.link(nc.vector.tensor_tensor_reduce(small[:, 32:37], cexp, sums, 1.0, 0.0, ALU.mult, ALU.add,
                                                           total))
                    me.link(nc.vector.reciprocal(rtotal, total))
                    me.link(nc.vector.tensor_scalar(cexp, cexp, rtotal, None, ALU.mult))
                    after(dve, pv, s + 1)
                    dve.wait_ge(v_free, s * 4 + 6)
                    me.link(nc.vector.tensor_scalar(acc, psum[:, OB, 0:P], cexp[:, 0:1], None, ALU.mult))
                    for g in (1, 2, 3):
                        me.link(nc.vector.scalar_tensor_tensor(acc, psum[:, OB, g * P:(g + 1) * P], cexp[:, g:g + 1],
                                                               acc, ALU.mult, ALU.add))
                    nc.vector.scalar_tensor_tensor(osb[:, bass.ds(s, 1), :], psum[:, MB:MB + 1, M_O], cexp[:, 4:5],
                                                   acc.unsqueeze(1), ALU.mult, ALU.add).then_inc(o_ok, 1)
                me.n = dve_count[0] + 7 * NSEQ
                dve.wait_ge(topk, base + 6 * ROUNDS * NSEQ)
                me.add(nc.vector.tensor_copy(bias_p[:, 0:P], tri[:, 2, :]))
                for b in (1, 2, 3):
                    me.add(nc.vector.tensor_scalar(SP[b], SP[b], 0.9 * TAKEN, MASKED, ALU.is_gt, ALU.mult))
                me.wait()
                for b in (1, 2, 3):
                    d = SP[b][:, b * P:]
                    me.add(nc.vector.tensor_tensor(d, d, tri[:, 2, :], ALU.add))
                me.wait()
                dve_count[0] = me.n
        at[0] = KEEP2
        cum, dec, qE, kE = (carve(4 * TOK).rearrange("p (h n) -> p h n", h=HA) for _ in range(4))
        sc = carve(NT * 512).rearrange("p (c n) -> p c n", c=NT)
        sc_n = carve(HA * NS)[0:NS]
        levels_mem = carve(len(LEVELS) * HA * P // 4)
        levels = levels_mem.bitcast(U8).rearrange("p (l n) -> p l n", l=len(LEVELS))
        levels_f = qE.rearrange("p h n -> p (h n)")[:, 0:len(LEVELS) * P].rearrange("p (l n) -> p l n", l=len(LEVELS))
        states = [carve(HA * P) for _ in range(2)]
        seqcols = carve(NSEQ * NS)
        el_p, el_n = carve(HA * NT), carve(HA * NSEQ)
        ia, ga = aT[:, :, 0:W2], aT[:, :, W2:D]
        xflat = xT[:].rearrange("p c n -> p (c n)")
        lgt = [xflat[:, 512 * a:512 * a + 512] for a in range(2)]
        prb = [xflat[:, 1024 + 512 * a:1536 + 512 * a] for a in range(2)]
        prT = [xflat[:, 2048 + 512 * a:2560 + 512 * a] for a in range(2)]
        wo = wbuf[:].rearrange("p b c n -> p (b c n)").rearrange("p (c n) -> p c n", c=KC)
        nm4, rs4, ri4 = small[:, 40:44], small[:, 44:48], small[:, 48:52]

        par_in, wo_in, lev_in = sem("par_in"), sem("wo_in"), sem("lev_in")
        gate_ok, f_ok, ln_ok = sem("gate_ok"), sem("f_ok"), sem("ln_ok")
        ke_z = sem("ke_z")
        key_ok, q_ok, diff_ok, dec_ok, qe_ok, ke_ok = (sem("key_ok"), sem("q_ok"), sem("diff_ok"), sem("dec_ok"),
                                                       sem("qe_ok"), sem("ke_ok"))
        lv, lv_ev = sem("lv"), sem("lv_ev")
        diff_k_ok, scan_ok, sc_z = sem("diff_k_ok"), sem("scan_ok"), sem("sc_z")
        e_ok, qc_ok, el_ok, dl_ok, dl_ex, kd_ok = (sem("e_ok"), sem("qc_ok"), sem("el_ok"), sem("dl_ok"), sem("dl_ex"),
                                                   sem("kd_ok"))
        lg, lmax, lex, ltr, ltr_ev, lpv, lout = (sem("lg"), sem("lmax"), sem("lex"), sem("ltr"), sem("ltr_ev"),
                                                 sem("lpv"), sem("lout"))
        NLEV = len(LEVELS)
        JOBS = [(l, c) for l in range(NLEV) for c in range(NT + (LEVELS[l] < NNEW))]
        FIRST = [min(n for n, j in enumerate(JOBS) if j[0] == l) for l in range(NLEV)] + [len(JOBS)]
        NA = HB * NT

        LEAD, STEP = 4, 3
        LAST = LEAD + STEP * NLEV

        def level_of(a):
            l, c = (a - LEAD) // STEP, (a - LEAD) % STEP
            return (l, c) if 0 <= l < NLEV else (None, c)

        def jobs_of(a):
            l, c = level_of(a)
            if l is None or c == 2:
                return range(0)
            n0, n1 = FIRST[l], FIRST[l + 1]
            return range(n0, n0 + 3) if c == 0 else range(n0 + 3, n1)

        def span(l):
            return TOK if LEVELS[l] < NNEW else SEQ

        def halves(x, l):
            b = LEVELS[l]
            v = x[:, :, 0:span(l)].rearrange("p h (n r) -> p h n r", r=2 * b)
            return v[:, :, :, 0:b], v[:, :, :, b:2 * b], v[:, :, :, b - 1:b]

        with nc.Block() as block:
            @block.sync
            def _(sp):
                sp.dma_start(levels_f, c_levels.rearrange("p (l n) -> p l n", l=NLEV)).then_inc(lev_in, 16)
                sp.dma_start(seqcols, c_seqcols).then_inc(par_in, 16)
                for c in range(2):
                    sp.dma_start(wo[:, 4 * c:4 * c + 4], wo_rows[:, 4 * c:4 * c + 4]).then_inc(wo_in, 16)
                sp.wait_ge(par_in, 16)
                sp.wait_ge(lev_in, 16)
                sp.wait_ge(wo_in, 32)

            @block.tensor
            def _(pe):
                def level_job(n):
                    l, c = JOBS[n]
                    if n >= 3:
                        pe.wait_ge(lv_ev, n - 2)
                    if l == 0:
                        pe.wait_ge(q_ok, 1)
                        pe.wait_ge(key_ok, 1)
                    else:
                        pe.wait_ge(qe_ok, l)
                        pe.wait_ge(ke_ok, l)
                    kk, qq = (ky, qa) if l == 0 else (kE, qE)
                    w, c0 = (P, c * P) if c < NT else (NS, SEQ)
                    for h in range(HA):
                        mm = pe.matmul(psum[0:w, n % 3, h * w:(h + 1) * w], kk[:, h, c0:c0 + w], qq[:, h, c0:c0 + w],
                                       start=True, stop=True, skip_group_check=True)
                    mm.then_inc(lv, 1)

                def prompt_logits(a):
                    h, b = a // NT, a % NT
                    if a >= 2:
                        pe.wait_ge(lmax, a - 1)
                    r = DH * (h % 2)
                    pe.matmul(psum[:, 3 + a % 2, 0:(b + 1) * P], qT[r:r + DH, h // 2, b * P:(b + 1) * P],
                              kT[r:r + DH, h // 2, 0:(b + 1) * P], start=True, stop=True).then_inc(lg, 1)

                def turn(a):
                    b = a % NT
                    pe.wait_ge(lex, a + 1)
                    if a >= 2:
                        pe.wait_ge(ltr_ev, a - 1)
                    for k in range(b + 1):
                        mm = pe.transpose(psum[:, 5 + a % 2, k * P:(k + 1) * P], prb[a % 2][:, k * P:(k + 1) * P], ident[:])
                    mm.then_inc(ltr, 1)

                def prompt_values(a):
                    h, b = a // NT, a % NT
                    pe.wait_ge(ltr_ev, a + 1)
                    if a >= 1:
                        pe.wait_ge(lout, a)
                    for k in range(b + 1):
                        mm = pe.matmul(psum[:, 7, 0:P], prT[a % 2][:, k * P:(k + 1) * P],
                                       v_tok[:, k, (h // 2) * P:(h // 2 + 1) * P], start=(k == 0), stop=(k == b))
                    mm.then_inc(lpv, 1)

                for a in range(NA + 2):
                    if a < NA:
                        prompt_logits(a)
                        for n in jobs_of(a):
                            level_job(n)
                    if 1 <= a <= NA:
                        turn(a - 1)
                    if a >= 2:
                        prompt_values(a - 2)

            @block.scalar
            def _(act):
                def exponential(a):
                    b = a % NT
                    act.wait_ge(lmax, a + 1)
                    if a >= 2:
                        act.wait_ge(ltr, a - 1)
                        act.wait_ge(lout, a - 3) if a >= 4 else None
                    w = (b + 1) * P
                    nc.scalar.activation(prb[a % 2][:, 0:w], lgt[a % 2][:, 0:w], ACT.Exp, bias=nm4[:, a % 4:a % 4 + 1],
                                         scale=-1.0, accum_out=rs4[:, a % 4:a % 4 + 1]).then_inc(lex, 1)

                def probs_out(a):
                    act.wait_ge(ltr, a + 1)
                    if a >= 2:
                        act.wait_ge(lpv, a - 1)
                    w = (a % NT + 1) * P
                    nc.scalar.copy(prT[a % 2][:, 0:w], psum[:, 5 + a % 2, 0:w]).then_inc(ltr_ev, 1)

                for a in range(NA + 1):
                    if a == 2:
                        nc.scalar.activation(qa, qa, ACT.Silu).then_inc(q_ok, 1)
                        act.wait_ge(f_ok, HA)
                        nc.scalar.activation(dec, dec, ACT.Ln).then_inc(ln_ok, 1)
                    if a == LEAD + 3 * STEP:
                        nc.scalar.activation(ga[:, 0:NT], ga[:, 0:NT], ACT.Silu).then_inc(gate_ok, 1)
                        nc.scalar.activation(ga[0:NS, NT], ga[0:NS, NT], ACT.Silu).then_inc(gate_ok, 1)
                    if a < NA:
                        l, step = level_of(a)
                        if step == 1 and l is not None and l + 1 < NLEV:
                            act.wait_ge(diff_ok, l + 1)
                            act.wait_ge(diff_k_ok, l + 1)
                            nc.scalar.activation(dec[:, :, 0:span(l + 1)], dec[:, :, 0:span(l + 1)],
                                                 ACT.Exp).then_inc(dec_ok, 1)
                        if a == LAST:
                            act.wait_ge(ke_ok, NLEV - 1)
                            act.wait_ge(qe_ok, NLEV - 1)
                            nc.scalar.activation(dec, cum, ACT.Exp).then_inc(e_ok, 1)
                        if a == LAST + 2:
                            act.wait_ge(dl_ok, 2)
                            nc.scalar.activation(dec, dec, ACT.Exp).then_inc(dl_ex, 1)
                        exponential(a)
                    if a >= 1:
                        probs_out(a - 1)

            @block.gpsimd
            def _(pool):
                nc.gpsimd.memset(kE, 0.0).then_inc(ke_z, 1)
                nc.gpsimd.memset(sc, 0.0).then_inc(sc_z, 1)
                nc.gpsimd.memset(sc_n, 0.0).then_inc(sc_z, 1)
                pool.wait_ge(ke_z, 1)

                def differences(l):
                    left, _, edge = halves(cum, l)
                    if l > 1:
                        pool.wait_ge(ke_ok, l - 1)
                        pool.wait_ge(qe_ok, l - 1)
                    nc.gpsimd.tensor_tensor(halves(dec, l)[0], edge.to_broadcast(list(left.shape)), left,
                                            ALU.subtract).then_inc(diff_k_ok, 1)

                pool.wait_ge(scan_ok, HA)
                differences(1)
                for l in range(1, NLEV):
                    pool.wait_ge(dec_ok, l)
                    pool.wait_ge(key_ok, 1)
                    if l > 1:
                        pool.wait_ge(lv, FIRST[l])
                    nc.gpsimd.tensor_tensor(halves(kE, l)[0], halves(ky, l)[0], halves(dec, l)[0], ALU.mult).then_inc(ke_ok, 1)
                    if l + 1 < NLEV:
                        differences(l + 1)
                pool.wait_ge(gn_in, 16)
                pool.wait_ge(gate_ok, 2)
                for t in range(NT + 1):
                    r = ROWS[t]
                    v = ga[0:r, t].rearrange("p (h n) -> p h n", h=HA)
                    nc.gpsimd.tensor_tensor(v, v, gn[0:r].unsqueeze(1).to_broadcast([r, HA, P]), ALU.mult).then_inc(gate_ok, 1)
                pool.wait_ge(dl_ex, 1)
                pool.wait_ge(lv, len(JOBS))
                nc.gpsimd.tensor_tensor(kE[:, 0:1], ky[:, 0:1], dec[:, 0:1], ALU.mult).then_inc(kd_ok, 1)

            @block.vector
            def _(dve):
                me = Tally(dve, dve_own, dve_count[0])
                def forget_gate():
                    dve.wait_ge(sig_ok, 1)
                    for h in range(HA):
                        nc.vector.tensor_scalar(dec[:, h], dec[:, h], lbc[:, h:h + 1], lb[:, h:h + 1], ALU.mult, ALU.add).then_inc(f_ok, 1)

                def input_key():
                    dve.wait_ge(sig_ok, 2)
                    for h in range(HA):
                        ins = nc.vector.tensor_scalar(ky[:, h], ky[:, h], lbc[:, h:h + 1], None, ALU.mult)
                    ins.then_inc(key_ok, 1)

                def masks_in():
                    dve.wait_ge(lev_in, 16)
                    for h in range(HA):
                        me.add(nc.vector.tensor_copy(levels[:, :, h * P:(h + 1) * P], levels_f))
                    me.wait()
                    me.link(nc.vector.memset(qE, 0.0))
                    dve.wait_ge(sc_z, 2)

                def running_sums():
                    dve.wait_ge(ln_ok, 1)
                    for h in range(HA):
                        nc.vector.tensor_tensor_scan(cum[:, h], keep[:], dec[:, h], 0.0, ALU.mult, ALU.add).then_inc(scan_ok, 1)
                    dve.wait_ge(scan_ok, HA)

                def differences(l):
                    _, right, edge = halves(cum, l)
                    if l > 1:
                        dve.wait_ge(ke_ok, l - 1)
                        dve.wait_ge(qe_ok, l - 1)
                    nc.vector.tensor_tensor(halves(dec, l)[1], right, edge.to_broadcast(list(right.shape)),
                                            ALU.subtract).then_inc(diff_ok, 1)

                def scores_out(n):
                    l, c = JOBS[n]
                    dve.wait_ge(lv, n + 1)
                    if c < NT:
                        out, mask, src = sc[:, c], levels[:, l], psum[:, n % 3, :]
                    else:
                        out = sc_n.rearrange("p (h n) -> p h n", h=HA)
                        mask = levels[0:NS, l].rearrange("p (h n) -> p h n", h=HA)[:, :, 0:NS]
                        src = psum[0:NS, n % 3, 0:HA * NS].rearrange("p (h n) -> p h n", h=HA)
                    nc.vector.copy_predicated(out, mask, src).then_inc(lv_ev, 1)

                def mask_and_max(a):
                    b = a % NT
                    w = (b + 1) * P
                    dve.wait_ge(lg, a + 1)
                    if a >= 2:
                        dve.wait_ge(lex, a - 1)
                    nc.vector.tensor_tensor_reduce(lgt[a % 2][:, 0:w], psum[:, 3 + a % 2, 0:w],
                                                   bias_p[:, POFF[b]:POFF[b] + w], -1.0, 3.0e38, ALU.add, ALU.min,
                                                   nm4[:, a % 4:a % 4 + 1]).then_inc(lmax, 1)

                def attended(a):
                    h, b = a // NT, a % NT
                    dve.wait_ge(lex, a + 1)
                    me.link(nc.vector.reciprocal(ri4[:, a % 4:a % 4 + 1], rs4[:, a % 4:a % 4 + 1]))
                    dve.wait_ge(lpv, a + 1)
                    g = gB[:, b, h * DH:(h + 1) * DH]
                    nc.vector.scalar_tensor_tensor(g, psum[:, 7, DH * (h % 2):DH * (h % 2) + DH], ri4[:, a % 4:a % 4 + 1],
                                                   g, ALU.mult, ALU.mult).then_inc(lout, 1)

                def decay_queries():
                    dve.wait_ge(e_ok, 1)
                    dve.wait_ge(lv, len(JOBS))
                    nc.vector.tensor_tensor(qE, qa, dec, ALU.mult).then_inc(qc_ok, 1)
                    nc.vector.tensor_copy(el_p.rearrange("p (h n) -> p h n", h=HA), dec[:, :, P - 1:SEQ:P]).then_inc(el_ok, 1)
                    nc.vector.tensor_copy(el_n.rearrange("p (h n) -> p h n", h=HA),
                                          dec[:, :, SEQ + NNEW - 1:TOK:NNEW]).then_inc(el_ok, 1)

                def to_chunk_end():
                    dve.wait_ge(el_ok, 2)
                    dve.wait_ge(qc_ok, 1)
                    for (a, b, w) in ((0, SEQ, P), (SEQ, TOK, NNEW)):
                        v = cum[:, :, a:b].rearrange("p h (n r) -> p h n r", r=w)
                        last = v[:, :, :, w - 1:w].to_broadcast(list(v.shape))
                        nc.vector.tensor_tensor(dec[:, :, a:b].rearrange("p h (n r) -> p h n r", r=w), last, v,
                                                ALU.subtract).then_inc(dl_ok, 1)

                for a in range(NA + 2):
                    if a < NA:
                        l, step = level_of(a)
                        if step == 0 and l is not None and l + 1 < NLEV:
                            differences(l + 1)
                        mask_and_max(a)
                        for n in jobs_of(a):
                            scores_out(n)
                        if step == 2 and l is not None and l + 1 < NLEV:
                            dve.wait_ge(dec_ok, l + 1)
                            dve.wait_ge(lv, FIRST[l + 1])
                            dve.wait_ge(q_ok, 1)
                            nc.vector.tensor_tensor(halves(qE, l + 1)[1], halves(qa, l + 1)[1], halves(dec, l + 1)[1],
                                                    ALU.mult).then_inc(qe_ok, 1)
                        if a == LAST:
                            decay_queries()
                        if a == LAST + 1:
                            to_chunk_end()
                        if a == LAST + 2:
                            dve.wait_ge(dl_ex, 1)
                            dve.wait_ge(lv, len(JOBS))
                            me.add(nc.vector.tensor_tensor(kE[:, 1:HA], ky[:, 1:HA], dec[:, 1:HA], ALU.mult))
                    if a >= 2:
                        attended(a - 2)
                    for slot, part in ((0, forget_gate), (1, masks_in), (1, input_key), (2, running_sums)):
                        if a == slot:
                            part()
                dve_count[0] = me.n

        kdT = arena[:, KEEP2:KEEP2 + (NT + 1) * W2].rearrange("p (t n) -> p t n", n=W2)
        lng, lnb = (arena[:, a:a + D] for a in (KEEP2 + 2560, KEEP2 + 2560 + D))
        aF_flat = aF.rearrange("p c n -> p (c n)")
        oa = aF_flat[:, 0:(NT + 1) * W2].rearrange("p (t n) -> p t n", n=W2)
        xr = [aF_flat[:, 2560 + a * D:2560 + (a + 1) * D] for a in range(2)]
        kE_flat = kE.rearrange("p h n -> p (h n)")
        z = [kE_flat[:, a * D:(a + 1) * D] for a in range(2)]
        s0 = xflat[:, 0:NSEQ * HA * P].rearrange("p (s h n) -> p s h n", s=NSEQ, h=HA)
        vflat = v_tok[:].rearrange("p t n -> p (t n)")
        scflat = sc.rearrange("p c n -> p (c n)")
        vx = [v[0:NS, a * 1024:(a + 1) * 1024].rearrange("p (s n) -> p s n", s=NSEQ)
              for v in (vflat, scflat) for a in range(2)]
        qx = [v.rearrange("p (s n) -> p s n", s=NSEQ) for v in (bias_p[:, 0:512], bias_p[:, 512:1024],
                                                                levels_mem[:, 0:512], levels_mem[:, 512:1024])]
        sq = vflat[:, 2048:2048 + W2]
        ss = small[:, 56:56 + 4 * (NT + 1)]
        mixA, mixB = qT, kT
        st2 = small[:, 80:92].rearrange("p (a n) -> p a n", a=2)
        mv2 = small[:, 92:94]
        sd = small[:, 94:95]
        state_st, s0_in = sem("state_st"), sem("s0_in")
        turned, turned_ev, kv, st_ok, oc, oc_ev = (sem("turned"), sem("turned_ev"), sem("kv"), sem("st_ok"), sem("oc"),
                                                   sem("oc_ev"))
        qx_ok, vx_ok, dec_o, skv, skv_ev, sdec = (sem("qx_ok"), sem("vx_ok"), sem("dec_o"), sem("skv"), sem("skv_ev"),
                                                  sem("sdec"))
        ss_ok, ss_v, ss_r, mixed = sem("ss_ok"), sem("ss_v"), sem("ss_r"), sem("mixed")
        os_tr, os_ev, ma, ma_ev = sem("os_tr"), sem("os_ev"), sem("ma"), sem("ma_ev")
        ln_in, xr_in = sem("ln_in"), sems("xr_in", 2)
        yb, y_half, zr, zv, zs, zf = sem("yb"), sem("y_half"), sem("zr"), sem("zv"), sem("zs"), sem("zf")
        y_st = sems("y_st", 2)
        YB = 2
        with nc.Block() as block:
            @block.sync
            def _(sp):
                sp.dma_start(s0, state_hgrn[0].rearrange("s h k v -> k s h v")).then_inc(s0_in, 16)

                def load_x(t):
                    sp.dma_start(xr[t % 2][0:ROWS[t]], xp_rows[t] if t < NT else xs_rows).then_inc(xr_in[t % 2], 16)

                load_x(0)
                load_x(1)
                sp.dma_start(lng, ln_g.partition_broadcast(P)).then_inc(ln_in, 16)
                sp.dma_start(lnb, ln_b.partition_broadcast(P)).then_inc(ln_in, 16)
                sp.wait_ge(st_ok, HA * NT)
                sp.dma_start(st_prompt[0, 0].rearrange("h k v -> k h v"),
                             states[(NT - 1) % 2].rearrange("p (h n) -> p h n", h=HA)).then_inc(state_st, 16)
                sp.wait_ge(skv_ev, HA)
                sp.dma_start(st_sample[0].rearrange("s h k v -> k s h v"), s0).then_inc(state_st, 16)
                for t in range(NT + 1):
                    if t + 2 <= NT:
                        sp.wait_ge(zr, 2 * (t + 1))
                        load_x(t + 2)
                    sp.wait_ge(zf, t + 1)
                    sp.dma_start(y_prompt[0].rearrange("(t p) d -> t p d", p=P)[t] if t < NT
                                 else y_sample.rearrange("s t d -> (s t) d"), z[t % 2][0:ROWS[t]]).then_inc(y_st[t % 2], 16)
                sp.wait_ge(state_st, 32)
                sp.wait_ge(y_st[0], 48)
                sp.wait_ge(y_st[1], 32)
                sp.wait_ge(stored, NSTORE[0])

            @block.tensor
            def _(pe):
                def turn(n, piece, r, width):
                    if n >= 2:
                        pe.wait_ge(turned_ev, n - 1)
                    for c in range(4):
                        src = piece(c)
                        rows = src.shape[0]
                        mm = pe.transpose(psum[0:r, n % 2, c * P:c * P + width], src, ident[0:rows, 0:rows])
                    mm.then_inc(turned, 1)

                for t in range(NT + 1):
                    turn(t, lambda h: kE[:, h, t * P:t * P + ROWS[t]], ROWS[t], P)

                def turn_gated(t):
                    turn(NT + 1 + t, lambda c: gB[0:ROWS[t], t, c * P:(c + 1) * P], P, ROWS[t])

                for c in range(NT):
                    pe.wait_ge(turned_ev, c + 1)
                    if c >= 2:
                        pe.wait_ge(st_ok, HA * (c - 1))
                    for h in range(HA):
                        mm = pe.matmul(psum[:, 4 + c % 2, h * P:(h + 1) * P], kdT[:, c, h * P:(h + 1) * P],
                                       ia[:, c, h * P:(h + 1) * P], start=True, stop=True, skip_group_check=True)
                    mm.then_inc(kv, 1)
                    turn_gated(c)
                    if c >= 2:
                        pe.wait_ge(oc_ev, c - 1)
                    for h in range(HA):
                        out = psum[:, 2 + c % 2, h * P:(h + 1) * P]
                        mm = pe.matmul(out, sc[:, c, h * P:(h + 1) * P], ia[:, c, h * P:(h + 1) * P],
                                       start=True, stop=(c == 0), skip_group_check=True)
                        if c:
                            pe.wait_ge(st_ok, HA * c)
                            mm = pe.matmul(out, qE[:, h, c * P:(c + 1) * P], states[(c - 1) % 2][:, h * P:(h + 1) * P],
                                           start=False, stop=True, skip_group_check=True)
                    mm.then_inc(oc, 1)
                turn_gated(NT)
                for a in range(2):
                    pe.wait_ge(turned_ev, 2 * (NT + 1) - 1 + a)
                    for s in range(4):
                        mm = pe.transpose(psum[:, a, s * P:(s + 1) * P], osb[:, 4 * a + s, :], ident[:])
                    mm.then_inc(os_tr, 1)
                def turn_normed(t):
                    pe.wait_ge(mixed, t + 1)
                    if t == 1:
                        pe.wait_ge(os_ev, 2)
                    if t >= 2:
                        pe.wait_ge(skv_ev, HA - 1)
                        pe.wait_ge(ma_ev, t - 1)
                    for c in range(4):
                        mm = pe.transpose(psum[:, (7, 1)[t % 2], c * P:c * P + ROWS[t]], oa[0:ROWS[t], t, c * P:(c + 1) * P],
                                          ident[0:ROWS[t], 0:ROWS[t]])
                    mm.then_inc(ma, 1)

                def mix(c, t):
                    return (mixA, mixB)[c // 4][:, c % 4, t * P:t * P + ROWS[t]]

                def decode_outputs():
                    pe.wait_ge(s0_in, 16)
                    for g in range(HA // 2):
                        pe.wait_ge(qx_ok, 2 * g + 2)
                        for s in range(-1, NSEQ):
                            for a in range(2):
                                h = 2 * g + a
                                out = psum[NS * a:NS * a + NS, 6, g * P:(g + 1) * P]
                                if s < 0:
                                    mm = pe.matmul(out, sc_n[:, h * NS:(h + 1) * NS], ia[0:NS, NT, h * P:(h + 1) * P],
                                                   start=True, stop=False, skip_group_check=True)
                                else:
                                    mm = pe.matmul(out, qx[h][:, s, :], s0[:, s, h, :], start=False, stop=(s == NSEQ - 1),
                                                   skip_group_check=True)
                        mm.then_inc(dec_o, 1)
                def decode_states():
                    pe.wait_ge(turned_ev, NT + 1)
                    for h in range(HA):
                        pe.wait_ge(vx_ok, h + 1)
                        if h == 0:
                            pe.wait_ge(ma_ev, 2)
                        elif h == 1:
                            pe.wait_ge(st_ok, HA * NT)
                        else:
                            pe.wait_ge(skv_ev, h - 1)
                        for a in range(2):
                            mm = pe.matmul(psum[:, 4 * (h % 2) + a, :], kdT[0:NS, NT, h * P:(h + 1) * P],
                                           vx[h][:, 4 * a:4 * a + 4, :], start=True, stop=True)
                        mm.then_inc(skv, 1)

                def project_out(t):
                    pe.wait_ge(ma_ev, t + 1)
                    if t < NT:
                        for a in range(2):
                            m = 2 * t + a
                            if m == 0:
                                pe.wait_ge(oc_ev, NT)
                            if m == 2:
                                pe.wait_ge(skv_ev, HA)
                            if m >= 4:
                                pe.wait_ge(zr, m - 3)
                            for c in range(KC):
                                mm = pe.matmul(psum[:, YB + m % 4, :], mix(c, t), wo[:, c, a * 512:(a + 1) * 512],
                                               start=(c == 0), stop=(c == KC - 1))
                            mm.then_inc(yb, 1)
                    else:
                        pe.wait_ge(zr, 2 * NT - 3)
                        for c in range(KC):
                            for a in range(2):
                                mm = pe.matmul(psum[NS * a:NS * a + NS, YB + (2 * t) % 4, :], mix(c, t),
                                               wo[:, c, a * 512:(a + 1) * 512], start=(c == 0), stop=(c == KC - 1),
                                               skip_group_check=True)
                        mm.then_inc(yb, 1)

                turn_normed(0)
                decode_outputs()
                turn_normed(1)
                project_out(0)
                decode_states()
                for t in range(1, NT + 1):
                    if t < NT:
                        turn_normed(t + 1)
                    project_out(t)

            @block.scalar
            def _(act):
                for t in range(NT + 1):
                    r = ROWS[t]
                    act.wait_ge(turned, t + 1)
                    nc.scalar.copy(kdT[0:r, t, :], psum[0:r, t % 2, :]).then_inc(turned_ev, 1)

                def gated_out(t):
                    n = NT + 1 + t
                    act.wait_ge(turned, n + 1)
                    nc.scalar.copy(mixB[:, :, t * P:t * P + ROWS[t]],
                                   psum[:, n % 2, :].rearrange("p (c n) -> p c n", c=4)[:, :, 0:ROWS[t]]
                                   ).then_inc(turned_ev, 1)

                def squares(t):
                    act.wait_ge(oc_ev, t + 1)
                    if t:
                        act.wait_ge(ss_ok, HA * t)
                    for h in range(HA):
                        w = slice(h * P, (h + 1) * P)
                        nc.scalar.activation(sq[0:ROWS[t], w], oa[0:ROWS[t], t, w], ACT.Square,
                                             accum_out=ss[0:ROWS[t], t * HA + h:t * HA + h + 1]).then_inc(ss_ok, 1)

                def root(t):
                    act.wait_ge(ss_v, t + 1)
                    v = ss[0:ROWS[t], t * HA:(t + 1) * HA]
                    nc.scalar.activation(v, v, ACT.Sqrt).then_inc(ss_r, 1)

                def deviation(t):
                    if t == NT:
                        act.wait_ge(yb, 2 * NT + 1)
                        act.wait_ge(y_st[t % 2], 16 * (t // 2))
                        nc.scalar.copy(z[t % 2][0:NS, 512:D], psum[NS:2 * NS, YB + (2 * t) % 4, :]).then_inc(y_half, 1)
                    act.wait_ge(zv, t + 1)
                    nc.scalar.activation(sd[0:ROWS[t]], sd[0:ROWS[t]], ACT.Sqrt).then_inc(zs, 1)

                def normed_out(t):
                    act.wait_ge(ma, t + 1)
                    nc.scalar.copy(mixA[:, :, t * P:t * P + ROWS[t]],
                                   psum[:, (7, 1)[t % 2], :].rearrange("p (c n) -> p c n", c=4)[:, :, 0:ROWS[t]]
                                   ).then_inc(ma_ev, 1)

                for t in range(NT + 2):
                    if t <= NT:
                        gated_out(t)
                    if t == NT:
                        normed_out(0)
                    if 1 <= t <= NT:
                        squares(t - 1)
                    if t >= 2:
                        root(t - 2)
                normed_out(1)
                squares(NT)
                root(NT)
                deviation(0)
                for t in range(1, NT + 1):
                    if t < NT:
                        normed_out(t + 1)
                    deviation(t)

            @block.gpsimd
            def _(pool):
                for h in range(HA):
                    nc.gpsimd.tensor_tensor(qx[h], seqcols.rearrange("p (s n) -> p s n", s=NSEQ),
                                            qE[:, h, SEQ:TOK].unsqueeze(1).to_broadcast([P, NSEQ, NS]),
                                            ALU.mult).then_inc(qx_ok, 1)

                def values_apart(h):
                    nc.gpsimd.tensor_tensor(vx[h], ia[0:NS, NT, h * P:(h + 1) * P].unsqueeze(1).to_broadcast([NS, NSEQ, P]),
                                            ofseq[:].unsqueeze(2).to_broadcast([NS, NSEQ, P]), ALU.mult).then_inc(vx_ok, 1)

                values_apart(0)
                values_apart(1)
                pool.wait_ge(oc, NT)
                values_apart(2)
                values_apart(3)
                for h in range(HA):
                    pool.wait_ge(dec_o, h // 2 + 1)
                    nc.gpsimd.tensor_tensor(s0[:, :, h, :], s0[:, :, h, :],
                                            el_n[:, h * NSEQ:(h + 1) * NSEQ].unsqueeze(2).to_broadcast([P, NSEQ, P]),
                                            ALU.mult).then_inc(sdec, 1)
            @block.vector
            def _(dve):
                me = Tally(dve, dve_own, dve_count[0])

                def new_state(c):
                    dve.wait_ge(kv, c + 1)
                    if c >= 2:
                        dve.wait_ge(oc, c)
                    for h in range(HA):
                        old, st = (states[(c + a) % 2][:, h * P:(h + 1) * P] for a in (1, 0))
                        src = psum[:, 4 + c % 2, h * P:(h + 1) * P]
                        if c == 0:
                            nc.vector.tensor_copy(st, src).then_inc(st_ok, 1)
                        else:
                            if h == 0:
                                dve.wait_ge(st_ok, HA * c)
                            nc.vector.scalar_tensor_tensor(st, old, el_p[:, h * NT + c:h * NT + c + 1], src,
                                                           ALU.mult, ALU.add).then_inc(st_ok, 1)

                def outputs(t):
                    if t < NT:
                        dve.wait_ge(oc, t + 1)
                        nc.vector.tensor_copy(oa[:, t, :], psum[:, 2 + t % 2, :]).then_inc(oc_ev, 1)
                        return
                    dve.wait_ge(dec_o, HA // 2)
                    for a in range(2):
                        ins = nc.vector.tensor_copy(oa[0:NS, t, :].rearrange("p (g a n) -> p a g n", g=2, a=2)[:, a],
                                                    psum[NS * a:NS * a + NS, 6, 0:2 * P].rearrange("p (g n) -> p g n", g=2))
                        if a == 0:
                            me.add(ins)
                    me.wait()
                    ins.then_inc(oc_ev, 1)

                def mean_square(t):
                    dve.wait_ge(ss_ok, HA * (t + 1))
                    v = ss[0:ROWS[t], t * HA:(t + 1) * HA]
                    nc.vector.tensor_scalar(v, v, 1.0 / P, EPS, ALU.mult, ALU.add).then_inc(ss_v, 1)

                def norm_and_gate(t):
                    dve.wait_ge(ss_r, t + 1)
                    r = ROWS[t]
                    v = ss[0:r, t * HA:(t + 1) * HA]
                    me.link(nc.vector.reciprocal(v, v))
                    for h in range(HA):
                        o = oa[0:r, t, h * P:(h + 1) * P]
                        ins = nc.vector.scalar_tensor_tensor(o, o, v[:, h:h + 1], ga[0:r, t, h * P:(h + 1) * P],
                                                             ALU.mult, ALU.mult)
                    ins.then_inc(mixed, 1)

                def new_decode_state(h):
                    dve.wait_ge(skv, h + 1)
                    dve.wait_ge(sdec, h + 1)
                    for a in range(2):
                        v = s0[:, 4 * a:4 * a + 4, h, :]
                        ins = nc.vector.tensor_tensor(v, v, psum[:, 4 * (h % 2) + a, :].rearrange("p (s n) -> p s n", s=4),
                                                      ALU.add)
                    ins.then_inc(skv_ev, 1)

                def decode_gate(a):
                    dve.wait_ge(turned_ev, 2 * (NT + 1))
                    dve.wait_ge(os_tr, a + 1)
                    for h in range(2):
                        g = mixB[DH * h:DH * h + DH, :, SEQ + 32 * a:SEQ + 32 * a + 32].rearrange(
                            "p j (s q) -> p j s q", q=NNEW)
                        src = psum[DH * h:DH * h + DH, a, :].rearrange("p (s j x) -> p j s x", s=4, j=4)[
                            :, :, :, NNEW * h:NNEW * h + NNEW]
                        ins = nc.vector.tensor_tensor(g, src, g, ALU.mult)
                        if h == 0:
                            me.add(ins)
                    ins.then_inc(os_ev, 1)

                for c in range(NT):
                    new_state(c)
                    if c >= 1:
                        outputs(c - 1)
                    if c >= 2:
                        mean_square(c - 2)
                    if c >= 3:
                        norm_and_gate(c - 3)
                outputs(NT - 1)
                mean_square(NT - 2)
                norm_and_gate(NT - 3)
                decode_gate(0)
                decode_gate(1)
                mean_square(NT - 1)
                norm_and_gate(NT - 2)
                norm_and_gate(NT - 1)

                def add_and_norm(t):
                    r = ROWS[t]
                    zz = z[t % 2][0:r]
                    dve.wait_ge(xr_in[t % 2], 16 * (t // 2 + 1))
                    if t >= 2:
                        dve.wait_ge(y_st[t % 2], 16 * (t // 2))
                    for a in range(2):
                        m = 2 * t + a
                        w = slice(a * 512, a * 512 + 512)
                        if t < NT:
                            dve.wait_ge(yb, m + 1)
                            y = psum[:, YB + m % 4, :]
                        elif a == 0:
                            dve.wait_ge(yb, m + 1)
                            y = psum[0:NS, YB + m % 4, :]
                        else:
                            dve.wait_ge(y_half, 1)
                            y = zz[:, w]
                        nc.vector.scalar_tensor_tensor(zz[:, w], xr[t % 2][0:r, w], ALPHA, y,
                                                       ALU.mult, ALU.add).then_inc(zr, 1)
                        dve.wait_ge(zr, m + 1)
                        me.add(nc.vector.bn_stats(st2[0:r, a], zz[:, w]))
                    me.wait()
                    me.link(nc.vector.bn_aggr(mv2[0:r], st2[0:r]))
                    nc.vector.tensor_scalar(sd[0:r], mv2[0:r, 1:2], EPS, None, ALU.add).then_inc(zv, 1)
                    dve.wait_ge(zs, t + 1)
                    me.link(nc.vector.reciprocal(sd[0:r], sd[0:r]))
                    if t == 0:
                        dve.wait_ge(ln_in, 32)
                    me.link(nc.vector.scalar_tensor_tensor(zz, zz, mv2[0:r, 0:1], lng[0:r], ALU.subtract, ALU.mult))
                    nc.vector.scalar_tensor_tensor(zz, zz, sd[0:r], lnb[0:r], ALU.mult, ALU.add).then_inc(zf, 1)

                outputs(NT)
                mean_square(NT)
                norm_and_gate(NT)
                for h in range(HA):
                    new_decode_state(h)
                for t in range(NT + 1):
                    add_and_norm(t)


_INS = ["x_prompt", "x_sample", "cache_k", "cache_v", "cache_kidx", "state_hgrn", "page_table", "w_in",
        "hgrn_lb_logits", "hgrn_norm_g", "idx_norm_g", "idx_norm_b", "w_out", "ln_g", "ln_b"]
_OUTS = [(1, SEQ, D), (NSEQ, NNEW, D), (1, NT, 1, PAGE, HB, DH), (1, NT, 1, PAGE, HB, DH), (1, NT, 1, PAGE, DH),
         (1, 1, HA, P, P), (NSEQ, 1, NNEW, HB, DH), (NSEQ, 1, NNEW, HB, DH), (NSEQ, 1, NNEW, DH),
         (1, NSEQ, HA, P, P)]


def kernel(**inputs):
    import numpy as _np
    import concourse.bacc as _bacc
    from concourse import mybir as _mybir
    from concourse.bass_utils import run_bass_kernel_spmd as _run

    nc = _bacc.Bacc("TRN2", target_bir_lowering=False, num_devices=1)
    arrays, args = {}, []
    given = {name: _np.ascontiguousarray(inputs[name]) for name in _INS}
    given.update({f"c_{name}": a for name, a in shape_constants().items()})
    for name, a in given.items():
        arrays[f"in_{name}"] = a
        args.append(nc.dram_tensor(f"in_{name}", a.shape, _mybir.dt.from_np(a.dtype), kind="ExternalInput").ap())
    for i, shape in enumerate(_OUTS):
        args.append(nc.dram_tensor(f"out_{i}", shape, F32, kind="ExternalOutput").ap())
    hybrid_step(nc, *args)
    r = _run(nc, [arrays], core_ids=[0])
    return tuple(r.results[0][f"out_{i}"] for i in range(len(_OUTS)))
```
